# Optimizing a Trainium2 kernel written in Bass

```python
import jax, jax.numpy as jnp
from jax import lax
import numpy as np

D_MODEL = 1024
BATCH = 1
SEQ = 256
DEPTH = 1

CHUNK = 64
SG_BLOCK = 128
A_WIDTH = 1024
A_GROUPS = 8
A_GROUP_DIM = A_WIDTH // A_GROUPS
B_WIDTH = 1024
B_GROUPS = 8
CONV_WIDTH = 3
D_FF = 4 * D_MODEL
N_BRANCHES = 2
EPS = 1e-6
IN_COLS = 2 * A_WIDTH + 3 * B_WIDTH + N_BRANCHES * D_MODEL


def rmsnorm(x, g):
    xf = x.astype(jnp.float32)
    y = xf * lax.rsqrt(jnp.mean(xf * xf, axis=-1, keepdims=True) + EPS)
    return (y * g.astype(jnp.float32)).astype(x.dtype)

def chunk_mask():
    c = jnp.arange(SG_BLOCK) // CHUNK
    return c[None, :] <= c[:, None]

def spatial_gating(u, v, w_s, b_s):
    bsz, s, _ = v.shape
    vb = v.reshape(bsz, s // SG_BLOCK, SG_BLOCK, A_GROUPS, A_GROUP_DIM)
    w = jnp.where(chunk_mask()[None], w_s, jnp.zeros_like(w_s))
    mixed = jnp.einsum('gij,bnjgc->bnigc', w, vb) + b_s.T[None, None, :, :, None]
    return u * mixed.reshape(bsz, s, A_WIDTH)

def causal_dwconv(z, w):
    s = z.shape[1]
    zp = jnp.pad(z, ((0, 0), (CONV_WIDTH - 1, 0), (0, 0)))
    y = w[0] * zp[:, 0:s]
    for k in range(1, CONV_WIDTH):
        y = y + w[k] * zp[:, k:k + s]
    return y

def first_inputs(seed: int = 0) -> dict:
    key = jax.random.key(seed)
    ks = jax.random.split(key, 16)
    f32 = jnp.float32
    nrm = lambda k, shape, scale: jax.random.normal(k, shape, f32) * scale
    return {
        "x": nrm(ks[0], (BATCH, SEQ, D_MODEL), 1.0),
        "norm_mix_g": 1.0 + nrm(ks[1], (DEPTH, D_MODEL), 0.1),
        "w_in": nrm(ks[2], (DEPTH, D_MODEL, IN_COLS), D_MODEL ** -0.5),
        "b_gate": nrm(ks[3], (DEPTH, N_BRANCHES * D_MODEL), 0.01),
        "norm_v_g": 1.0 + nrm(ks[4], (DEPTH, A_WIDTH), 0.1),
        "w_s": nrm(ks[5], (DEPTH, A_GROUPS, SG_BLOCK, SG_BLOCK), SG_BLOCK ** -0.5),
        "b_s": 1.0 + nrm(ks[6], (DEPTH, A_GROUPS, SG_BLOCK), 0.1),
        "conv_w": nrm(ks[7], (DEPTH, CONV_WIDTH, B_WIDTH), CONV_WIDTH ** -0.5),
        "w_proj_a": nrm(ks[8], (DEPTH, A_WIDTH, D_MODEL), A_WIDTH ** -0.5),
        "w_proj_b": nrm(ks[9], (DEPTH, B_WIDTH, D_MODEL), B_WIDTH ** -0.5),
        "w_out": nrm(ks[10], (DEPTH, D_MODEL, D_MODEL), D_MODEL ** -0.5),
        "norm_ff_g": 1.0 + nrm(ks[11], (DEPTH, D_MODEL), 0.1),
        "w_ff1": nrm(ks[12], (DEPTH, D_MODEL, D_FF), D_MODEL ** -0.5),
        "w_ff2": nrm(ks[13], (DEPTH, D_FF, D_MODEL), D_FF ** -0.5),
        "norm_final_g": 1.0 + nrm(ks[14], (D_MODEL,), 0.1),
    }

def first_block(x, norm_mix_g, w_in, b_gate, norm_v_g, w_s, b_s, conv_w, w_proj_a, w_proj_b,
              w_out, norm_ff_g, w_ff1, w_ff2, norm_final_g):
    split_at = [A_WIDTH, 2 * A_WIDTH, 2 * A_WIDTH + B_WIDTH, 2 * A_WIDTH + 2 * B_WIDTH,
                2 * A_WIDTH + 3 * B_WIDTH, 2 * A_WIDTH + 3 * B_WIDTH + D_MODEL]
    for l in range(DEPTH):
        h = rmsnorm(x, norm_mix_g[l])
        proj = jnp.einsum('bsd,dc->bsc', h, w_in[l])
        u, v, bg, cg, xs, ga, gb = jnp.split(proj, split_at, axis=-1)
        ga = ga + b_gate[l, :D_MODEL]
        gb = gb + b_gate[l, D_MODEL:]

        u = jax.nn.gelu(u, approximate=False)
        v = rmsnorm(jax.nn.gelu(v, approximate=False), norm_v_g[l])
        a = spatial_gating(u, v, w_s[l], b_s[l])

        c = bg * causal_dwconv(cg * xs, conv_w[l])

        m = (jax.nn.sigmoid(ga) * jnp.einsum('bsc,cd->bsd', a, w_proj_a[l])
             + jax.nn.sigmoid(gb) * jnp.einsum('bsc,cd->bsd', c, w_proj_b[l]))
        x = x + jnp.einsum('bsd,de->bse', m, w_out[l])

        hf = rmsnorm(x, norm_ff_g[l])
        z = jax.nn.relu(jnp.einsum('bsd,df->bsf', hf, w_ff1[l]))
        x = x + jnp.einsum('bsf,fd->bsd', z * z, w_ff2[l])
    return rmsnorm(x, norm_final_g)


D_MIX = D_MODEL
D_MLSTM = D_MIX // 2
D_MOBA = D_MIX - D_MLSTM
MLSTM_HEADS = 4
MLSTM_HEAD_DIM = D_MLSTM // MLSTM_HEADS
MLSTM_CHUNK = 64
CONV_WIDTH_2 = 4
MOBA_HEADS = 8
MOBA_HEAD_DIM = D_MOBA // MOBA_HEADS
MOBA_BLOCK = 256
MOBA_TOPK = 3
MOBA_Q_CHUNK = 32
N_GROUPS = 4
EXPERTS_PER_GROUP = 8
N_EXPERTS = N_GROUPS * EXPERTS_PER_GROUP
EXPERT_TOPK = 2
D_EXPERT = 512
MOE_ROW_BLOCK = 256
IN_COLS_2 = 4 * D_MLSTM + 2 * MLSTM_HEADS + 3 * D_MOBA


def rms_norm(x, g):
    xf = x.astype(jnp.float32)
    y = xf * lax.rsqrt(jnp.mean(xf * xf, axis=-1, keepdims=True) + EPS)
    return (y * g.astype(jnp.float32)).astype(x.dtype)

def split_heads(a, n_heads):
    b, s, _ = a.shape
    return a.reshape(b, s, n_heads, -1).transpose(0, 2, 1, 3)

def merge_heads(a):
    b, h, s, d = a.shape
    return a.transpose(0, 2, 1, 3).reshape(b, s, h * d)

def causal_depthwise_conv(x, w, b):
    s = x.shape[1]
    xp = jnp.pad(x, ((0, 0), (CONV_WIDTH_2 - 1, 0), (0, 0)))
    y = b
    for j in range(CONV_WIDTH_2):
        y = y + w[j] * xp[:, j:j + s]
    return y

def mlstm_chunkwise(q, k, v, i_pre, f_pre):
    b, h, s, d = q.shape
    dv = v.shape[-1]
    nc = s // MLSTM_CHUNK
    out_dtype = v.dtype
    qf = q.astype(jnp.float32) * (d ** -0.5)
    kf = k.astype(jnp.float32)
    vf = v.astype(jnp.float32)
    log_i = i_pre.astype(jnp.float32)
    log_f = jax.nn.log_sigmoid(f_pre.astype(jnp.float32))

    def to_chunks(a):
        a = a.reshape(b, h, nc, MLSTM_CHUNK, *a.shape[3:])
        return jnp.moveaxis(a, 2, 0)

    causal = jnp.tril(jnp.ones((MLSTM_CHUNK, MLSTM_CHUNK), dtype=bool))

    def step(carry, inp):
        C, n, m = carry
        qt, kt, vt, it, ft = inp
        cum_f = jnp.cumsum(ft, axis=-1)
        cum_last = cum_f[..., -1]
        dmat = cum_f[..., :, None] - cum_f[..., None, :] + it[..., None, :]
        dmat = jnp.where(causal, dmat, -jnp.inf)
        inter = cum_f + m[..., None]
        m_t = jnp.maximum(inter, jnp.max(dmat, axis=-1))
        w_inter = jnp.exp(inter - m_t)
        sc = jnp.einsum('bhtd,bhsd->bhts', qt, kt) * jnp.exp(dmat - m_t[..., None])
        num = w_inter[..., None] * jnp.einsum('bhtd,bhde->bhte', qt, C) + jnp.einsum('bhts,bhse->bhte', sc, vt)
        den = w_inter * jnp.einsum('bhtd,bhd->bht', qt, n) + jnp.sum(sc, axis=-1)
        h_t = num / jnp.maximum(jnp.abs(den), jnp.exp(-m_t))[..., None]
        g_end = cum_last[..., None] - cum_f + it
        m_new = jnp.maximum(cum_last + m, jnp.max(g_end, axis=-1))
        w_old = jnp.exp(cum_last + m - m_new)
        w_new = jnp.exp(g_end - m_new[..., None])
        C_new = w_old[..., None, None] * C + jnp.einsum('bhs,bhsd,bhse->bhde', w_new, kt, vt)
        n_new = w_old[..., None] * n + jnp.einsum('bhs,bhsd->bhd', w_new, kt)
        return (C_new, n_new, m_new), h_t

    init = (jnp.zeros((b, h, d, dv), jnp.float32), jnp.zeros((b, h, d), jnp.float32),
            jnp.zeros((b, h), jnp.float32))
    _, hs = lax.scan(step, init, (to_chunks(qf), to_chunks(kf), to_chunks(vf),
                                  to_chunks(log_i), to_chunks(log_f)))
    return jnp.moveaxis(hs, 0, 2).reshape(b, h, s, dv).astype(out_dtype)

def moba_attention(q, k, v):
    b, h, s, d = q.shape
    nb = -(-s // MOBA_BLOCK)
    pad = nb * MOBA_BLOCK - s
    kp = jnp.pad(k.astype(jnp.float32), ((0, 0), (0, 0), (0, pad), (0, 0)))
    vp = jnp.pad(v.astype(jnp.float32), ((0, 0), (0, 0), (0, pad), (0, 0)))
    kb = kp.reshape(b, h, nb, MOBA_BLOCK, d)
    vb = vp.reshape(b, h, nb, MOBA_BLOCK, d)
    k_mean = jnp.mean(kb, axis=3)
    scale = d ** -0.5
    n_sel = min(MOBA_TOPK, nb - 1)
    bi = jnp.arange(b)[:, None, None, None]
    hi = jnp.arange(h)[None, :, None, None]
    blk_ids = jnp.arange(nb)

    def chunk(ci):
        t0 = ci * MOBA_Q_CHUNK
        qc = lax.dynamic_slice_in_dim(q, t0, MOBA_Q_CHUNK, axis=2).astype(jnp.float32)
        q_pos = t0 + jnp.arange(MOBA_Q_CHUNK)
        own = t0 // MOBA_BLOCK
        k_own = lax.dynamic_index_in_dim(kb, own, axis=2, keepdims=False)
        v_own = lax.dynamic_index_in_dim(vb, own, axis=2, keepdims=False)
        own_pos = own * MOBA_BLOCK + jnp.arange(MOBA_BLOCK)
        s_own = jnp.einsum('bhqd,bhkd->bhqk', qc, k_own) * scale
        s_own = jnp.where(own_pos[None, :] <= q_pos[:, None], s_own, -jnp.inf)
        if n_sel > 0:
            gate = jnp.einsum('bhqd,bhnd->bhqn', qc, k_mean)
            gate = jnp.where(blk_ids < own, gate, -jnp.inf)
            _, sel = lax.top_k(gate, n_sel)
            valid = sel < own
            k_sel = kb[bi, hi, sel]
            v_sel = vb[bi, hi, sel]
            s_sel = jnp.einsum('bhqd,bhqskd->bhqsk', qc, k_sel) * scale
            s_sel = jnp.where(valid[..., None], s_sel, -jnp.inf)
            p = jax.nn.softmax(jnp.concatenate(
                [s_sel.reshape(b, h, MOBA_Q_CHUNK, n_sel * MOBA_BLOCK), s_own], axis=-1), axis=-1)
            p_sel = p[..., :n_sel * MOBA_BLOCK].reshape(b, h, MOBA_Q_CHUNK, n_sel, MOBA_BLOCK)
            p_own = p[..., n_sel * MOBA_BLOCK:]
            return (jnp.einsum('bhqsk,bhqskd->bhqd', p_sel, v_sel)
                    + jnp.einsum('bhqk,bhkd->bhqd', p_own, v_own))
        p_own = jax.nn.softmax(s_own, axis=-1)
        return jnp.einsum('bhqk,bhkd->bhqd', p_own, v_own)

    outs = lax.map(chunk, jnp.arange(s // MOBA_Q_CHUNK))
    return jnp.moveaxis(outs, 0, 2).reshape(b, h, s, d).astype(q.dtype)

def hierarchical_moe(hx, w_rg, b_rg, w_re, b_re, w_gate, w_up, w_down):
    b, s, dm = hx.shape
    t = b * s
    xt = hx.reshape(t, dm)
    g_prob = jax.nn.softmax((xt @ w_rg).astype(jnp.float32) + b_rg, axis=-1)
    g_w, g_idx = lax.top_k(g_prob, 1)
    e_logits = ((xt @ w_re).astype(jnp.float32) + b_re).reshape(t, N_GROUPS, EXPERTS_PER_GROUP)
    e_logits = jnp.take_along_axis(e_logits, g_idx[:, :, None], axis=1)[:, 0]
    e_top, e_loc = lax.top_k(e_logits, EXPERT_TOPK)
    e_w = jax.nn.softmax(e_top, axis=-1) * g_w
    e_id = g_idx * EXPERTS_PER_GROUP + e_loc

    n_assign = t * EXPERT_TOPK
    flat_e = e_id.reshape(n_assign)
    flat_tok = jnp.repeat(jnp.arange(t), EXPERT_TOPK)
    flat_w = e_w.reshape(n_assign)
    order = jnp.argsort(flat_e)
    se, stok, sw = flat_e[order], flat_tok[order], flat_w[order]
    counts = jnp.zeros((N_EXPERTS,), jnp.int32).at[flat_e].add(1)
    starts = jnp.cumsum(counts) - counts
    padded = (counts + MOE_ROW_BLOCK - 1) // MOE_ROW_BLOCK * MOE_ROW_BLOCK
    pad_ends = jnp.cumsum(padded)
    pad_starts = pad_ends - padded
    dest = pad_starts[se] + (jnp.arange(n_assign) - starts[se])
    n_blocks = -(-n_assign // MOE_ROW_BLOCK) + N_EXPERTS
    rows = n_blocks * MOE_ROW_BLOCK
    x_pad = jnp.zeros((rows, dm), hx.dtype).at[dest].set(xt[stok])
    blk_expert = jnp.minimum(
        jnp.searchsorted(pad_ends, jnp.arange(n_blocks) * MOE_ROW_BLOCK, side='right'), N_EXPERTS - 1)

    def run_block(args):
        xb, e = args
        return (jax.nn.silu(xb @ w_gate[e]) * (xb @ w_up[e])) @ w_down[e]

    y_pad = lax.map(run_block, (x_pad.reshape(n_blocks, MOE_ROW_BLOCK, dm), blk_expert))
    y_sorted = y_pad.reshape(rows, dm)[dest].astype(jnp.float32)
    out = jnp.zeros((t, dm), jnp.float32).at[stok].add(y_sorted * sw[:, None])
    return out.reshape(b, s, dm).astype(hx.dtype)

def second_inputs(seed: int = 0) -> dict:
    key = jax.random.key(seed)
    ks = jax.random.split(key, 24)
    f32 = jnp.float32

    def nrm(k, shape, sc):
        return sc * jax.random.normal(k, shape, f32)

    L = DEPTH
    x = nrm(ks[0], (BATCH, SEQ, D_MODEL), 1.0)
    c = nrm(ks[1], (BATCH, D_MODEL), 1.0)
    w_ada = nrm(ks[2], (L, D_MODEL, 6 * D_MODEL), 0.5 * D_MODEL ** -0.5)
    b_ada = nrm(ks[3], (L, 6 * D_MODEL), 0.02)
    g_norm1 = 1.0 + nrm(ks[4], (L, D_MODEL), 0.02)
    w_in = nrm(ks[5], (L, D_MODEL, IN_COLS_2), D_MODEL ** -0.5)
    w_conv = nrm(ks[6], (L, CONV_WIDTH_2, 2 * D_MLSTM), CONV_WIDTH_2 ** -0.5)
    b_conv = nrm(ks[7], (L, 2 * D_MLSTM), 0.02)
    b_i = nrm(ks[8], (L, MLSTM_HEADS), 0.1)
    b_f = jnp.linspace(3.0, 6.0, MLSTM_HEADS, dtype=f32) + nrm(ks[9], (L, MLSTM_HEADS), 0.1)
    b_gates = jnp.concatenate([b_i, b_f], axis=-1)
    g_mlstm_head = 1.0 + nrm(ks[10], (L, D_MLSTM), 0.02)
    w_out = nrm(ks[11], (L, D_MIX, D_MODEL), D_MIX ** -0.5)
    g_norm2 = 1.0 + nrm(ks[12], (L, D_MODEL), 0.02)
    w_router_group = nrm(ks[13], (L, D_MODEL, N_GROUPS), D_MODEL ** -0.5)
    b_router_group = nrm(ks[14], (L, N_GROUPS), 0.01)
    w_router_expert = nrm(ks[15], (L, D_MODEL, N_EXPERTS), D_MODEL ** -0.5)
    b_router_expert = nrm(ks[16], (L, N_EXPERTS), 0.01)
    w_expert_gate = nrm(ks[17], (L, N_EXPERTS, D_MODEL, D_EXPERT), D_MODEL ** -0.5)
    w_expert_up = nrm(ks[18], (L, N_EXPERTS, D_MODEL, D_EXPERT), D_MODEL ** -0.5)
    w_expert_down = nrm(ks[19], (L, N_EXPERTS, D_EXPERT, D_MODEL), D_EXPERT ** -0.5)
    g_final = 1.0 + nrm(ks[20], (D_MODEL,), 0.02)
    return {'x': x, 'c': c, 'w_ada': w_ada, 'b_ada': b_ada, 'g_norm1': g_norm1, 'w_in': w_in,
            'w_conv': w_conv, 'b_conv': b_conv, 'b_gates': b_gates, 'g_mlstm_head': g_mlstm_head,
            'w_out': w_out, 'g_norm2': g_norm2, 'w_router_group': w_router_group,
            'b_router_group': b_router_group, 'w_router_expert': w_router_expert,
            'b_router_expert': b_router_expert, 'w_expert_gate': w_expert_gate,
            'w_expert_up': w_expert_up, 'w_expert_down': w_expert_down, 'g_final': g_final}

def second_block(x, c, w_ada, b_ada, g_norm1, w_in, w_conv, b_conv, b_gates, g_mlstm_head,
              w_out, g_norm2, w_router_group, b_router_group, w_router_expert,
              b_router_expert, w_expert_gate, w_expert_up, w_expert_down, g_final):
    split_at = np.cumsum([D_MLSTM, D_MLSTM, D_MLSTM, D_MLSTM, 2 * MLSTM_HEADS, D_MOBA, D_MOBA]).tolist()
    for l in range(DEPTH):
        mod = jax.nn.silu(c) @ w_ada[l] + b_ada[l]
        shift1, scale1, gate1, shift2, scale2, gate2 = [m[:, None, :] for m in jnp.split(mod, 6, axis=-1)]

        hn = rms_norm(x, g_norm1[l]) * (1.0 + scale1) + shift1
        proj = hn @ w_in[l]
        q_m, k_m, v_m, o_m, gates, q_a, k_a, v_a = jnp.split(proj, split_at, axis=-1)

        qk = jax.nn.silu(causal_depthwise_conv(jnp.concatenate([q_m, k_m], axis=-1), w_conv[l], b_conv[l]))
        q_m, k_m = jnp.split(qk, 2, axis=-1)
        gates = gates + b_gates[l]
        i_pre = gates[..., :MLSTM_HEADS].transpose(0, 2, 1)
        f_pre = gates[..., MLSTM_HEADS:].transpose(0, 2, 1)
        h_m = mlstm_chunkwise(split_heads(q_m, MLSTM_HEADS), split_heads(k_m, MLSTM_HEADS),
                              split_heads(v_m, MLSTM_HEADS), i_pre, f_pre)
        h_m = rms_norm(h_m, g_mlstm_head[l].reshape(MLSTM_HEADS, 1, MLSTM_HEAD_DIM))
        h_m = merge_heads(h_m) * jax.nn.sigmoid(o_m)

        h_a = merge_heads(moba_attention(split_heads(q_a, MOBA_HEADS), split_heads(k_a, MOBA_HEADS),
                                         split_heads(v_a, MOBA_HEADS)))

        mix = jnp.concatenate([h_m, h_a], axis=-1) @ w_out[l]
        x = x + gate1 * mix

        hn2 = rms_norm(x, g_norm2[l]) * (1.0 + scale2) + shift2
        ffn = hierarchical_moe(hn2, w_router_group[l], b_router_group[l], w_router_expert[l],
                               b_router_expert[l], w_expert_gate[l], w_expert_up[l], w_expert_down[l])
        x = x + gate2 * ffn
    return rms_norm(x, g_final)


def setup_inputs(seed=0):
    out = dict(first_inputs(seed))
    for name, value in second_inputs(seed + 1).items():
        if name != "x":
            out[name + "_2"] = value
    return out


def reference(
    x, norm_mix_g, w_in, b_gate, norm_v_g, w_s, b_s, conv_w, w_proj_a, w_proj_b, w_out,
    norm_ff_g, w_ff1, w_ff2, norm_final_g, c_2, w_ada_2, b_ada_2, g_norm1_2, w_in_2, w_conv_2,
    b_conv_2, b_gates_2, g_mlstm_head_2, w_out_2, g_norm2_2, w_router_group_2, b_router_group_2,
    w_router_expert_2, b_router_expert_2, w_expert_gate_2, w_expert_up_2, w_expert_down_2,
    g_final_2,
):
    x = first_block(
        x, norm_mix_g, w_in, b_gate, norm_v_g, w_s, b_s, conv_w, w_proj_a, w_proj_b, w_out,
        norm_ff_g, w_ff1, w_ff2, norm_final_g,
    )
    return second_block(
        x, c_2, w_ada_2, b_ada_2, g_norm1_2, w_in_2, w_conv_2, b_conv_2, b_gates_2,
        g_mlstm_head_2, w_out_2, g_norm2_2, w_router_group_2, b_router_group_2,
        w_router_expert_2, b_router_expert_2, w_expert_gate_2, w_expert_up_2, w_expert_down_2,
        g_final_2,
    )


_drawn_inputs = setup_inputs


def setup_inputs(seed=0):
    import zlib

    import numpy as np

    out = dict(_drawn_inputs(seed))
    spreads = {}
    factors = {'b_gate': 8.0,
     'b_ada_2': 2.906,
     'g_norm1_2': 8.0,
     'b_conv_2': 8.0,
     'g_mlstm_head_2': 8.0,
     'g_norm2_2': 5.031,
     'b_router_group_2': 8.0,
     'b_router_expert_2': 8.0,
     'g_final_2': 2.86}
    for name, (base, spread) in spreads.items():
        noise = np.random.default_rng([zlib.crc32(name.encode()), seed]).standard_normal(out[name].shape)
        drawn = base * np.exp(spread * noise) if base else spread * noise
        out[name] = __import__('jax').numpy.asarray(drawn.astype(out[name].dtype))
    for name, factor in factors.items():
        out[name] = (out[name] * factor).astype(out[name].dtype)
    return out
```

```python
import numpy as np

import concourse.bass as bass
from concourse import mybir

DT = mybir.dt
F32 = DT.float32
F32R = DT.float32r
I32 = DT.int32
ACT = mybir.ActivationFunctionType
ALU = mybir.AluOpType
AX = mybir.AxisListType.X

EPS = 1e-6
D = 1024
BIG = 1.0e30
FAR = 4096.0
NE = 32
SLOTS = 64
NOV = 8
RAW = 6
RING = 3

VEC = {}
_at = 0
for _n, _w in (("g_mix", 8), ("g_ff", 8), ("g1", 8), ("b_s", 8), ("conv", 24), ("conv2", 32), ("bconv2", 8),
               ("c", 8), ("bg", 2)):
    VEC[_n] = _at
    _at += _w
NVEC = _at
CST = {}
_at = 0
for _n, _w in (("ident", 128), ("ident2", 64), ("lt", 128), ("pen_ts", 128), ("pen_st", 128), ("iota64", 64),
               ("iota32", 32), ("ones", 128)):
    CST[_n] = _at
    _at += _w
NCST = _at


class Step:

    def __init__(self, n):
        self.n = n
        self.sem = self.value = None


class Load:

    def __init__(self, sem, value):
        self.sem, self.value = sem, value


class Queues:

    ENGINES = ("pe", "act", "dve", "pool", "sp")

    def __init__(self, who, eng, named, sems):
        self.who, self.eng, self.named, self.sems = who, eng, named, sems
        self.era = 0
        self.n = 0
        self.value = {}
        self.last = {}
        self.seen = {}

    def put(self, engine, fn, *after):
        flat, open_ = [], list(after)
        while open_:
            a = open_.pop(0)
            if isinstance(a, (list, tuple)):
                open_ += a
            elif a is not None:
                flat.append(a)
        s = Step(self.n)
        self.n += 1
        self.last[engine] = s
        if self.who is None:
            self.named.update(a.n for a in flat if isinstance(a, Step))
            return s
        if s.n in self.named:
            key = engine, self.era
            self.value[key] = self.value.get(key, 0) + 1
            s.sem, s.value = self.sems[key], self.value[key]
        if engine == self.who:
            for a in flat:
                if self.seen.get(a.sem.name, 0) < a.value:
                    self.eng.wait_ge(a.sem, a.value)
                    self.seen[a.sem.name] = a.value
            ins = fn(self.eng)
            if s.value is not None:
                ins.then_inc(s.sem, 1)
        return s


def program(nc, A, out, kept, Q):
    base = 16512
    offs = {"raw": base, "hi": base + RAW * 8192, "lo": base + (RAW + RING) * 8192,
            "slot": base + (RAW + 2 * RING) * 8192}
    rest = [offs["slot"] + 13 * 8192]

    def at(name, shape, dt, off):
        if name not in kept:
            kept[name] = nc.alloc_sbuf_tensor_at(name, shape, dt, offset=off)
        return kept[name]

    def slot(name, k, shape, dt=F32, off=0):
        n = int(np.prod(shape[1:])) * 4
        assert off + n <= 8192, name
        return at(name, shape, dt, offs["slot"] + 8192 * k + off)

    def small(name, shape, dt=F32):
        n = (int(np.prod(shape[1:])) * 4 + 31) // 32 * 32
        t = at(name, shape, dt, rest[0])
        rest[0] += n
        assert rest[0] <= 229360, name
        return t

    def sem(name):
        if name not in kept:
            kept[name] = nc.alloc_semaphore(name)
        return kept[name]

    put = Q.put
    for e in Q.ENGINES:
        for era in (0, 1):
            Q.sems[e, era] = sem(f"s_{e}{era}")

    def pe(fn, *a):
        return put("pe", fn, *a)

    def act(fn, *a):
        return put("act", fn, *a)

    def dve(fn, *a):
        return put("dve", fn, *a)

    def pool(fn, *a):
        return put("pool", fn, *a)

    def load(name, dst, src, *after, eng="act"):
        s = sem(f"l_{name}")
        put(eng, lambda e: e.dma_start(dst, src).then_inc(s, 16), *after)
        return Load(s, 16)

    cst = small("cst", [128, NCST])
    vec = small("vec", [128, NVEC])
    wr = slot("wr", 5, [128, 8, 36], F32, 4096)
    st = small("st", [128, 128])
    tab = small("tab", [128, 6, 2, 32])
    ovf = small("ovf", [128, 32], I32)

    def C(n, lo=0, hi=None, rows=slice(0, 128)):
        a = CST[n]
        w = {"ident": 128, "ident2": 64, "lt": 128, "pen_ts": 128, "pen_st": 128, "iota64": 64, "iota32": 32,
             "ones": 128}[n]
        return cst[rows, a + lo:a + (w if hi is None else hi)]

    def V(n, k, rows=slice(0, 128)):
        return vec[rows, VEC[n] + k:VEC[n] + k + 1]

    x = slot("x", 0, [128, 2, 1024])
    l_x = load("x", x[:, :, :], A["x"][0].rearrange("(t p) d -> p t d", p=128))
    l_cst = load("cst", cst[:, :], A["cst"])
    l_vec = load("vec", vec[:, :], A["vecs"])

    if "banks" not in kept:
        kept["banks"] = [nc.alloc_psum_tensor(f"bank{i}", [128, 512], F32) for i in range(8)]
    bank = kept["banks"]
    freed = [[] for _ in range(8)]
    turn = [0]
    pool_of_banks = [list(range(8))]

    def take(n=1):
        got = []
        for _ in range(n):
            got.append(pool_of_banks[0][turn[0] % len(pool_of_banks[0])])
            turn[0] += 1
        return got if n > 1 else got[0]

    raw = [at(f"raw{i}", [128, 2048], F32, offs["raw"] + 8192 * i) for i in range(RAW)]
    whi = [at(f"whi{i}", [128, 2048], F32R, offs["hi"] + 8192 * i) for i in range(RING)]
    wlo = [at(f"wlo{i}", [128, 2048], F32R, offs["lo"] + 8192 * i) for i in range(RING)]
    raw_sem = [sem(f"s_raw{i}") for i in range(RAW)]

    halves = []

    def cols(w, r0, c0):
        return ("mm", lambda: w[r0:r0 + 512, c0:c0 + 512].rearrange("(c p) n -> p c n", p=128), 4)

    def rows(w, r0):
        return ("mm", lambda: w[r0:r0 + 256, :].rearrange("(c p) n -> p c n", p=128), 2)

    def group(w, c0):
        return [cols(w, 0, c0), cols(w, 512, c0)]

    w_in, w_in2 = A["w_in"][0], A["w_in_2"][0]
    ada_at = []

    def ada(g):
        ada_at.append(len(halves))
        for k in range(2):
            kind = cols(A["w_ada_2"][0], 512 * k, 512 * g)
            halves.append(("ada", kind[1], (g, k)))

    for g in (2, 3, 0, 1, 6, 7, 8, 9, 4, 5, 10, 11, 12, 13):
        halves += group(w_in, 512 * g)
    for w in (A["w_proj_a"][0], A["w_proj_b"][0], A["w_out"][0]):
        halves += group(w, 0) + group(w, 512)
    order = [0, 1, 2, 3, 4, 5, 6, 7, 8, 9, 10, 11]
    for g in range(9):
        if g < 8:
            halves += group(A["w_ff1"][0], 512 * g)
        if g > 0:
            halves += [rows(A["w_ff2"][0], 512 * (g - 1)), rows(A["w_ff2"][0], 512 * (g - 1) + 256)]
        for _ in range(2 if g < 4 else 1):
            if order and g < 8:
                ada(order.pop(0))
    QK, VM, OM, GT, QA, KA, VA = 0, 1024, 1536, 2048, 2056, 2568, 3080
    for c0 in (QK, QK + 512, VM, OM, QA, KA, VA):
        halves += group(w_in2, c0)
    halves += group(A["w_out_2"][0], 0) + group(A["w_out_2"][0], 512)

    def expert(e, what):
        if what == "d":
            w = A["w_expert_down_2"][0, e]
            return [rows(w, 0), ("whole", *rows(w, 256)[1:])]
        return group(A["w_expert_gate_2" if what == "g" else "w_expert_up_2"][0, e], 0)

    for e in range(NE + 1):
        if e < NE:
            halves += expert(e, "g") + expert(e, "u")
        if e > 0:
            halves += expert(e - 1, "d")
    n_static = len(halves)

    def moving(name, j, r0, n_rows, chunks):
        w = A[name]

        def src(e):
            v = e.value_load(ovf[0:1, 8 + j:9 + j], min_val=0, max_val=NE - 1)
            return w[0, bass.ds(v, 1), r0:r0 + n_rows, :].rearrange("a (c p) n -> p (a c) n", p=128)
        return ("mm", src, chunks)

    for j in range(NOV + 1):
        if j < NOV:
            for n in ("w_expert_gate_2", "w_expert_up_2"):
                halves += [moving(n, j, 0, 512, 4), moving(n, j, 512, 512, 4)]
        if j > 0:
            halves += [moving("w_expert_down_2", j - 1, 0, 256, 2), moving("w_expert_down_2", j - 1, 256, 256, 2)]

    n_loaded = [0]
    read = {}
    loads = {}
    in_branch = [False]
    ids_ready = []

    def feed():
        while n_loaded[0] < (len(halves) if in_branch[0] else n_static):
            i = n_loaded[0]
            if i >= RAW and i - RAW not in read:
                return
            n_loaded[0] += 1
            kind, src, k = halves[i]
            r = i % RAW
            dst = raw[r][:, :].rearrange("p (c n) -> p c n", c=4 if kind == "ada" else k)
            if i >= n_static:
                put("sp", lambda e: e.dma_start(dst, src(e)).then_inc(raw_sem[r], 16), read[i - RAW], ids_ready)
            else:
                put("sp", lambda e: e.dma_start(dst, src()).then_inc(raw_sem[r], 16), read.get(i - RAW))
            loads[i] = Load(raw_sem[r], 16 * (i // RAW + 1))

    feed()

    n_split = [0]
    n_mm = [0]
    parts = {}
    parts_free = [[] for _ in range(RING)]
    used = [0]

    def split_ahead():
        while n_split[0] < n_loaded[0]:
            i = n_split[0]
            kind, _, info = halves[i]
            r = i % RAW
            n_split[0] += 1
            if kind == "ada":
                ada_half(i, *info)
                feed()
            elif kind == "mm":
                s = n_mm[0] % RING
                n_mm[0] += 1
                h = act(lambda e: e.activation(whi[s][:, :], raw[r][:, :], ACT.Copy), loads[i], parts_free[s])
                lo = dve(lambda e: e.tensor_tensor(wlo[s][:, :], raw[r][:, :], whi[s][:, :].bitcast(F32),
                                                   ALU.subtract), h, parts_free[s])
                parts[i] = (s, h, lo)
                read[i] = [lo]
                feed()
                return

    def next_half():
        i = used[0]
        while halves[i][0] == "ada":
            i += 1
        used[0] = i + 1
        if halves[i][0] == "whole":
            return i, i % RAW, loads[i], None
        return i, *parts.pop(i)

    def half_done(i, s, step):
        if halves[i][0] == "whole":
            read[i] = [step]
            feed()
        else:
            parts_free[s] = [step]
            split_ahead()

    def times(o, a, half, c, start, stop, *after):
        _, s, ready, lo = half
        if lo is None:
            return pe(lambda e: e.matmul(o, a.bitcast(F32), raw[s][:, c], start=start, stop=stop), ready, *after)
        pe(lambda e: e.matmul(o, a, whi[s][:, c], start=start, stop=False), ready, *after)
        return pe(lambda e: e.matmul(o, a, wlo[s][:, c], start=False, stop=stop), lo)

    sc = small("silu_c", [128, 8])
    ada_acc = [slot(f"ada_acc{k}", 10, [128, 512], F32, 2048 * k) for k in range(2)]
    ada_free = [[], []]
    ada_done = {}
    ada_mat = slot("gate1b", 7, [128, 1024]), slot("gate2b", 7, [128, 1024], F32, 4096), \
        slot("scale2b", 8, [128, 1024]), slot("shift2b", 8, [128, 1024], F32, 4096)
    gate1b, gate2b, scale2b, shift2b = ada_mat
    ada_cols = small("ada_cols", [128, 16])
    ada_tasks = []
    ada_cell = {}
    bada = [[sem(f"l_bada{k}"), 0] for k in range(2)]
    silu_c = act(lambda e: e.activation(sc[:, :], vec[:, VEC["c"]:VEC["c"] + 8], ACT.Silu), l_vec)

    def ada_half(i, g, k):
        acc = ada_acc[g % 2]
        r = i % RAW
        if k == 0:
            if any(t[0] % 2 == g % 2 for t in ada_tasks):
                ada_finish()
            z = pool(lambda e: e.memset(acc[:, :], 0.0), ada_free[g % 2])
            row = A["b_ada_2"][0:1, 512 * g:512 * g + 512]
            s = bada[g % 2]
            s[1] += 16
            put("pool", lambda e: e.dma_start(acc[0:1, :], row).then_inc(s[0], 16), z)
            ada_cell["b", g] = Load(s[0], s[1])
        last = ada_cell.get(("last", g))
        for c in range(4):
            last = dve(lambda e, c=c: e.scalar_tensor_tensor(
                out=acc[:, :], in0=raw[r][:, 512 * c:512 * c + 512], scalar=sc[:, 4 * k + c:4 * k + c + 1],
                in1=acc[:, :], op0=ALU.mult, op1=ALU.add), loads[i], silu_c, ada_cell["b", g], last)
        read[i] = [last]
        ada_cell["last", g] = last
        if k == 1:
            ada_tasks.append((g, last))

    def ada_finish():
        while ada_tasks:
            g, ready = ada_tasks.pop(0)
            acc = ada_acc[g % 2]
            b = take()
            if g < 4:
                for c in range(4):
                    m = pe(lambda e, c=c: e.matmul(bank[b][:, c:c + 1], acc[:, 128 * c:128 * c + 128],
                                                   C("ones", 0, 1), start=True, stop=True), ready, freed[b], l_cst)
                ev = dve(lambda e: e.tensor_copy(ada_cols[:, 4 * g:4 * g + 4], bank[b][:, 0:4]), m)
            else:
                t = [gate1b, shift2b, scale2b, gate2b][g // 2 - 2]
                m = pe(lambda e: e.matmul(bank[b][:, :], C("ones"), acc[:, :], start=True, stop=True),
                       ready, freed[b], l_cst)
                ev = dve(lambda e: e.tensor_copy(t[:, 512 * (g % 2):512 * (g % 2) + 512], bank[b][:, :]), m,
                         ada_dst_free)
            freed[b] = [ev]
            ada_free[g % 2] = [m]
            ada_done[g] = ev

    ada_dst_free = []

    def dense(xh, xl, x_ready, n_halves=2, banks=None):
        b = take(2)
        last = None
        total = 4 * n_halves
        for hf in range(n_halves):
            i, s, h, lo = next_half()
            for c in range(4):
                k = 4 * hf + c
                for t in range(2):
                    o = bank[b[t]][:, :]
                    a_h, a_l = xh[:, k, 128 * t:128 * t + 128], xl[:, k, 128 * t:128 * t + 128]
                    r_h, r_l = whi[s][:, 512 * c:512 * c + 512], wlo[s][:, 512 * c:512 * c + 512]
                    pe(lambda e, o=o, a=a_h, r=r_h, f=(k == 0): e.matmul(o, a, r, start=f, stop=False),
                       h, x_ready, freed[b[t]] if k == 0 else None)
                    pe(lambda e, o=o, a=a_h, r=r_l: e.matmul(o, a, r, start=False, stop=False), lo)
                    last = pe(lambda e, o=o, a=a_l, r=r_h, f=(k == total - 1): e.matmul(
                        o, a, r, start=False, stop=f))
            half_done(i, s, last)
        return b, last

    def stat(k, n=1):
        return st[:, k:k + n]

    def rms(src, n, k0, junk, after):
        sq = [act(lambda e, t=t: e.activation(junk[:, t, :], src[:, t, :], ACT.Square,
                                              accum_out=stat(k0 + t)), after) for t in range(2)]
        a = dve(lambda e: e.tensor_scalar(stat(k0 + 2, 2), stat(k0, 2), 1.0 / n, EPS, ALU.mult, ALU.add), sq)
        b = act(lambda e: e.activation(stat(k0 + 4, 2), stat(k0 + 2, 2), ACT.Sqrt), a)
        return dve(lambda e: e.reciprocal(stat(k0, 2), stat(k0 + 4, 2)), b)

    def scaled(dst, src, k0, r, after):
        a = dve(lambda e: e.tensor_scalar(dst[:, 0, :], src[:, 0, :], stat(k0), None, ALU.mult), r, after)
        b = act(lambda e: e.activation(dst[:, 1, :], src[:, 1, :], ACT.Copy, scale=stat(k0 + 1)), r, after)
        return [a, b]

    def turned(src, chunks, ready, use):
        n = len(chunks)
        outs = []
        for k in range(n // 2):
            b = take()
            for c in range(2):
                for t in range(2):
                    piece = src(t, chunks[2 * k + c])
                    m = pe(lambda e: e.transpose(
                        bank[b][:, 256 * c + 128 * t:256 * c + 128 * t + 128], piece, C("ident")), ready, freed[b], l_cst)
            r = use(k, bank[b], m)
            freed[b] = list(r)
            outs += list(r)
        return outs

    def hi_lo(dh, dl, after=None):
        def use(k, b, m):
            o = slice(2 * k, 2 * k + 2)
            src = b[:, :].rearrange("p (c t) -> p c t", c=2)
            h = act(lambda e: e.activation(dh[:, o, :], src, ACT.Copy), m, after)
            lo = dve(lambda e: e.tensor_tensor(dl[:, o, :], src, dh[:, o, :].bitcast(F32), ALU.subtract), h, after)
            return h, lo
        return use

    def hi_lo_scaled(dh, dl, name, after=None):
        def use(k, b, m):
            out = []
            for c in range(2):
                ch = 2 * k + c
                s = b[:, 256 * c:256 * c + 256]
                h = act(lambda e, s=s, ch=ch: e.activation(dh[:, ch, :], s, ACT.Copy, scale=V(name, ch)),
                        m, after, l_vec)
            for c in range(2):
                ch = 2 * k + c
                s = b[:, 256 * c:256 * c + 256]
                out.append(dve(lambda e, s=s, ch=ch: e.scalar_tensor_tensor(
                    out=dl[:, ch, :], in0=s, scalar=V(name, ch), in1=dh[:, ch, :].bitcast(F32),
                    op0=ALU.mult, op1=ALU.subtract), h, after))
                out.append(h)
            return out
        return use

    def tok(t, n0, n1):
        return t[:, :, n0:n1]

    dbg = A.get("_dbg")
    n_dbg = [0]

    def dump(name, ap, ready):
        if dbg is not None and name in dbg:
            d = load(f"dbg_{name}", dbg[name], ap, ready, eng="sp")
            for q in Q.ENGINES:
                put(q, lambda e: None, d)

    ws = slot("ws", 8, [128, 8, 128])
    gvb = slot("gvb", 8, [128, 1024], F32, 4096)
    z_ws = dve(lambda e: e.memset(ws[64:128, :, 0:64], 0.0))
    l_ws0 = load("ws0", ws[0:64, :, :], A["w_sT"][0:64])
    l_ws1 = load("ws1", ws[64:128, :, 64:128], A["w_sT"][64:128, :, 64:128])
    l_gvb = load("gvb", gvb[:, :], A["norm_v_g"].broadcast_to([128, 1024]))

    hh = slot("hh", 1, [128, 8, 256], F32R)
    hl = slot("hl", 2, [128, 8, 256], F32R)
    xn = slot("xn", 3, [128, 2, 1024])
    r = rms(x, D, 0, xn, l_x)
    xn_ready = scaled(xn, x, 0, r, None)
    for _ in range(RING):
        split_ahead()
    h_ready = turned(lambda t, c: xn[:, t, 128 * c:128 * c + 128], range(8), xn_ready, hi_lo_scaled(hh, hl, "g_mix"))
    dump("hh", hh[:, :, :].bitcast(F32), h_ready)

    vt = slot("vt", 3, [128, 2, 1024])
    ut = slot("ut", 4, [128, 2, 1024])

    def gelu_into(dst):
        out = []
        for g in range(2):
            b, m = dense(hh, hl, h_ready)
            for t in range(2):
                s = act(lambda e, t=t, g=g, b=b: e.activation(dst[:, t, 512 * g:512 * g + 512], bank[b[t]][:, :],
                                                              ACT.Gelu), m, h_ready)
                freed[b[t]] = [s]
                out.append(s)
        return out

    v_ready = gelu_into(vt)
    bgb = slot("bgb", 9, [128, 2048])
    l_bgb = load("bgb", bgb[:, :], A["b_gate"].broadcast_to([128, 2048]), v_ready[0], eng="pool")
    nfb = slot("nfb", 10, [128, 1024], F32, 4096)
    l_nfb = load("nfb", nfb[:, :], A["norm_final_g"].broadcast_to([128, 1024]), v_ready[0], eng="pool")
    junk5 = slot("junk5", 5, [128, 2, 1024])
    r = rms(vt, D, 8, junk5, v_ready)
    vs = [dve(lambda e, t=t: e.scalar_tensor_tensor(out=vt[:, t, :], in0=vt[:, t, :], scalar=stat(8 + t),
                                                   in1=gvb[:, :], op0=ALU.mult, op1=ALU.mult), r, l_gvb)
          for t in range(2)]
    u_ready = gelu_into(ut)
    a_steps = []
    for t in range(2):
        for q in range(2):
            b = take()
            for g in range(4):
                gg = 4 * q + g
                m = pe(lambda e, t=t, g=g, gg=gg, b=b: e.matmul(
                    bank[b][:, 128 * g:128 * g + 128], ws[:, gg, :], vt[:, t, 128 * gg:128 * gg + 128],
                    start=True, stop=True), vs, z_ws, l_ws0, l_ws1, freed[b])
            fr = []
            for g in range(4):
                gg = 4 * q + g
                fr.append(dve(lambda e, t=t, g=g, gg=gg, b=b: e.scalar_tensor_tensor(
                    out=ut[:, t, 128 * gg:128 * gg + 128], in0=bank[b][:, 128 * g:128 * g + 128],
                    scalar=V("b_s", gg), in1=ut[:, t, 128 * gg:128 * gg + 128], op0=ALU.add, op1=ALU.mult),
                    m, u_ready, l_vec))
            freed[b] = fr
            mixed = m
            a_steps += fr
    dump("a", ut[:, :, :], a_steps)

    zt = slot("zt", 3, [128, 2, 1024])
    z_ready = []
    cg = []
    for g in range(2):
        b, m = dense(hh, hl, h_ready)
        for t in range(2):
            s = act(lambda e, t=t, g=g, b=b: e.activation(zt[:, t, 512 * g:512 * g + 512], bank[b[t]][:, :],
                                                          ACT.Copy), m, mixed)
            freed[b[t]] = [s]
            cg.append(s)
    ah = slot("ah", 5, [128, 8, 256], F32R)
    al = slot("al", 6, [128, 8, 256], F32R)
    a_ready = turned(lambda t, c: ut[:, t, 128 * c:128 * c + 128], range(8), a_steps, hi_lo(ah, al, vs))
    for g in range(2):
        b, m = dense(hh, hl, h_ready)
        for t in range(2):
            s = dve(lambda e, t=t, g=g, b=b: e.tensor_tensor(
                zt[:, t, 512 * g:512 * g + 512], zt[:, t, 512 * g:512 * g + 512], bank[b[t]][:, :], ALU.mult),
                m, cg)
            freed[b[t]] = [s]
            z_ready.append(s)
    b, m = dense(hh, hl, h_ready)
    first_bg = (b, m)
    zT = slot("zT", 4, [128, 8, 256])

    def plain(dst, after=None):
        def use(k, b, m):
            src = b[:, :].rearrange("p (c t) -> p c t", c=2)
            return [act(lambda e: e.activation(dst[:, 2 * k:2 * k + 2, :], src, ACT.Copy), m, after)]
        return use

    zT_ready = turned(lambda t, c: zt[:, t, 128 * c:128 * c + 128], range(8), z_ready, plain(zT, a_ready))
    bt = slot("bt", 3, [128, 2, 1024])
    b_ready = []
    for g in range(2):
        b, m = first_bg if g == 0 else dense(hh, hl, h_ready)
        for t in range(2):
            s = act(lambda e, t=t, g=g, b=b: e.activation(bt[:, t, 512 * g:512 * g + 512], bank[b[t]][:, :],
                                                          ACT.Copy), m, zT_ready)
            freed[b[t]] = [s]
            b_ready.append(s)
    y = slot("y", 7, [128, 8, 256])
    y_ready = []
    for c in range(8):
        s = dve(lambda e, c=c: e.tensor_scalar(y[:, c, :], zT[:, c, :], V("conv", 16 + c), None, ALU.mult),
                zT_ready, l_vec)
        for k, d in ((1, 1), (0, 2)):
            s = dve(lambda e, c=c, k=k, d=d: e.scalar_tensor_tensor(
                out=y[:, c, d:256], in0=zT[:, c, 0:256 - d], scalar=V("conv", 8 * k + c), in1=y[:, c, d:256],
                op0=ALU.mult, op1=ALU.add), s)
        y_ready.append(s)
    ga = slot("ga", 3, [128, 2, 1024])
    gate_raw = dense(hh, hl, h_ready)
    ch = slot("ch", 8, [128, 8, 256], F32R)
    cl = slot("cl", 4, [128, 8, 256], F32R)

    def into_c(k, b, m):
        o = slice(2 * k, 2 * k + 2)
        src = b[:, :].rearrange("p (c t) -> p c t", c=2)
        p = dve(lambda e: e.tensor_tensor(y[:, o, :], y[:, o, :], src, ALU.mult), m, y_ready)
        h = act(lambda e: e.activation(ch[:, o, :], y[:, o, :], ACT.Copy), p, mixed, vs)
        lo = dve(lambda e: e.tensor_tensor(cl[:, o, :], y[:, o, :], ch[:, o, :].bitcast(F32), ALU.subtract),
                 h, y_ready)
        return p, h, lo

    c_ready = turned(lambda t, c: bt[:, t, 128 * c:128 * c + 128], range(8), b_ready, into_c)
    dump("cT", y[:, :, :], c_ready)
    gb = slot("gb", 7, [128, 2, 1024])
    sig = {0: [], 1: []}
    for which, dst in ((0, ga), (1, gb)):
        for g in range(2):
            b, m = gate_raw if (which, g) == (0, 0) else dense(hh, hl, h_ready)
            for t in range(2):
                o = slice(512 * g, 512 * g + 512)
                q = slice(1024 * which + 512 * g, 1024 * which + 512 * g + 512)
                s = dve(lambda e, t=t, o=o, q=q, b=b, dst=dst: e.tensor_tensor(
                    dst[:, t, o], bank[b[t]][:, :], bgb[:, q], ALU.add), m, l_bgb, c_ready)
                freed[b[t]] = [s]
                sig[which].append(act(lambda e, t=t, o=o, dst=dst: e.activation(
                    dst[:, t, o], dst[:, t, o], ACT.Sigmoid), s))
    hh_done = m
    m_ready = []
    for which, xh_, xl_, rd, dst in ((0, ah, al, a_ready, ga), (1, ch, cl, c_ready, gb)):
        for g in range(2):
            b, m = dense(xh_, xl_, rd)
            for t in range(2):
                o = slice(512 * g, 512 * g + 512)
                s = dve(lambda e, t=t, o=o, b=b, dst=dst: e.tensor_tensor(
                    dst[:, t, o], dst[:, t, o], bank[b[t]][:, :], ALU.mult), m, sig[which])
                freed[b[t]] = [s]
                if which:
                    s = dve(lambda e, t=t, o=o: e.tensor_tensor(
                        ga[:, t, o], ga[:, t, o], gb[:, t, o], ALU.add), s)
                    m_ready.append(s)
    proj_done = m
    ada_dst_free += [m, m_ready[-1]]
    dump("m", ga[:, :, :], m_ready)
    mh = slot("mh", 1, [128, 8, 256], F32R)
    ml = slot("ml", 2, [128, 8, 256], F32R)
    mT_ready = turned(lambda t, c: ga[:, t, 128 * c:128 * c + 128], range(8), m_ready, hi_lo(mh, ml, hh_done))

    def residual(g, b, m, x, after=None):
        out = []
        for t in range(2):
            o = slice(512 * g, 512 * g + 512)
            s = dve(lambda e, t=t, o=o, b=b: e.tensor_tensor(x[:, t, o], x[:, t, o], bank[b[t]][:, :], ALU.add),
                    m, after)
            freed[b[t]] = [s]
            out.append(s)
        return out

    x_ready = []
    for g in range(2):
        b, m = dense(mh, ml, mT_ready)
        x_ready += residual(g, b, m, x)
    mm_out = m
    dump("x1", x[:, :, :], x_ready)

    xn2 = slot("xn2", 3, [128, 2, 1024])
    r = rms(x, D, 16, xn2, [*x_ready, *mT_ready])
    xn_ready = scaled(xn2, x, 16, r, None)
    fh = slot("fh", 5, [128, 8, 256], F32R)
    fl = slot("fl", 6, [128, 8, 256], F32R)
    f_ready = turned(lambda t, c: xn2[:, t, 128 * c:128 * c + 128], range(8), xn_ready,
                     hi_lo_scaled(fh, fl, "g_ff", proj_done))
    pool_of_banks[0] = [0, 1, 2, 3]
    zz = [slot(f"zz{k}", 3, [128, 2, 512], F32, 4096 * k) for k in range(2)]
    zh = [slot(f"zh{k}", 1, [128, 4, 256], F32R, 4096 * k) for k in range(2)]
    zl = [slot(f"zl{k}", 2, [128, 4, 256], F32R, 4096 * k) for k in range(2)]
    zz_free = [list(f_ready), list(f_ready)]
    z2_free = [[mm_out], [mm_out]]
    ff_b = [4, 5, 6, 7]
    zr = {}
    zT2 = {}
    for g in range(9):
        if g < 8:
            b, m = dense(fh, fl, f_ready)
            zr[g] = []
            for t in range(2):
                s = act(lambda e, t=t, b=b, g=g: e.activation(zz[g % 2][:, t, :], bank[b[t]][:, :], ACT.Relu),
                        m, zz_free[g % 2])
                freed[b[t]] = [s]
                zr[g].append(dve(lambda e, t=t, g=g: e.tensor_tensor(
                    zz[g % 2][:, t, :], zz[g % 2][:, t, :], zz[g % 2][:, t, :], ALU.mult), s))
        if g > 0:
            p = g - 1
            for hf in range(2):
                i, s, h, lo = next_half()
                for c in range(2):
                    f = 2 * hf + c
                    for t in range(2):
                        for which, lhs in ((0, zh), (1, zl)):
                            a = lhs[p % 2][:, f, 128 * t:128 * t + 128]
                            for n in range(2):
                                o = bank[ff_b[2 * t + n]][:, :]
                                r_h = whi[s][:, 1024 * c + 512 * n:1024 * c + 512 * n + 512]
                                r_l = wlo[s][:, 1024 * c + 512 * n:1024 * c + 512 * n + 512]
                                first = p == 0 and f == 0 and which == 0
                                end = p == 7 and f == 3 and which == 1
                                m = pe(lambda e, o=o, a=a, r=r_h, i=first, j=end: e.matmul(
                                    o, a, r, start=i, stop=j), h, zT2[p], freed[ff_b[2 * t + n]] if first else None)
                                if which == 0:
                                    m = pe(lambda e, o=o, a=a, r=r_l: e.matmul(o, a, r, start=False, stop=False),
                                           lo)
                half_done(i, s, m)
            z2_free[p % 2] = [m]
        if g < 8:
            zT2[g] = turned(lambda t, c: zz[g % 2][:, t, 128 * c:128 * c + 128], range(4), zr[g],
                            hi_lo(zh[g % 2], zl[g % 2], z2_free[g % 2]))
            zz_free[g % 2] = [Q.last["pe"]]
        ada_finish()
    ff_done = m
    x_ready = []
    for t in range(2):
        for n in range(2):
            o = slice(512 * n, 512 * n + 512)
            b = ff_b[2 * t + n]
            s = dve(lambda e, t=t, o=o, b=b: e.tensor_tensor(x[:, t, o], x[:, t, o], bank[b][:, :], ALU.add), m)
            freed[b] = [s]
            x_ready.append(s)
    dump("x2", x[:, :, :], x_ready)
    pool_of_banks[0] = list(range(8))
    ada_finish()

    junk3 = slot("junk3", 3, [128, 2, 1024])
    r = rms(x, D, 24, junk3, [*x_ready, ff_done])
    x_ready = [dve(lambda e, t=t: e.scalar_tensor_tensor(
        out=x[:, t, :], in0=x[:, t, :], scalar=stat(24 + t), in1=nfb[:, :], op0=ALU.mult, op1=ALU.mult),
        r, l_nfb) for t in range(2)]
    dump("xb", x[:, :, :], x_ready)
    r = rms(x, D, 32, junk3, x_ready)
    xn_ready = scaled(junk3, x, 32, r, None)
    a1 = small("a1", [128, 8])
    a1_ready = dve(lambda e: e.scalar_tensor_tensor(
        out=a1[:, :], in0=ada_cols[:, 8:16], scalar=1.0, in1=vec[:, VEC["g1"]:VEC["g1"] + 8], op0=ALU.add,
        op1=ALU.mult), ada_done[2], ada_done[3], l_vec)
    nh = slot("nh", 5, [128, 8, 256], F32R)
    nl = slot("nl", 6, [128, 8, 256], F32R)
    nf = slot("nf", 4, [128, 8, 256])

    def modulated(k, b, m):
        out = []
        for c in range(2):
            q = 2 * k + c
            src = b[:, 256 * c:256 * c + 256]
            f = dve(lambda e, q=q, src=src: e.tensor_scalar(
                nf[:, q, :], src, a1[:, q:q + 1], ada_cols[:, q:q + 1], ALU.mult, ALU.add), m, a1_ready,
                ada_done[0], ada_done[1], proj_done)
            out.append(f)
        o = slice(2 * k, 2 * k + 2)
        h = act(lambda e: e.activation(nh[:, o, :], nf[:, o, :], ACT.Copy), out, ff_done)
        lo = dve(lambda e: e.tensor_tensor(nl[:, o, :], nf[:, o, :], nh[:, o, :].bitcast(F32), ALU.subtract),
                 h, ff_done)
        return out + [h, lo]

    n_ready = turned(lambda t, c: junk3[:, t, 128 * c:128 * c + 128], range(8), xn_ready, modulated)
    dump("nf", nf[:, :, :], n_ready)
    gw = slot("gw", 10, [128, 8, 8])
    gwh = slot("gwh", 9, [128, 8, 128], F32R)
    gwl = slot("gwl", 9, [128, 8, 128], F32R, 4096)
    l_gw = load("gw", gw[:, :, :], w_in2[:, GT:GT + 8].rearrange("(c p) n -> p c n", p=128), ff_done,
                ada_done[11], eng="pool")
    zg = [pool(lambda e: e.memset(gwh[:, :, :].bitcast(F32), 0.0), ff_done),
          pool(lambda e: e.memset(gwl[:, :, :].bitcast(F32), 0.0), ff_done)]
    gs = []
    for k in range(2):
        o, i_ = slice(32 * k, 32 * k + 4), slice(4 * k, 4 * k + 4)
        h = dve(lambda e, o=o, i_=i_: e.tensor_copy(gwh[:, :, o], gw[:, :, i_]), l_gw, zg)
        gs.append(dve(lambda e, o=o, i_=i_: e.tensor_tensor(gwl[:, :, o], gw[:, :, i_], gwh[:, :, o].bitcast(F32),
                                                            ALU.subtract), h))
    b = take()
    for c in range(8):
        for a_, r_ in ((gwh, nh), (gwh, nl), (gwl, nh)):
            m = pe(lambda e, a_=a_, r_=r_, c=c, b=b, i=(c == 0 and a_ is gwh and r_ is nh),
                   j=(c == 7 and a_ is gwl): e.matmul(bank[b][:, 0:256], a_[:, c, :], r_[:, c, :],
                                                      start=i, stop=j), gs, n_ready, freed[b])
    gates_mm = m
    R = {}
    for k, n in enumerate(("i", "f", "w0", "w1")):
        R[n] = slot(f"row_{n}", 10, [4, 256], F32, 2048 + 1024 * k)
    for k, n in enumerate(("F", "M")):
        R[n] = slot(f"row_{n}", 10, [4, 256], F32, 6144 + 1024 * k)
    rd = [gates_mm, x_ready, ada_done[11]]
    s1 = dve(lambda e, b=b: e.tensor_scalar(R["i"][:, :], bank[b][0:4, 0:256], V("bg", 0, slice(0, 4)), None,
                                            ALU.add), rd)
    s2 = dve(lambda e, b=b: e.tensor_scalar(R["f"][:, :], bank[b][32:36, 0:256], V("bg", 1, slice(32, 36)), None,
                                            ALU.add), rd)
    freed[b] = [s1, s2]
    s3 = dve(lambda e: e.tensor_scalar(R["w0"][:, :], R["f"][:, :], -1.0, None, ALU.mult), s2)
    s3 = dve(lambda e: e.tensor_tensor(R["w0"][:, :], R["w0"][:, :], R["f"][:, :], ALU.min), s3)
    s3 = act(lambda e: e.activation(R["w0"][:, :], R["w0"][:, :], ACT.Exp), s3)
    s3 = dve(lambda e: e.tensor_scalar(R["w0"][:, :], R["w0"][:, :], 1.0, None, ALU.add), s3)
    s3 = act(lambda e: e.activation(R["w0"][:, :], R["w0"][:, :], ACT.Ln), s3)
    s3 = dve(lambda e: e.scalar_tensor_tensor(out=R["f"][:, :], in0=R["f"][:, :], scalar=0.0, in1=R["w0"][:, :],
                                              op0=ALU.min, op1=ALU.subtract), s3)
    z1 = dve(lambda e: e.memset(R["w1"][:, :], 0.0), rd)
    s4 = dve(lambda e: e.tensor_tensor_scan(R["F"][:, :], R["f"][:, :], R["w1"][:, :], 0.0, ALU.add, ALU.add),
             s3, z1)
    s5 = dve(lambda e: e.tensor_tensor(R["i"][:, :], R["i"][:, :], R["F"][:, :], ALU.subtract), s4, s1)
    s6 = dve(lambda e: e.tensor_tensor_scan(R["M"][:, :], R["i"][:, :], R["w1"][:, :], 0.0, ALU.max, ALU.max), s5)
    s7 = dve(lambda e: e.tensor_tensor(R["w0"][:, :], R["F"][:, :], R["M"][:, :], ALU.add), s6)
    s7 = act(lambda e: e.activation(R["w0"][:, :], R["w0"][:, :], ACT.Exp, scale=-1.0), s7)
    acol = small("acol", [128, 2, 4])
    ecol = small("ecol", [128, 2, 4])

    qt = slot("qt", 3, [128, 2, 1024])
    q_ready = []
    for g in range(2):
        b, m = dense(nh, nl, n_ready)
        for t in range(2):
            s = act(lambda e, t=t, g=g, b=b: e.activation(qt[:, t, 512 * g:512 * g + 512], bank[b[t]][:, :],
                                                          ACT.Copy), m, n_ready)
            freed[b[t]] = [s]
            q_ready.append(s)
    b = take()
    for k, (n, rdy) in enumerate((("i", s5), ("w0", s7))):
        for t in range(2):
            m = pe(lambda e, n=n, t=t, k=k, b=b: e.transpose(
                bank[b][:, 8 * k + 4 * t:8 * k + 4 * t + 4], R[n][:, 128 * t:128 * t + 128],
                cst[0:4, CST["ident"]:CST["ident"] + 4]), rdy, freed[b])
    col1 = dve(lambda e, b=b: e.tensor_copy(acol[:, :, :], bank[b][:, 0:8].rearrange("p (t h) -> p t h", t=2)), m)
    col2 = dve(lambda e, b=b: e.tensor_copy(ecol[:, :, :], bank[b][:, 8:16].rearrange("p (t h) -> p t h", t=2)), m)
    freed[b] = [col1, col2]
    ET = slot("ET", 9, [128, 4, 2, 256])
    e_ready = {}
    for h in range(4):
        b = take()
        m = pe(lambda e, h=h, b=b: e.matmul(
            bank[b][:, 0:256], cst[0:4, CST["ident"] + h:CST["ident"] + h + 1].to_broadcast([4, 128]),
            R["M"][:, :], start=True, stop=True), s6, freed[b])
        fr = []
        for s_ in range(2):
            o = slice(128 * s_, 256)
            d = dve(lambda e, h=h, s_=s_, o=o, b=b: e.tensor_scalar(
                ET[:, h, s_, o], bank[b][:, o], acol[:, s_, h:h + 1], 0.0, ALU.subtract, ALU.max), m, col1,
                gates_mm)
            fr.append(d)
            d = dve(lambda e, h=h, s_=s_: e.tensor_tensor(
                ET[:, h, s_, 128 * s_:128 * s_ + 128], ET[:, h, s_, 128 * s_:128 * s_ + 128], C("pen_st"),
                ALU.add), d)
            e_ready[h, s_] = act(lambda e, h=h, s_=s_, o=o: e.activation(ET[:, h, s_, o], ET[:, h, s_, o],
                                                                       ACT.Exp, scale=-1.0), d)
        freed[b] = fr
    vmt = slot("vmt", 2, [128, 2, 512])
    vat = slot("vat", 2, [128, 2, 512], F32, 4096)
    omt = slot("omt", 1, [128, 2, 512])
    b, m = dense(nh, nl, n_ready)
    vm_ready = []
    for t in range(2):
        s = act(lambda e, t=t, b=b: e.activation(vmt[:, t, :], bank[b[t]][:, :], ACT.Copy), m)
        freed[b[t]] = [s]
        vm_ready.append(s)
    qT = slot("qT", 4, [128, 8, 256])
    qT_ready = turned(lambda t, c: qt[:, t, 128 * c:128 * c + 128], range(8), q_ready, plain(qT, n_ready))
    b, m = dense(nh, nl, n_ready)
    om_ready = []
    for t in range(2):
        s = act(lambda e, t=t, b=b: e.activation(omt[:, t, :], bank[b[t]][:, :], ACT.Sigmoid), m)
        freed[b[t]] = [s]
        om_ready.append(s)
    qc = slot("qc", 3, [128, 8, 256])
    qc_ready = []
    for c in range(8):
        s = dve(lambda e, c=c: e.tensor_scalar(qc[:, c, :], qT[:, c, :], V("conv2", 24 + c), V("bconv2", c),
                                               ALU.mult, ALU.add), qT_ready)
        for k, d in ((2, 1), (1, 2), (0, 3)):
            s = dve(lambda e, c=c, k=k, d=d: e.scalar_tensor_tensor(
                out=qc[:, c, d:256], in0=qT[:, c, 0:256 - d], scalar=V("conv2", 8 * k + c), in1=qc[:, c, d:256],
                op0=ALU.mult, op1=ALU.add), s)
        qc_ready.append(act(lambda e, c=c: e.activation(qc[:, c, :], qc[:, c, :], ACT.Silu), s))
    dump("qc", qc[:, :, :], qc_ready)
    qa = slot("qa", 4, [128, 2, 1024])
    qa_ready = []
    for g in range(2):
        b, m = dense(nh, nl, n_ready)
        for t in range(2):
            s = act(lambda e, t=t, g=g, b=b: e.activation(qa[:, t, 512 * g:512 * g + 512], bank[b[t]][:, :],
                                                          ACT.Copy), m, qc_ready)
            freed[b[t]] = [s]
            qa_ready.append(s)
    MSC = 128 ** -0.5
    ASC = 64 ** -0.5
    sc_ready = {}
    for h in range(4):
        b = take()
        for s_ in range(2):
            o = slice(128 * s_, 256)
            po = slice(256 * s_ + 128 * s_, 256 * s_ + 256)
            m = pe(lambda e, h=h, s_=s_, o=o, po=po, b=b: e.matmul(
                bank[b][:, po], qc[:, 4 + h, 128 * s_:128 * s_ + 128], qc[:, h, o], start=True, stop=True),
                qc_ready, freed[b])
        for s_ in range(2):
            o = slice(128 * s_, 256)
            po = slice(256 * s_ + 128 * s_, 256 * s_ + 256)
            sc_ready[h, s_] = dve(lambda e, h=h, s_=s_, o=o, po=po, b=b: e.scalar_tensor_tensor(
                out=ET[:, h, s_, o], in0=bank[b][:, po], scalar=MSC, in1=ET[:, h, s_, o], op0=ALU.mult,
                op1=ALU.mult), m, e_ready[h, s_])
        freed[b] = [sc_ready[h, 0], sc_ready[h, 1]]
    b, m = dense(nh, nl, n_ready)
    va_ready = []
    for t in range(2):
        s = act(lambda e, t=t, b=b: e.activation(vat[:, t, :], bank[b[t]][:, :], ACT.Copy), m)
        freed[b[t]] = [s]
        va_ready.append(s)
    nh_done = m
    mix = slot("mix", 10, [128, 2, 1024])
    rows_done = [s7, col1, col2, *e_ready.values(), gs[-1]]
    junk1 = slot("junk1", 1, [128, 128], F32, 4096)
    hm_last = []
    for t in range(2):
        b = take()
        dn = take()
        for h in range(4):
            for s_ in range(t + 1):
                lhs = ET[:, h, s_, 128 * t:128 * t + 128]
                pe(lambda e, h=h, s_=s_, t=t, lhs=lhs, b=b: e.matmul(
                    bank[b][:, 128 * h:128 * h + 128], lhs, vmt[:, s_, 128 * h:128 * h + 128],
                    start=(s_ == 0), stop=(s_ == t)), sc_ready[h, s_], vm_ready, freed[b])
            for s_ in range(t + 1):
                lhs = ET[:, h, s_, 128 * t:128 * t + 128]
                m = pe(lambda e, h=h, s_=s_, t=t, lhs=lhs, dn=dn: e.matmul(
                    bank[dn][:, h:h + 1], lhs, C("ones", 0, 1), start=(s_ == 0), stop=(s_ == t)), freed[dn])
        k = 40 + 16 * t
        d1 = dve(lambda e, k=k, dn=dn: e.tensor_scalar(stat(k, 4), bank[dn][:, 0:4], -1.0, None, ALU.mult), m)
        d2 = dve(lambda e, k=k, dn=dn: e.tensor_tensor(stat(k, 4), stat(k, 4), bank[dn][:, 0:4], ALU.max), d1)
        d3 = dve(lambda e, k=k, t=t: e.tensor_tensor(stat(k, 4), stat(k, 4), ecol[:, t, :], ALU.max), d2)
        d4 = dve(lambda e, k=k: e.reciprocal(stat(k, 4), stat(k, 4)), d3)
        freed[dn] = [d2]
        hs, ss = [], []
        for h in range(4):
            o = slice(128 * h, 128 * h + 128)
            s = dve(lambda e, t=t, h=h, o=o, k=k, b=b: e.tensor_scalar(
                mix[:, t, o], bank[b][:, o], stat(k + h), None, ALU.mult), d4, m, rows_done)
            hs.append(s)
            ss.append(act(lambda e, t=t, h=h, o=o, k=k: e.activation(junk1[:, :], mix[:, t, o], ACT.Square,
                                                                    accum_out=stat(k + 4 + h)), s,
                          ss[-1] if ss else hm_last[-1:]))
        freed[b] = hs
        d = dve(lambda e, k=k: e.tensor_scalar(stat(k + 8, 4), stat(k + 4, 4), 1.0 / 128, EPS, ALU.mult, ALU.add),
                ss)
        d = act(lambda e, k=k: e.activation(stat(k + 8, 4), stat(k + 8, 4), ACT.Sqrt), d)
        d = dve(lambda e, k=k: e.reciprocal(stat(k + 8, 4), stat(k + 8, 4)), d)
        for h in range(4):
            o = slice(128 * h, 128 * h + 128)
            s = dve(lambda e, t=t, h=h, o=o, k=k: e.scalar_tensor_tensor(
                out=mix[:, t, o], in0=mix[:, t, o], scalar=stat(k + 8 + h), in1=omt[:, t, o], op0=ALU.mult,
                op1=ALU.mult), d, om_ready)
            hm_last.append(s)
    msc_done = m
    qaT = slot("qaT", 3, [128, 8, 256])
    qaT_ready = turned(lambda t, c: qa[:, t, 128 * c:128 * c + 128], range(8), qa_ready, plain(qaT, [*sc_ready.values()]))
    ghb = slot("ghb", 5, [128, 512])
    l_ghb = load("ghb", ghb[:, :], A["g_mlstm_head_2"].broadcast_to([128, 512]), nh_done, gates_mm, eng="pool")
    l_wr0 = load("wr0", wr[:, :, 0:4], A["w_router_group_2"][0].rearrange("(c p) n -> p c n", p=128), nh_done,
                 eng="pool")
    l_wr1 = load("wr1", wr[:, :, 4:36], A["w_router_expert_2"][0].rearrange("(c p) n -> p c n", p=128), nh_done,
                 eng="pool")
    for t in range(2):
        hm_last.append(dve(lambda e, t=t: e.tensor_tensor(mix[:, t, 0:512], mix[:, t, 0:512], ghb[:, :], ALU.mult),
                           l_ghb, hm_last))
    S = [slot(f"S{k}", 4, [128, 4, 384]) if k == 0 else slot(f"S{k}", 6, [128, 4, 384]) for k in range(2)]
    PTt = slot("PTt", 9, [128, 4, 384])
    pt_free = [[*hm_last, msc_done]]
    att_last = []
    for half in range(2):
        Sx = S[half]
        b0, b1, b2 = take(3)
        where = {}
        for hq in range(4):
            h = 2 * hq + half
            c, p0 = h // 2, 64 * (h % 2)
            q0 = qaT[p0:p0 + 64, c, :]
            k0 = qaT[p0:p0 + 64, 4 + c, :]
            where[hq] = (bank[b0][:, 128 * hq:128 * hq + 128],
                         bank[[b1, b2][hq // 2]][:, 256 * (hq % 2):256 * (hq % 2) + 256])
            pe(lambda e, q0=q0, k0=k0, o=where[hq][0]: e.matmul(o, q0[:, 0:128], k0[:, 0:128], start=True,
                                                               stop=True), qaT_ready, freed[b0])
            m = pe(lambda e, q0=q0, k0=k0, o=where[hq][1]: e.matmul(o, q0[:, 128:256], k0, start=True, stop=True),
                   freed[[b1, b2][hq // 2]])
        w = []
        pen = C("pen_ts").unsqueeze(1)
        w.append(dve(lambda e, b0=b0, Sx=Sx: e.tensor_tensor(
            Sx[:, :, 0:128], bank[b0][:, :].rearrange("p (h s) -> p h s", h=4),
            pen.broadcast_to([128, 4, 128]), ALU.add), m, qaT_ready, nh_done))
        for k, bb in enumerate((b1, b2)):
            src = bank[bb][:, :].rearrange("p (h s) -> p h s", h=2)
            w.append(act(lambda e, src=src, k=k, Sx=Sx: e.activation(Sx[:, 2 * k:2 * k + 2, 128:256],
                                                                    src[:, :, 0:128], ACT.Copy), m,
                         qaT_ready, nh_done))
            w.append(dve(lambda e, src=src, k=k, Sx=Sx: e.tensor_tensor(
                Sx[:, 2 * k:2 * k + 2, 256:384], src[:, :, 128:256], pen.broadcast_to([128, 2, 128]), ALU.add),
                m, w[-1], qaT_ready, nh_done))
        freed[b0], freed[b1], freed[b2] = [w[0]], [w[1], w[2]], [w[3], w[4]]
        k = 72 + 28 * half
        mx = [dve(lambda e, k=k, Sx=Sx: e.tensor_reduce(stat(k, 4), Sx[:, :, 0:128], AX, ALU.max, negate=False), w),
              dve(lambda e, k=k, Sx=Sx: e.tensor_reduce(stat(k + 4, 4), Sx[:, :, 128:384], AX, ALU.max,
                                                        negate=False), w)]
        mx = dve(lambda e, k=k: e.tensor_scalar(stat(k, 8), stat(k, 8), -ASC, None, ALU.mult), mx)
        ex = []
        for hq in range(4):
            for t, o in ((0, slice(0, 128)), (1, slice(128, 384))):
                ex.append(act(lambda e, hq=hq, t=t, o=o, k=k, Sx=Sx: e.activation(
                    Sx[:, hq, o], Sx[:, hq, o], ACT.Exp, bias=stat(k + 4 * t + hq), scale=ASC,
                    accum_out=stat(k + 8 + 4 * t + hq)), mx))
        rc = dve(lambda e, k=k: e.reciprocal(stat(k + 16, 8), stat(k + 8, 8)), ex)
        pts = []
        for hq in range(4):
            b = take()
            for j in range(3):
                m = pe(lambda e, hq=hq, j=j, b=b, Sx=Sx: e.transpose(
                    bank[b][:, 128 * j:128 * j + 128], Sx[:, hq, 128 * j:128 * j + 128], C("ident")),
                    ex, freed[b])
            s = (act if hq % 2 else dve)(
                (lambda e, hq=hq, b=b: e.activation(PTt[:, hq, :], bank[b][:, 0:384], ACT.Copy)) if hq % 2 else
                (lambda e, hq=hq, b=b: e.tensor_copy(PTt[:, hq, :], bank[b][:, 0:384])), m, pt_free[0])
            freed[b] = [s]
            pts.append(s)
        b = take()
        for hq in range(4):
            h = 2 * hq + half
            vv = [vat[:, s_, 64 * h:64 * h + 64] for s_ in range(2)]
            o0 = bank[b][:, 64 * hq:64 * hq + 64]
            o1 = bank[b][:, 256 + 64 * hq:256 + 64 * hq + 64]
            pe(lambda e, hq=hq, o0=o0, vv=vv: e.matmul(o0, PTt[:, hq, 0:128], vv[0], start=True, stop=True),
               pts, va_ready, freed[b])
            pe(lambda e, hq=hq, o1=o1, vv=vv: e.matmul(o1, PTt[:, hq, 128:256], vv[0], start=True, stop=False))
            m = pe(lambda e, hq=hq, o1=o1, vv=vv: e.matmul(o1, PTt[:, hq, 256:384], vv[1], start=False, stop=True))
        pt_free[0] = [m]
        fr = []
        for t in range(2):
            o = mix[:, t, 512:1024].rearrange("p (h w d) -> p w h d", h=4, w=2)[:, half, :, :]
            s = dve(lambda e, t=t, o=o, b=b, k=k: e.tensor_tensor(
                o,
                bank[b][:, 256 * t:256 * t + 256].rearrange("p (h d) -> p h d", h=4),
                stat(k + 16 + 4 * t, 4).unsqueeze(2).broadcast_to([128, 4, 64]), ALU.mult), m, rc, rows_done)
            fr.append(s)
        freed[b] = fr
        att_last += fr
    dump("mix", mix[:, :, :], [*att_last, *hm_last])
    mxh = slot("mxh", 1, [128, 8, 256], F32R)
    mxl = slot("mxl", 2, [128, 8, 256], F32R)
    mix_ready = turned(lambda t, c: mix[:, t, 128 * c:128 * c + 128], range(8), [*att_last, *hm_last],
                       hi_lo(mxh, mxl, [*hm_last, m]))
    gx = slot("gx", 3, [128, 2, 512])
    x_ready = []
    gx_free = [list(mix_ready)]
    for g in range(2):
        b, m = dense(mxh, mxl, mix_ready)
        for t in range(2):
            o = slice(512 * g, 512 * g + 512)
            s = dve(lambda e, t=t, o=o, b=b: e.tensor_tensor(gx[:, t, :], bank[b[t]][:, :], gate1b[:, o], ALU.mult),
                    m, ada_done[4], ada_done[5], x_ready[-2:])
            freed[b[t]] = [s]
            x_ready.append(dve(lambda e, t=t, o=o: e.tensor_tensor(x[:, t, o], x[:, t, o], gx[:, t, :], ALU.add),
                               s))
    mixes_done = m
    dump("x3", x[:, :, :], x_ready)
    gfb = slot("gfb", 7, [128, 1024])
    l_gfb = load("gfb", gfb[:, :], A["g_final_2"].broadcast_to([128, 1024]), x_ready, eng="pool")
    g2b = slot("g2b", 9, [128, 1024])
    brb = slot("brb", 9, [128, 36], F32, 4096)
    l_g2b = load("g2b", g2b[:, :], A["g_norm2_2"].broadcast_to([128, 1024]), mix_ready, eng="pool")
    l_br0 = load("br0", brb[:, 0:4], A["b_router_group_2"].broadcast_to([128, 4]), mix_ready, eng="pool")
    l_br1 = load("br1", brb[:, 4:36], A["b_router_expert_2"].broadcast_to([128, 32]), mix_ready, eng="pool")
    s_a2 = dve(lambda e: e.scalar_tensor_tensor(out=scale2b[:, :], in0=scale2b[:, :], scalar=1.0, in1=g2b[:, :],
                                                op0=ALU.add, op1=ALU.mult), l_g2b, ada_done[8], ada_done[9])
    h2 = slot("h2", 10, [128, 2, 1024])
    junk4 = slot("junk4", 4, [128, 2, 1024])
    r = rms(x, D, 0, junk4, [*x_ready, *mix_ready])
    h2r = []
    for t in range(2):
        s = dve(lambda e, t=t: e.scalar_tensor_tensor(out=h2[:, t, :], in0=x[:, t, :], scalar=stat(t),
                                                      in1=scale2b[:, :], op0=ALU.mult, op1=ALU.mult), r, s_a2,
                mix_ready)
        h2r.append(dve(lambda e, t=t: e.tensor_tensor(h2[:, t, :], h2[:, t, :], shift2b[:, :], ALU.add), s,
                       ada_done[6], ada_done[7]))
    dump("h2", h2[:, :, :], h2r)
    h2T = slot("h2T", 3, [128, 8, 256])
    h2T_ready = turned(lambda t, c: h2[:, t, 128 * c:128 * c + 128], range(8), h2r, plain(h2T, x_ready))
    th = slot("th", 2, [128, 2, 1024], F32R)
    tl = slot("tl", 9, [128, 2, 1024], F32R)
    b = take()
    for t in range(2):
        for c in range(8):
            m = pe(lambda e, t=t, c=c, b=b: e.matmul(
                bank[b][:, 36 * t:36 * t + 36], h2T[:, c, 128 * t:128 * t + 128], wr[:, c, :], start=(c == 0),
                stop=(c == 7)), h2T_ready, l_wr0, l_wr1, freed[b])
    router_mm = m
    th_r = [act(lambda e, t=t: e.activation(th[:, t, :], h2[:, t, :], ACT.Copy), h2r, mixes_done)
            for t in range(2)]

    lg = small("lg", [128, 2, 36])
    WT, MK, RK, T0, T1, T2 = (tab[:, k, :, :] for k in range(6))
    rs = small("rs", [128, 2, 16])

    def B(ap, n):
        return ap.broadcast_to([128, 2, n])

    s = dve(lambda e, b=b: e.tensor_tensor(
        lg[:, :, :], bank[b][:, 0:72].rearrange("p (t n) -> p t n", t=2),
        brb[:, 0:36].unsqueeze(1).broadcast_to([128, 2, 36]), ALU.add), m, l_br0, l_br1)
    freed[b] = [s]
    tl_r = [dve(lambda e, t=t: e.tensor_tensor(tl[:, t, :], h2[:, t, :], th[:, t, :].bitcast(F32), ALU.subtract),
                th_r, s_a2, s) for t in range(2)]
    dump("lg", lg[:, :, :], s)

    def chain(fn, *after):
        cur[0] = dve(fn, cur[0], *after)
        return cur[0]

    cur = [s]

    def first_max(src, n, top, hot, tmp):
        chain(lambda e: e.tensor_reduce(top, src, AX, ALU.max))
        chain(lambda e: e.tensor_tensor(tmp, src, B(top, n), ALU.is_lt))
        io = C("iota32", 0, n).unsqueeze(1).broadcast_to([128, 2, n])
        chain(lambda e: e.scalar_tensor_tensor(out=tmp, in0=tmp, scalar=FAR, in1=io, op0=ALU.mult, op1=ALU.add))
        chain(lambda e: e.tensor_reduce(rs[:, :, 15:16], tmp, AX, ALU.min))
        return chain(lambda e: e.tensor_tensor(hot, io, B(rs[:, :, 15:16], n), ALU.is_equal))

    G = lg[:, :, 0:4]
    E_ = lg[:, :, 4:36]
    first_max(G, 4, rs[:, :, 0:1], rs[:, :, 4:8], rs[:, :, 8:12])
    chain(lambda e: e.tensor_tensor(rs[:, :, 8:12], G, B(rs[:, :, 0:1], 4), ALU.subtract))
    ex = act(lambda e: e.activation(rs[:, :, 8:12], rs[:, :, 8:12], ACT.Exp), cur[0])
    cur[0] = ex
    chain(lambda e: e.tensor_reduce(rs[:, :, 1:2], rs[:, :, 8:12], AX, ALU.add))
    chain(lambda e: e.reciprocal(rs[:, :, 1:2], rs[:, :, 1:2]))
    hot8 = rs[:, :, 4:8].unsqueeze(3).broadcast_to([128, 2, 4, 8])
    chain(lambda e: e.tensor_copy(T0.rearrange("p t (g n) -> p t g n", g=4), hot8))
    chain(lambda e: e.tensor_tensor(T1, T0, E_, ALU.mult))
    chain(lambda e: e.tensor_scalar(T0, T0, BIG, -BIG, ALU.mult, ALU.add))
    chain(lambda e: e.tensor_tensor(T1, T1, T0, ALU.add))
    first_max(T1, 32, rs[:, :, 2:3], WT, T0)
    chain(lambda e: e.scalar_tensor_tensor(out=T1, in0=WT, scalar=-2 * BIG, in1=T1, op0=ALU.mult, op1=ALU.add))
    first_max(T1, 32, rs[:, :, 3:4], T2, T0)
    chain(lambda e: e.tensor_tensor(MK, WT, T2, ALU.add))
    chain(lambda e: e.tensor_tensor(rs[:, :, 8:9], rs[:, :, 3:4], rs[:, :, 2:3], ALU.subtract))
    cur[0] = act(lambda e: e.activation(rs[:, :, 8:9], rs[:, :, 8:9], ACT.Exp), cur[0])
    chain(lambda e: e.tensor_scalar(rs[:, :, 9:10], rs[:, :, 8:9], 1.0, None, ALU.add))
    chain(lambda e: e.reciprocal(rs[:, :, 9:10], rs[:, :, 9:10]))
    chain(lambda e: e.tensor_tensor(rs[:, :, 9:10], rs[:, :, 9:10], rs[:, :, 1:2], ALU.mult))
    chain(lambda e: e.tensor_tensor(rs[:, :, 8:9], rs[:, :, 8:9], rs[:, :, 9:10], ALU.mult))
    chain(lambda e: e.tensor_tensor(WT, WT, B(rs[:, :, 9:10], 32), ALU.mult))
    chain(lambda e: e.tensor_tensor(T2, T2, B(rs[:, :, 8:9], 32), ALU.mult))
    wt_ready = chain(lambda e: e.tensor_tensor(WT, WT, T2, ALU.add))
    b = take()
    pe(lambda e, b=b: e.matmul(bank[b][:, 0:32], C("lt"), MK[:, 0, :], start=True, stop=True), cur[0], freed[b])
    pe(lambda e, b=b: e.matmul(bank[b][:, 32:64], C("lt"), MK[:, 1, :], start=True, stop=False))
    pe(lambda e, b=b: e.matmul(bank[b][:, 32:64], C("ones"), MK[:, 0, :], start=False, stop=True))
    pe(lambda e, b=b: e.matmul(bank[b][:, 64:96], C("ones"), MK[:, 0, :], start=True, stop=False))
    m = pe(lambda e, b=b: e.matmul(bank[b][:, 64:96], C("ones"), MK[:, 1, :], start=False, stop=True))
    chain(lambda e: e.tensor_scalar(T0, MK, -FAR, FAR, ALU.mult, ALU.add), m)
    rk_ready = chain(lambda e, b=b: e.tensor_tensor(
        RK, T0, bank[b][:, 0:64].rearrange("p (t n) -> p t n", t=2), ALU.add))
    cnt = small("cnt", [128, 8, 32])
    chain(lambda e, b=b: e.tensor_copy(cnt[:, 0, :], bank[b][:, 64:96]))
    freed[b] = [cur[0]]
    THR = [float(SLOTS * k) for k in (1, 2, 3)]
    for k in range(3):
        chain(lambda e, k=k: e.tensor_scalar(cnt[:, 1 + k, :], cnt[:, 0, :], THR[k], None, ALU.is_gt))
    chain(lambda e: e.tensor_tensor(cnt[:, 1, :], cnt[:, 1, :], cnt[:, 2, :], ALU.add))
    chain(lambda e: e.tensor_tensor(cnt[:, 1, :], cnt[:, 1, :], cnt[:, 3, :], ALU.add))
    chain(lambda e: e.memset(cnt[:, 2, :], 0.0))
    chain(lambda e: e.tensor_tensor_scan(cnt[:, 3, :], cnt[:, 1, :], cnt[:, 2, :], 0.0, ALU.add, ALU.add))
    chain(lambda e: e.tensor_tensor(cnt[:, 4, :], cnt[:, 3, :], cnt[:, 1, :], ALU.subtract))
    ov_ready = chain(lambda e: e.tensor_copy(ovf[:, 0:1], cnt[:, 3, 31:32]))
    for j in range(NOV):
        chain(lambda e, j=j: e.tensor_scalar(cnt[:, 5, :], cnt[:, 3, :], float(j), None, ALU.is_le))
        chain(lambda e, j=j: e.tensor_reduce(cnt[:, 6, j:j + 1], cnt[:, 5, :], AX, ALU.add))
    chain(lambda e: e.tensor_scalar(cnt[:, 7, 0:NOV], cnt[:, 6, 0:NOV], float(NE - 1), None, ALU.min))
    ids_step = chain(lambda e: e.tensor_copy(ovf[:, 8:8 + NOV], cnt[:, 7, 0:NOV]))
    ids_ready.append(ids_step)
    dump("tab", tab[:, :, :, :], cur[0])

    x_rk = [*th_r, *tl_r, rk_ready, wt_ready]
    XT = [[slot(f"XT{k}{q}", (3, 4, 8, 11)[2 * k + q], [128, 2, 8, 2, SLOTS], F32R) for q in range(2)]
          for k in range(2)]
    GU = [slot(f"GU{k}", 6, [128, 2, 512], F32, 4096 * k) for k in range(2)]
    YH = [slot(f"YH{k}", 5, [128, 512], F32R, 4096 * k) for k in range(2)]
    YL = [slot(f"YL{k}", 5, [128, 512], F32R, 4096 * k + 2048) for k in range(2)]
    HF = [slot(f"HF{k}", 1, [128, 256], F32, 1024 * k) for k in range(2)]
    HS = [slot(f"HS{k}", 1, [128, 4, 2, SLOTS], F32R, 2048 + 2048 * k) for k in range(2)]
    PP = [slot(f"PP{k}", 10, [128, 2, 4, 2, SLOTS], F32R, 4096 * k) for k in range(2)]
    PT = [slot(f"PT{k}", 12, [128, 256], F32R, 1024 * k) for k in range(4)]
    wsl = small("wsl", [128, 4])
    pool_of_banks[0] = [0, 1, 2, 3]
    acc = [4, 5, 6, 7]
    h2_done = [*tl_r, *th_r, *h2T_ready]
    fr = {("PP", k): list(h2_done) for k in range(2)}
    fr.update({("PT", k): list(h2_done) for k in range(4)})
    fr.update({("XT", k): [router_mm, *h2T_ready] for k in range(2)})
    fr.update({("GU", k): [*mix_ready] for k in range(2)})
    fr.update({("Y", k): [*hm_last] for k in range(2)})
    fr.update({("H", k): [mixes_done] for k in range(2)})
    fr.update({("wsl", k): [] for k in range(4)})
    io4 = C("iota64").unsqueeze(1).unsqueeze(1).broadcast_to([128, 4, 2, SLOTS])

    def blocks(n, rk, wt, after, first, last_of_all, base):
        ready = {}

        def one_hots(p):
            k = p % 2
            s = []
            for t in range(2):
                src = rk(t, 4 * p, 4).unsqueeze(2).unsqueeze(3).broadcast_to([128, 4, 2, SLOTS])
                s.append(dve(lambda e, t=t, k=k, src=src: e.tensor_tensor(PP[k][:, t, :, :, :], io4, src,
                                                                          ALU.is_equal), after, fr["PP", k]))
            ready["P", p] = s

        def gather(p, c):
            k = p % 2
            b = take()
            dst = bank[b][:, :].rearrange("p (x h s) -> p x h s", x=4, h=2)
            for hl_, src in ((0, th), (1, tl)):
                for t in range(2):
                    m = pe(lambda e: e.matmul(
                        dst[:, :, hl_, :], src[:, t, 128 * c:128 * c + 128], PP[k][:, t, :, 0, :],
                        start=(t == 0), stop=(t == 1)), ready["P", p], x_rk, freed[b])
            fs = []
            for q in range(2):
                v = dst[:, 2 * q:2 * q + 2, :, :]
                o = XT[k][q][:, :, c, :, :]
                if c % 2:
                    fs.append(act(lambda e: e.activation(o, v, ACT.Copy), m, fr["XT", k]))
                else:
                    fs.append(dve(lambda e: e.tensor_copy(o, v), m, fr["XT", k]))
            freed[b] = fs
            ready.setdefault(("X", p), []).append(fs)

        def turn_p(j):
            k = j // 4 % 2
            b = take()
            Pm = [PP[k][:, t, j % 4, :, :].rearrange("p d s -> p (d s)").bitcast(F32) for t in range(2)]
            for t in range(2):
                pe(lambda e: e.transpose(bank[b][:, 128 * t:128 * t + 128], Pm[t], C("ident")),
                   ready["P", j // 4], freed[b])
            for t in range(2):
                m = pe(lambda e, w=wt(t, j): e.matmul(bank[b][:, 256:257], Pm[t], w, start=(t == 0), stop=(t == 1)),
                       after, x_rk)
            q = j % 4
            s1 = act(lambda e: e.activation(PT[q][:, :], bank[b][:, 0:256], ACT.Copy), m, fr["PT", q])
            s2 = act(lambda e: e.activation(wsl[:, q:q + 1], bank[b][:, 256:257], ACT.Copy), m, fr["wsl", q])
            freed[b] = [s1, s2]
            ready["T", j] = [s1]
            ready["w", j] = [s2]
            if j % 4 == 3:
                fr["PP", k] = [m]

        def gate_up(j, w, hf):
            k = j % 2
            if hf == 0:
                ready["b", w] = take()
            b = ready["b", w]
            half = next_half()
            for c in range(4):
                q = 4 * hf + c
                a = XT[j // 4 % 2][j % 4 // 2][:, j % 2, q, :, :].rearrange("p h s -> p (h s)")
                m = times(bank[b][:, :], a, half, slice(512 * c, 512 * c + 512), q == 0, q == 7,
                          ready["X", j // 4], freed[b])
            if hf == 1:
                e_ = act(lambda e: e.activation(GU[k][:, w, :], bank[b][:, :], ACT.Copy), m, fr["GU", k])
                freed[b] = [e_]
                ready["GU", j, w] = e_
            half_done(half[0], half[1], m)
            if w == 1 and hf == 1 and j % 4 == 3:
                fr["XT", j // 4 % 2] = [m]

        def hidden(j):
            k = j % 2
            b = take()
            for w in range(2):
                for f in range(4):
                    m = pe(lambda e: e.matmul(
                        bank[b][:, 256 * w + 64 * f:256 * w + 64 * f + 64], GU[k][:, w, 128 * f:128 * f + 128],
                        C("ident2"), start=True, stop=True), ready["GU", j, w], freed[b])
            fr["GU", k] = [m]
            s1 = act(lambda e: e.activation(HF[k][:, :], bank[b][:, 0:256], ACT.Silu), m, fr["H", k])
            s2 = dve(lambda e: e.tensor_tensor(HF[k][:, :], HF[k][:, :], bank[b][:, 256:512], ALU.mult), s1)
            freed[b] = [s2]
            v = HF[k][:, :].rearrange("p (f s) -> p f s", f=4)
            s3 = act(lambda e: e.activation(HS[k][:, :, 0, :], v, ACT.Copy), s2, fr["H", k])
            s4 = dve(lambda e: e.tensor_tensor(HS[k][:, :, 1, :], v, HS[k][:, :, 0, :].bitcast(F32),
                                               ALU.subtract), s3)
            ready["H", j] = [s3, s4]

        def down(j, hf):
            k = j % 2
            if hf == 0:
                ready["b", 2] = take(2)
            b = ready["b", 2]
            half = next_half()
            for c in range(2):
                f = 2 * hf + c
                a = HS[k][:, f, :, :].rearrange("p h s -> p (h s)")
                for n in range(2):
                    o = slice(1024 * c + 512 * n, 1024 * c + 512 * n + 512)
                    m = times(bank[b[n]][:, :], a, half, o, f == 0, f == 3, ready["H", j], freed[b[n]])
            if hf == 1:
                fr["H", k] = [m]
                q = j % 4
                for n in range(2):
                    s1 = act(lambda e: e.activation(YH[n][:, :], bank[b[n]][:, :], ACT.Copy, scale=wsl[:, q:q + 1]),
                             m, fr["Y", n], ready["w", j])
                    s2 = dve(lambda e: e.scalar_tensor_tensor(
                        out=YL[n][:, :], in0=bank[b[n]][:, :], scalar=wsl[:, q:q + 1],
                        in1=YH[n][:, :].bitcast(F32), op0=ALU.mult, op1=ALU.subtract), s1, fr["Y", n])
                    freed[b[n]] = [s2]
                    ready["Y", j, n] = [s1, s2]
                fr["wsl", q] = [s2]
            half_done(half[0], half[1], m)

        def combine(j):
            q = j % 4
            for n in range(2):
                for t in range(2):
                    o = bank[acc[2 * t + n]][:, :]
                    a = PT[q][:, 128 * t:128 * t + 128]
                    i0 = first and j == 0
                    i1 = j == n_blocks - 1
                    m0 = [] if not i0 else freed[acc[2 * t + n]]
                    pe(lambda e: e.matmul(o, a, YH[n][:, :], start=i0, stop=False, skip_group_check=True),
                       ready["Y", j, n], ready["T", j], m0)
                    m = pe(lambda e: e.matmul(o, a, YL[n][:, :], start=False, stop=i1, skip_group_check=True))
                fr["Y", n] = [m]
            fr["PT", q] = [m]

        n_blocks = n
        one_hots(0)
        for c in range(8):
            gather(0, c)
        for j in range(n + 2):
            p, q = j // 4 + 1, j % 4
            if j < n:
                gate_up(j, 0, 0)
            if 0 < j <= n:
                hidden(j - 1)
            if j < n:
                gate_up(j, 0, 1)
            if j > 1:
                combine(j - 2)
            if q == 0 and 4 * p < n:
                one_hots(p)
            if j < n:
                gate_up(j, 1, 0)
                if 4 * p < n:
                    gather(p, 2 * q)
                gate_up(j, 1, 1)
                turn_p(j)
            if 0 < j <= n:
                down(j - 1, 0)
            if j < n and 4 * p < n:
                gather(p, 2 * q + 1)
            if 0 < j <= n:
                down(j - 1, 1)

    blocks(NE, lambda t, j, n: RK[:, t, j:j + n], lambda t, j: WT[:, t, j:j + 1], [rk_ready, wt_ready], True,
           False, 0)

    count = {}
    for e_ in Q.ENGINES:
        put(e_, lambda e: count.update(n=e.value_load(ovf[0:1, 0:1], min_val=0, max_val=NOV - 1)), ov_ready)
    def overflow():
        in_branch[0] = True
        ok = small("ok", [128, 2, NOV])
        ow = small("ow", [128, 2, NOV])
        kb = cnt[:, 4, :].unsqueeze(1).broadcast_to([128, 2, 32])
        cur[0] = dve(lambda e: e.scalar_tensor_tensor(out=T0, in0=kb, scalar=float(SLOTS), in1=RK, op0=ALU.mult,
                                                      op1=ALU.add), ids_step)
        for j in range(NOV):
            chain(lambda e, j=j: e.tensor_scalar(cnt[:, 5, :], cnt[:, 4, :], float(j), None, ALU.is_le))
            chain(lambda e, j=j: e.tensor_scalar(cnt[:, 6, :], cnt[:, 3, :], float(j), None, ALU.is_gt))
            chain(lambda e: e.tensor_tensor(cnt[:, 5, :], cnt[:, 5, :], cnt[:, 6, :], ALU.mult))
            hot = cnt[:, 5, :].unsqueeze(1).broadcast_to([128, 2, 32])
            chain(lambda e, hot=hot: e.tensor_tensor(T1, T0, hot, ALU.mult))
            chain(lambda e, j=j: e.tensor_reduce(ok[:, :, j:j + 1], T1, AX, ALU.add))
            chain(lambda e, j=j: e.tensor_scalar(ok[:, :, j:j + 1], ok[:, :, j:j + 1], float(-SLOTS * (j + 1)), None,
                                                 ALU.add))
            chain(lambda e: e.tensor_reduce(cnt[:, 7, 16:17], cnt[:, 5, :], AX, ALU.add))
            chain(lambda e: e.tensor_scalar(cnt[:, 7, 17:18], cnt[:, 7, 16:17], -FAR, FAR, ALU.mult, ALU.add))
            chain(lambda e, j=j: e.tensor_scalar(ok[:, :, j:j + 1], ok[:, :, j:j + 1], cnt[:, 7, 17:18], None,
                                                 ALU.add))
            chain(lambda e, hot=hot: e.tensor_tensor(T1, WT, hot, ALU.mult))
            chain(lambda e, j=j: e.tensor_reduce(ow[:, :, j:j + 1], T1, AX, ALU.add))
        ov_tab = cur[0]
        for _ in range(RAW):
            feed()
        for _ in range(RING):
            split_ahead()
        blocks(NOV, lambda t, j, n: ok[:, t, j:j + n], lambda t, j: ow[:, t, j:j + 1], [ov_tab], False, True, 0)

    known = dict(Q.seen)
    if Q.who:
        with Q.eng.If(count["n"] > 0):
            overflow()
    else:
        overflow()
    Q.seen = known

    Q.era = 1
    all_done = pe(lambda e: e.drain())
    ysc = slot("ysc", 3, [128, 2, 1024])
    xr = []
    for t in range(2):
        for n in range(2):
            o = slice(512 * n, 512 * n + 512)
            s = dve(lambda e, t=t, n=n, o=o: e.tensor_tensor(ysc[:, t, o], bank[acc[2 * t + n]][:, :],
                                                             gate2b[:, o], ALU.mult), all_done, ada_done[10],
                    ada_done[11])
            xr.append(dve(lambda e, t=t, o=o: e.tensor_tensor(x[:, t, o], x[:, t, o], ysc[:, t, o], ALU.add), s))
    fin = slot("fin", 4, [128, 2, 1024])
    s_out = sem("s_out")
    for t in range(2):
        k = 8 * t
        sq = act(lambda e, t=t, k=k: e.activation(fin[:, t, :], x[:, t, :], ACT.Square, accum_out=stat(k)), xr)
        a = dve(lambda e, k=k: e.tensor_scalar(stat(k + 1), stat(k), 1.0 / D, EPS, ALU.mult, ALU.add), sq)
        a = act(lambda e, k=k: e.activation(stat(k + 2), stat(k + 1), ACT.Sqrt), a)
        a = dve(lambda e, k=k: e.reciprocal(stat(k + 3), stat(k + 2)), a)
        a = dve(lambda e, t=t, k=k: e.scalar_tensor_tensor(out=fin[:, t, :], in0=x[:, t, :], scalar=stat(k + 3),
                                                           in1=gfb[:, :], op0=ALU.mult, op1=ALU.mult), a, l_gfb)
        put("sp", lambda e, t=t: e.dma_start(out[0, 128 * t:128 * t + 128, :], fin[:, t, :]).then_inc(s_out, 16),
            a)
    put("sp", lambda e: e.wait_ge(s_out, 32))


def build_two_blocks(nc, A, out):
    kept, named = {}, set()
    program(nc, A, out, kept, Queues(None, None, named, {}))
    with nc.Block() as block:
        block.sync(lambda eng: program(nc, A, out, kept, Queues("sp", eng, named, {})))
        block.scalar(lambda eng: program(nc, A, out, kept, Queues("act", eng, named, {})))
        block.gpsimd(lambda eng: program(nc, A, out, kept, Queues("pool", eng, named, {})))
        block.vector(lambda eng: program(nc, A, out, kept, Queues("dve", eng, named, {})))
        block.tensor(lambda eng: program(nc, A, out, kept, Queues("pe", eng, named, {})))


def constants():
    c = np.zeros((128, NCST), np.float32)
    i = np.arange(128)
    c[:, CST["ident"]:CST["ident"] + 128] = np.eye(128)
    c[:, CST["ident2"]:CST["ident2"] + 64] = (i[:, None] % 64 == np.arange(64)[None])
    c[:, CST["lt"]:CST["lt"] + 128] = i[:, None] < i[None]
    c[:, CST["pen_ts"]:CST["pen_ts"] + 128] = np.where(i[None] > i[:, None], -BIG, 0.0)
    c[:, CST["pen_st"]:CST["pen_st"] + 128] = np.where(i[:, None] > i[None], BIG, 0.0)
    c[:, CST["iota64"]:CST["iota64"] + 64] = np.arange(64)[None]
    c[:, CST["iota32"]:CST["iota32"] + 32] = np.arange(32)[None]
    c[:, CST["ones"]:CST["ones"] + 128] = 1.0
    return c


_PACKED = ("norm_mix_g", "norm_ff_g", "g_norm1_2", "b_s", "conv_w", "w_conv_2", "b_conv_2", "c_2", "b_gates_2", "w_s")
_NAMES = ("x", "w_in", "b_gate", "norm_v_g", "w_proj_a", "w_proj_b", "w_out", "w_ff1", "w_ff2", "norm_final_g",
          "w_ada_2", "b_ada_2", "w_in_2", "g_mlstm_head_2", "w_out_2", "g_norm2_2", "w_router_group_2",
          "b_router_group_2", "w_router_expert_2", "b_router_expert_2", "w_expert_gate_2", "w_expert_up_2",
          "w_expert_down_2", "g_final_2")


def lay_out(inputs):
    def by_part(a):
        return np.ascontiguousarray(np.asarray(a).reshape(-1, 8, 128).transpose(2, 0, 1).reshape(128, -1))

    i = {k: np.asarray(v) for k, v in inputs.items()}
    bg = np.zeros((128, 2), np.float32)
    bg[0:4, 0] = i["b_gates_2"][0, 0:4]
    bg[32:36, 1] = i["b_gates_2"][0, 4:8]
    vecs = np.concatenate([by_part(i["norm_mix_g"]), by_part(i["norm_ff_g"]), by_part(i["g_norm1_2"]),
                           i["b_s"][0].T, by_part(i["conv_w"]), by_part(i["w_conv_2"]), by_part(i["b_conv_2"]),
                           by_part(i["c_2"]), bg], axis=1)
    arrays = {k: np.ascontiguousarray(i[k]) for k in _NAMES}
    arrays["norm_final_g"] = arrays["norm_final_g"].reshape(1, -1)
    arrays["g_final_2"] = arrays["g_final_2"].reshape(1, -1)
    arrays["vecs"] = np.ascontiguousarray(vecs)
    arrays["w_sT"] = np.ascontiguousarray(i["w_s"][0].transpose(2, 0, 1))
    arrays["cst"] = constants()
    return arrays


def make(nc, arrays):
    A = {k: nc.dram_tensor(f"in_{k}", a.shape, F32, kind="ExternalInput").ap() for k, a in arrays.items()}
    out = nc.dram_tensor("out_0", (1, 256, 1024), F32, kind="ExternalOutput").ap()
    return A, out


def kernel(**inputs):
    import concourse.bacc as _bacc
    from concourse.bass_utils import run_bass_kernel_spmd as _run

    nc = _bacc.Bacc("TRN2", target_bir_lowering=False, num_devices=1)
    arrays = lay_out(inputs)
    A, out = make(nc, arrays)
    build_two_blocks(nc, A, out)
    r = _run(nc, [{f"in_{k}": a for k, a in arrays.items()}], core_ids=[0])
    return r.results[0]["out_0"]
```

```python
import numpy as np

import concourse.bass as bass
from concourse import mybir

DT = mybir.dt
F32 = DT.float32
F32R = DT.float32r
I32 = DT.int32
ACT = mybir.ActivationFunctionType
ALU = mybir.AluOpType
AX = mybir.AxisListType.X

EPS = 1e-6
D = 1024
BIG = 1.0e30
FAR = 4096.0
NE = 32
SLOTS = 64
NOV = 8
RAW = 6
RING = 3
POW = False

VEC = {}
_at = 0
for _n, _w in (("g_mix", 8), ("g_nf", 8), ("g_ff", 8), ("g1", 8), ("b_s", 8), ("conv", 24), ("conv2", 32), ("bconv2", 8),
               ("c", 8), ("bg", 2)):
    VEC[_n] = _at
    _at += _w
NVEC = _at
CST = {}
_at = 0
for _n, _w in (("ident", 128), ("ident2", 64), ("lt", 128), ("pen_ts", 128), ("pen_st", 128), ("iota64", 64),
               ("iota32", 32), ("ones", 128)):
    CST[_n] = _at
    _at += _w
NCST = _at


class Step:

    def __init__(self, n):
        self.n = n
        self.sem = self.value = None


class Load:

    def __init__(self, sem, value):
        self.sem, self.value = sem, value


class Queues:

    ENGINES = ("pe", "act", "dve", "pool", "sp")

    def __init__(self, who, eng, named, sems):
        self.who, self.eng, self.named, self.sems = who, eng, named, sems
        self.era = 0
        self.n = 0
        self.value = {}
        self.last = {}
        self.seen = {}

    def put(self, engine, fn, *after):
        flat, open_ = [], list(after)
        while open_:
            a = open_.pop(0)
            if isinstance(a, (list, tuple)):
                open_ += a
            elif a is not None:
                flat.append(a)
        s = Step(self.n)
        self.n += 1
        self.last[engine] = s
        if self.who is None:
            self.named.update(a.n for a in flat if isinstance(a, Step))
            return s
        if s.n in self.named:
            key = engine, self.era
            self.value[key] = self.value.get(key, 0) + 1
            s.sem, s.value = self.sems[key], self.value[key]
        if engine == self.who:
            for a in flat:
                if self.seen.get(a.sem.name, 0) < a.value:
                    self.eng.wait_ge(a.sem, a.value)
                    self.seen[a.sem.name] = a.value
            ins = fn(self.eng)
            if s.value is not None:
                ins.then_inc(s.sem, 1)
        return s


def program(nc, A, out, kept, Q):
    base = 16512
    offs = {"raw": base, "hi": base + RAW * 8192, "lo": base + (RAW + RING) * 8192,
            "slot": base + (RAW + 2 * RING) * 8192}
    rest = [offs["slot"] + 13 * 8192]

    def at(name, shape, dt, off):
        if name not in kept:
            kept[name] = nc.alloc_sbuf_tensor_at(name, shape, dt, offset=off)
        return kept[name]

    def slot(name, k, shape, dt=F32, off=0):
        n = int(np.prod(shape[1:])) * 4
        assert off + n <= 8192, name
        return at(name, shape, dt, offs["slot"] + 8192 * k + off)

    def small(name, shape, dt=F32):
        n = (int(np.prod(shape[1:])) * 4 + 31) // 32 * 32
        t = at(name, shape, dt, rest[0])
        rest[0] += n
        assert rest[0] <= 229360, name
        return t

    def sem(name):
        if name not in kept:
            kept[name] = nc.alloc_semaphore(name)
        return kept[name]

    put = Q.put
    for e in Q.ENGINES:
        for era in (0, 1):
            Q.sems[e, era] = sem(f"s_{e}{era}")

    def pe(fn, *a):
        return put("pe", fn, *a)

    def act(fn, *a):
        return put("act", fn, *a)

    def dve(fn, *a):
        return put("dve", fn, *a)

    def pool(fn, *a):
        return put("pool", fn, *a)

    def load(name, dst, src, *after, eng="act"):
        s = sem(f"l_{name}")
        put(eng, lambda e: e.dma_start(dst, src).then_inc(s, 16), *after)
        return Load(s, 16)

    cst = small("cst", [128, NCST])
    vec = small("vec", [128, NVEC])
    st = small("st", [128, 128])
    tab = small("tab", [128, 6, 2, 32])
    ovf = small("ovf", [128, 32], I32)

    def C(n, lo=0, hi=None, rows=slice(0, 128)):
        a = CST[n]
        w = {"ident": 128, "ident2": 64, "lt": 128, "pen_ts": 128, "pen_st": 128, "iota64": 64, "iota32": 32,
             "ones": 128}[n]
        return cst[rows, a + lo:a + (w if hi is None else hi)]

    def V(n, k, rows=slice(0, 128)):
        return vec[rows, VEC[n] + k:VEC[n] + k + 1]

    x = slot("x", 0, [128, 2, 1024])
    l_cst = load("cst", cst[:, :], A["cst"], eng="sp")
    l_x = [load(f"x{t}", x[:, t, :], A["x"][0, 128 * t:128 * t + 128, :], eng="sp") for t in range(2)]
    l_vec = load("vec", vec[:, :], A["vecs"], eng="sp")

    if "banks" not in kept:
        kept["banks"] = [nc.alloc_psum_tensor(f"bank{i}", [128, 512], F32) for i in range(8)]
    bank = kept["banks"]
    freed = [[] for _ in range(8)]
    turn = [0]
    opened = set()
    pool_of_banks = [list(range(8))]

    def take(n=1):
        got = []
        while len(got) < n:
            k = pool_of_banks[0][turn[0] % len(pool_of_banks[0])]
            turn[0] += 1
            if k not in opened:
                got.append(k)
        return got if n > 1 else got[0]

    raw = [at(f"raw{i}", [128, 2048], F32, offs["raw"] + 8192 * i) for i in range(RAW)]
    whi = [at(f"whi{i}", [128, 2048], F32R, offs["hi"] + 8192 * i) for i in range(RING)]
    wlo = [at(f"wlo{i}", [128, 2048], F32R, offs["lo"] + 8192 * i) for i in range(RING)]
    raw_sem = [sem(f"s_raw{i}") for i in range(RAW)]

    halves = []

    def cols(w, r0, c0):
        return ("mm", lambda: w[r0:r0 + 512, c0:c0 + 512].rearrange("(c p) n -> p c n", p=128), 4)

    def rows(w, r0):
        return ("mm", lambda: w[r0:r0 + 256, :].rearrange("(c p) n -> p c n", p=128), 2)

    def group(w, c0):
        return [cols(w, 0, c0), cols(w, 512, c0)]

    w_in, w_in2 = A["w_in"][0], A["w_in_2"][0]
    ada_at = []

    def ada():
        g, k = divmod(len(ada_at), 2)
        if g < 12:
            ada_at.append(len(halves))
            halves.append(("ada", cols(A["w_ada_2"][0], 512 * k, 512 * g)[1], (g, k)))

    for n, g in enumerate((2, 3, 0, 1, 6, 7, 8, 9, 4, 5, 10, 11, 12, 13)):
        pair = group(w_in, 512 * g)
        halves += pair[:1]
        if n > 1:
            ada()
        halves += pair[1:]
    for w in (A["w_proj_a"][0], A["w_proj_b"][0], A["w_out"][0]):
        for c0 in (0, 512):
            pair = group(w, c0)
            halves += pair[:1]
            if w is not A["w_out"][0]:
                ada()
            halves += pair[1:]
    for g in range(9):
        if g < 8:
            halves += group(A["w_ff1"][0], 512 * g)
            ada()
        if g > 0:
            halves += [rows(A["w_ff2"][0], 512 * (g - 1)), rows(A["w_ff2"][0], 512 * (g - 1) + 256)]
    QK, VM, OM, GT, QA, KA, VA = 0, 1024, 1536, 2048, 2056, 2568, 3080
    for c0 in (QK, QK + 512, QA, KA, VA, VM, OM):
        halves += group(w_in2, c0)
    halves += [cols(A["w_out_2"][0], r0, c0) for r0 in (512, 0) for c0 in (0, 512)]

    def expert(e, what):
        if what == "d":
            w = A["w_expert_down_2"][0, e]
            return [rows(w, 0), ("whole", *rows(w, 256)[1:])]
        return group(A["w_expert_gate_2" if what == "g" else "w_expert_up_2"][0, e], 0)

    for e in range(NE + 1):
        if e < NE:
            halves += expert(e, "g") + expert(e, "u")
        if e > 0:
            halves += expert(e - 1, "d")
    n_static = len(halves)

    def moving(name, j, r0, n_rows, chunks):
        w = A[name]

        def src(e):
            v = e.value_load(ovf[0:1, 8 + j:9 + j], min_val=0, max_val=NE - 1)
            return w[0, bass.ds(v, 1), r0:r0 + n_rows, :].rearrange("a (c p) n -> p (a c) n", p=128)
        return ("mm", src, chunks)

    for j in range(NOV + 1):
        if j < NOV:
            for n in ("w_expert_gate_2", "w_expert_up_2"):
                halves += [moving(n, j, 0, 512, 4), moving(n, j, 512, 512, 4)]
        if j > 0:
            halves += [moving("w_expert_down_2", j - 1, 0, 256, 2), moving("w_expert_down_2", j - 1, 256, 256, 2)]

    n_loaded = [0]
    read = {}
    loads = {}
    in_branch = [False]
    ids_ready = []

    def feed():
        while n_loaded[0] < (len(halves) if in_branch[0] else n_static):
            i = n_loaded[0]
            if i >= RAW and i - RAW not in read:
                return
            n_loaded[0] += 1
            kind, src, k = halves[i]
            r = i % RAW
            dst = raw[r][:, :].rearrange("p (c n) -> p c n", c=4 if kind == "ada" else k)
            if i >= n_static:
                put("sp", lambda e: e.dma_start(dst, src(e)).then_inc(raw_sem[r], 16), read[i - RAW], ids_ready)
            else:
                put("sp", lambda e: e.dma_start(dst, src()).then_inc(raw_sem[r], 16), read.get(i - RAW))
            loads[i] = Load(raw_sem[r], 16 * (i // RAW + 1))

    feed()

    n_split = [0]
    n_mm = [0]
    parts = {}
    parts_free = [[] for _ in range(RING)]
    used = [0]

    def split_ahead():
        while n_split[0] < n_loaded[0]:
            i = n_split[0]
            kind, _, info = halves[i]
            r = i % RAW
            n_split[0] += 1
            if kind == "ada":
                ada_half(i, *info)
                feed()
            elif kind == "mm":
                s = n_mm[0] % RING
                n_mm[0] += 1
                h = act(lambda e: e.activation(whi[s][:, :], raw[r][:, :], ACT.Copy), loads[i], parts_free[s])
                lo = dve(lambda e: e.tensor_tensor(wlo[s][:, :], raw[r][:, :], whi[s][:, :].bitcast(F32),
                                                   ALU.subtract), h, parts_free[s])
                parts[i] = (s, h, lo)
                read[i] = [lo]
                feed()
                return

    def next_half():
        flush()
        i = used[0]
        while halves[i][0] == "ada":
            i += 1
        used[0] = i + 1
        if halves[i][0] == "whole":
            return i, i % RAW, loads[i], None
        return i, *parts.pop(i)

    owed = [0]

    def flush():
        while owed[0]:
            owed[0] -= 1
            split_ahead()

    def half_done(i, s, step, later=False):
        if halves[i][0] == "whole":
            read[i] = [step]
            feed()
        else:
            parts_free[s] = [step]
            owed[0] += 1
            if not later:
                flush()

    def times(o, a, half, c, start, stop, *after):
        _, s, ready, lo = half
        if lo is None:
            return pe(lambda e: e.matmul(o, a.bitcast(F32), raw[s][:, c], start=start, stop=stop), ready, *after)
        pe(lambda e: e.matmul(o, a, whi[s][:, c], start=start, stop=False), ready, *after)
        return pe(lambda e: e.matmul(o, a, wlo[s][:, c], start=False, stop=stop), lo)

    sc = small("silu_c", [128, 8])
    ada_acc = [slot(f"ada_acc{k}", 10, [128, 512], F32, 2048 * k) for k in range(2)]
    ada_free = [[], []]
    ada_done = {}
    gate1b, scale2b = slot("gate1b", 11, [128, 1024]), slot("scale2b", 11, [128, 1024], F32, 4096)
    shift2b, gate2b = slot("shift2b", 12, [128, 1024]), slot("gate2b", 12, [128, 1024], F32, 4096)
    ada_cols = small("ada_cols", [128, 16])
    ada_tasks = []
    ada_cell = {}
    bada = [[sem(f"l_bada{k}"), 0] for k in range(2)]
    silu_c = act(lambda e: e.activation(sc[:, :], vec[:, VEC["c"]:VEC["c"] + 8], ACT.Silu), l_vec)

    def ada_half(i, g, k):
        acc = ada_acc[g % 2]
        r = i % RAW
        if k == 0:
            if any(t[0] % 2 == g % 2 for t in ada_tasks):
                ada_finish()
            z = pool(lambda e: e.memset(acc[:, :], 0.0), ada_free[g % 2])
            row = A["b_ada_2"][0:1, 512 * g:512 * g + 512]
            s = bada[g % 2]
            s[1] += 16
            put("pool", lambda e: e.dma_start(acc[0:1, :], row).then_inc(s[0], 16), z)
            ada_cell["b", g] = Load(s[0], s[1])
        last = ada_cell.get(("last", g))
        for c in range(4):
            last = dve(lambda e, c=c: e.scalar_tensor_tensor(
                out=acc[:, :], in0=raw[r][:, 512 * c:512 * c + 512], scalar=sc[:, 4 * k + c:4 * k + c + 1],
                in1=acc[:, :], op0=ALU.mult, op1=ALU.add), loads[i], silu_c, ada_cell["b", g], last)
        read[i] = [last]
        ada_cell["last", g] = last
        if k == 1:
            ada_tasks.append((g, last))

    ada_old = [0]

    def ada_finish(now=True):
        n = len(ada_tasks) if now else ada_old[0]
        ada_old[0] = len(ada_tasks) - n
        for _ in range(n):
            g, ready = ada_tasks.pop(0)
            acc = ada_acc[g % 2]
            b = take()
            if g < 4:
                for c in range(4):
                    m = pe(lambda e, c=c: e.matmul(bank[b][:, c:c + 1], acc[:, 128 * c:128 * c + 128],
                                                   C("ones", 0, 1), start=True, stop=True), ready, freed[b], l_cst)
                ev = act(lambda e: e.activation(ada_cols[:, 4 * g:4 * g + 4], bank[b][:, 0:4], ACT.Copy), m)
            else:
                t = [gate1b, shift2b, scale2b, gate2b][g // 2 - 2]
                m = pe(lambda e: e.matmul(bank[b][:, :], C("ones"), acc[:, :], start=True, stop=True),
                       ready, freed[b], l_cst)
                ev = act(lambda e: e.activation(t[:, 512 * (g % 2):512 * (g % 2) + 512], bank[b][:, :],
                                                ACT.Copy), m)
            freed[b] = [ev]
            ada_free[g % 2] = [m]
            ada_done[g] = ev

    def dense(xh, xl, x_ready, mid=None, hold=False):
        b = take(2)
        opened.update(b)
        for hf in range(2):
            half = next_half()
            last = dense_half(xh, xl, x_ready, b, half, hf, hf == 0, hf == 1)
            half_done(half[0], half[1], last, hf == 1)
            if hf == 0:
                if mid:
                    mid()
                ada_finish(False)
        if not hold:
            opened.difference_update(b)
        return b, last

    def dense_half(xh, xl, x_ready, b, half, hf, first, end):
        _, s, h, lo = half
        for c in range(4):
            k = 4 * hf + c
            for t in range(2):
                o = bank[b[t]][:, :]
                a_h, a_l = xh[:, k, 128 * t:128 * t + 128], xl[:, k, 128 * t:128 * t + 128]
                r_h, r_l = whi[s][:, 512 * c:512 * c + 512], wlo[s][:, 512 * c:512 * c + 512]
                pe(lambda e: e.matmul(o, a_h, r_h, start=first and c == 0, stop=False),
                   h, x_ready, freed[b[t]] if first and c == 0 else None)
                pe(lambda e: e.matmul(o, a_h, r_l, start=False, stop=False), lo)
                last = pe(lambda e: e.matmul(o, a_l, r_h, start=False, stop=end and c == 3))
        return last

    def stat(k, n=1):
        return st[:, k:k + n]

    def squares(src, k, junk, after):
        return act(lambda e: e.activation(junk, src, ACT.Square, accum_out=stat(k)), after)

    def inv_rms(k, n, ready, w=2):
        a = dve(lambda e: e.tensor_scalar(stat(k, w), stat(k, w), 1.0 / n, EPS, ALU.mult, ALU.add), ready)
        if POW:
            return dve(lambda e: e.tensor_scalar(stat(k, w), stat(k, w), -0.5, None, ALU.pow), a)
        b = act(lambda e: e.activation(stat(k, w), stat(k, w), ACT.Sqrt), a)
        return dve(lambda e: e.reciprocal(stat(k, w), stat(k, w)), b)

    def turned(src, pairs, ready, use):
        outs = []
        for k in pairs:
            b = take()
            for c in range(2):
                for t in range(2):
                    piece = src(t, 2 * k + c)
                    m = pe(lambda e: e.transpose(
                        bank[b][:, 256 * c + 128 * t:256 * c + 128 * t + 128], piece, C("ident")), ready, freed[b], l_cst)
            r = use(k, bank[b], m)
            freed[b] = list(r)
            outs += list(r)
        return outs

    def piece_of(t_):
        return lambda t, c: t_[:, t, 128 * c:128 * c + 128]

    def hi_lo(dh, dl, after=None):
        def use(k, b, m):
            o = slice(2 * k, 2 * k + 2)
            src = b[:, :].rearrange("p (c t) -> p c t", c=2)
            h = act(lambda e: e.activation(dh[:, o, :], src, ACT.Copy), m, after)
            lo = dve(lambda e: e.tensor_tensor(dl[:, o, :], src, dh[:, o, :].bitcast(F32), ALU.subtract), h, after)
            return h, lo
        return use

    def hi_lo_scaled(dh, dl, name, after=None):
        def use(k, b, m):
            out = []
            for c in range(2):
                ch = 2 * k + c
                s = b[:, 256 * c:256 * c + 256]
                h = act(lambda e, s=s, ch=ch: e.activation(dh[:, ch, :], s, ACT.Copy, scale=V(name, ch)),
                        m, after, l_vec)
            for c in range(2):
                ch = 2 * k + c
                s = b[:, 256 * c:256 * c + 256]
                out.append(dve(lambda e, s=s, ch=ch: e.scalar_tensor_tensor(
                    out=dl[:, ch, :], in0=s, scalar=V(name, ch), in1=dh[:, ch, :].bitcast(F32),
                    op0=ALU.mult, op1=ALU.subtract), h, after))
                out.append(h)
            return out
        return use

    dbg = A.get("_dbg")
    n_dbg = [0]

    def dump(name, ap, ready):
        if dbg is not None and name in dbg:
            d = load(f"dbg_{name}", dbg[name], ap, ready, eng="sp")
            for q in Q.ENGINES:
                put(q, lambda e: None, d)

    hh = slot("hh", 1, [128, 8, 256], F32R)
    hl = slot("hl", 2, [128, 8, 256], F32R)
    ws = slot("ws", 8, [128, 8, 128])
    gvb = slot("gvb", 8, [128, 1024], F32, 4096)
    junk3 = slot("junk3", 3, [128, 2, 1024])
    z_ws = dve(lambda e: e.memset(ws[64:128, :, 0:64], 0.0))
    h_ready = turned(piece_of(x), range(2), l_x, hi_lo_scaled(hh, hl, "g_mix"))
    for _ in range(RING):
        split_ahead()
    l_ws0 = load("ws0", ws[0:64, :, :], A["w_sT"][0:64], loads[1], eng="pool")
    l_ws1 = load("ws1", ws[64:128, :, 64:128], A["w_sT"][64:128, :, 64:128], loads[1], eng="pool")
    l_gvb = load("gvb", gvb[:, :], A["norm_v_g"].broadcast_to([128, 1024]), loads[2], eng="pool")
    bgb = slot("bgb", 9, [128, 2048])
    l_bgb = load("bgb", bgb[:, :], A["b_gate"].broadcast_to([128, 2048]), loads[4], eng="pool")
    nfb = slot("nfb", 10, [128, 1024], F32, 4096)
    l_nfb = load("nfb", nfb[:, :], A["norm_final_g"].broadcast_to([128, 1024]), loads[5], eng="pool")

    def more_h():
        h_ready.extend(turned(piece_of(x), range(2, 4), None, hi_lo_scaled(hh, hl, "g_mix")))
        r1.append(inv_rms(0, D, [squares(x[:, t, :], t, junk3[:, t, :], l_x[t]) for t in range(2)]))

    r1 = []

    vt = slot("vt", 3, [128, 2, 1024])
    ut = slot("ut", 4, [128, 2, 1024])

    def into(dst, fn, after, mids=(None, None), first=None):
        out = []
        for g in range(2):
            b, m = first if first and g == 0 else dense(hh, hl, h_ready, mids[g])
            for t in range(2):
                s = act(lambda e: e.activation(dst[:, t, 512 * g:512 * g + 512], bank[b[t]][:, :], fn,
                                               scale=stat(t)), m, r1, after)
                freed[b[t]] = [s]
                opened.discard(b[t])
                out.append(s)
        return out

    v_ready = into(vt, ACT.Gelu, None, (more_h, None))
    junk5 = slot("junk5", 5, [128, 2, 1024])
    vjunk = slot("vjunk", 4, [128, 1024])
    vs = []

    def norm_v():
        r = inv_rms(8, D, [squares(vt[:, t, :], 8 + t, junk5[:, t, :], v_ready) for t in range(2)])
        for t in range(2):
            vs.append(dve(lambda e: e.scalar_tensor_tensor(
                out=vt[:, t, :], in0=vt[:, t, :], scalar=stat(8 + t), in1=gvb[:, :], op0=ALU.mult,
                op1=ALU.mult), r, l_gvb))

    u_ready = into(ut, ACT.Gelu, None, (norm_v, None))
    a_steps = []
    mixed = []

    def mix_a(t):
        for q in range(2):
            b = take()
            for g in range(4):
                gg = 4 * q + g
                m = pe(lambda e: e.matmul(bank[b][:, 128 * g:128 * g + 128], ws[:, gg, :],
                                          vt[:, t, 128 * gg:128 * gg + 128], start=True, stop=True),
                       vs, z_ws, l_ws0, l_ws1, freed[b])
            fs = []
            for g in range(4):
                gg = 4 * q + g
                fs.append(dve(lambda e: e.scalar_tensor_tensor(
                    out=ut[:, t, 128 * gg:128 * gg + 128], in0=bank[b][:, 128 * g:128 * g + 128],
                    scalar=V("b_s", gg), in1=ut[:, t, 128 * gg:128 * gg + 128], op0=ALU.add, op1=ALU.mult),
                    m, u_ready, l_vec))
            freed[b] = fs
            mixed.append(m)
            a_steps.extend(fs)

    cgt = slot("cgt", 7, [128, 2, 1024])
    cg = into(cgt, ACT.Copy, None, (lambda: mix_a(0), lambda: mix_a(1)))
    dump("a", ut[:, :, :], a_steps)
    ah = slot("ah", 5, [128, 8, 256], F32R)
    al = slot("al", 6, [128, 8, 256], F32R)
    zt = slot("zt", 3, [128, 2, 1024])
    z_ready = []
    a_ready = []
    for g in range(2):
        b, m = dense(hh, hl, h_ready, lambda: a_ready.extend(
            turned(piece_of(ut), range(2 * g, 2 * g + 2), a_steps, hi_lo(ah, al, vs))))
        for t in range(2):
            s = dve(lambda e: e.scalar_tensor_tensor(
                out=zt[:, t, 512 * g:512 * g + 512], in0=bank[b[t]][:, :], scalar=stat(t),
                in1=cgt[:, t, 512 * g:512 * g + 512], op0=ALU.mult, op1=ALU.mult), m, cg, mixed)
            freed[b[t]] = [s]
            z_ready.append(s)
    zT = slot("zT", 4, [128, 8, 256])

    def plain(dst, after=None):
        def use(k, b, m):
            src = b[:, :].rearrange("p (c t) -> p c t", c=2)
            return [act(lambda e: e.activation(dst[:, 2 * k:2 * k + 2, :], src, ACT.Copy), m, after)]
        return use

    zT_ready = []
    y = slot("y", 7, [128, 8, 256])
    y_ready = []

    def conv(q):
        zT_ready.extend(turned(piece_of(zt), range(2 * q, 2 * q + 2), z_ready, plain(zT, a_ready)))
        for c in range(4 * q, 4 * q + 4):
            s = dve(lambda e: e.tensor_scalar(y[:, c, :], zT[:, c, :], V("conv", 16 + c), None, ALU.mult),
                    zT_ready, z_ready)
            for k, d in ((1, 1), (0, 2)):
                s = dve(lambda e: e.scalar_tensor_tensor(
                    out=y[:, c, d:256], in0=zT[:, c, 0:256 - d], scalar=V("conv", 8 * k + c), in1=y[:, c, d:256],
                    op0=ALU.mult, op1=ALU.add), s)
            y_ready.append(s)

    bt = slot("bt", 3, [128, 2, 1024])
    first_bg = dense(hh, hl, h_ready, lambda: conv(0), hold=True)
    flush()
    conv(1)
    b_ready = into(bt, ACT.Copy, zT_ready, first=first_bg)
    ga = slot("ga", 3, [128, 2, 1024])
    ch = slot("ch", 8, [128, 8, 256], F32R)
    cl = slot("cl", 4, [128, 8, 256], F32R)

    def into_c(k, b, m):
        o = slice(2 * k, 2 * k + 2)
        src = b[:, :].rearrange("p (c t) -> p c t", c=2)
        p = dve(lambda e: e.tensor_tensor(y[:, o, :], y[:, o, :], src, ALU.mult), m, y_ready)
        h = act(lambda e: e.activation(ch[:, o, :], y[:, o, :], ACT.Copy), p, mixed, vs)
        lo = dve(lambda e: e.tensor_tensor(cl[:, o, :], y[:, o, :], ch[:, o, :].bitcast(F32), ALU.subtract),
                 h, y_ready)
        return p, h, lo

    c_ready = []
    gate_raw = dense(hh, hl, h_ready, lambda: c_ready.extend(turned(piece_of(bt), range(4), b_ready, into_c)),
                     hold=True)
    dump("cT", y[:, :, :], c_ready)
    gb = slot("gb", 7, [128, 2, 1024])
    sig = {0: [], 1: []}
    for which, dst in ((0, ga), (1, gb)):
        for g in range(2):
            b, m = gate_raw if (which, g) == (0, 0) else dense(hh, hl, h_ready)
            for t in range(2):
                o = slice(512 * g, 512 * g + 512)
                q = slice(1024 * which + 512 * g, 1024 * which + 512 * g + 512)
                s = dve(lambda e: e.scalar_tensor_tensor(
                    out=dst[:, t, o], in0=bank[b[t]][:, :], scalar=stat(t), in1=bgb[:, q], op0=ALU.mult,
                    op1=ALU.add), m, l_bgb, c_ready)
                freed[b[t]] = [s]
                opened.discard(b[t])
                sig[which].append(act(lambda e: e.activation(dst[:, t, o], dst[:, t, o], ACT.Sigmoid), s))
    hh_done = m
    m_ready = []
    mh = slot("mh", 1, [128, 8, 256], F32R)
    ml = slot("ml", 2, [128, 8, 256], F32R)
    mT_ready = []

    def turn_m(q):
        mT_ready.extend(turned(piece_of(ga), range(2 * q, 2 * q + 2), m_ready, hi_lo(mh, ml, hh_done)))

    for which, xh_, xl_, rd, dst in ((0, ah, al, a_ready, ga), (1, ch, cl, c_ready, gb)):
        for g in range(2):
            b, m = dense(xh_, xl_, rd, (lambda: turn_m(0)) if (which, g) == (1, 1) else None)
            for t in range(2):
                o = slice(512 * g, 512 * g + 512)
                s = dve(lambda e: e.tensor_tensor(dst[:, t, o], dst[:, t, o], bank[b[t]][:, :], ALU.mult), m,
                        sig[which])
                freed[b[t]] = [s]
                if which:
                    s = dve(lambda e: e.tensor_tensor(ga[:, t, o], ga[:, t, o], gb[:, t, o], ALU.add), s)
                    m_ready.append(s)
    proj_done = m
    dump("m", ga[:, :, :], m_ready)

    x_ready = []
    fh = slot("fh", 5, [128, 8, 256], F32R)
    fl = slot("fl", 6, [128, 8, 256], F32R)
    f_ready = []

    def turn_f(q):
        f_ready.extend(turned(piece_of(x), range(2 * q, 2 * q + 2), x_ready, hi_lo_scaled(fh, fl, "g_ff", proj_done)))

    sq = []
    for g in range(2):
        b, m = dense(mh, ml, mT_ready, (lambda: turn_m(1)) if g == 0 else lambda: turn_f(0))
        for t in range(2):
            o = slice(512 * g, 512 * g + 512)
            s = dve(lambda e: e.tensor_tensor(x[:, t, o], x[:, t, o], bank[b[t]][:, :], ALU.add), m)
            freed[b[t]] = [s]
            x_ready.append(s)
            sq.append(squares(x[:, t, o], 16 + 2 * g + t, vjunk[:, 512 * t:512 * t + 512], s))
    mm_out = m
    dump("x1", x[:, :, :], x_ready)

    pool_of_banks[0] = [0, 1, 2, 3]
    zz = [slot(f"zz{k}", 3, [128, 2, 512], F32, 4096 * k) for k in range(2)]
    zh = [slot(f"zh{k}", 1, [128, 4, 256], F32R, 4096 * k) for k in range(2)]
    zl = [slot(f"zl{k}", 2, [128, 4, 256], F32R, 4096 * k) for k in range(2)]
    zz_free = [list(mT_ready), list(mT_ready)]
    z2_free = [[mm_out], [mm_out]]
    ff_b = [4, 5, 6, 7]
    r2 = []
    gw = slot("gw", 7, [128, 8, 8])
    gwh = slot("gwh", 8, [128, 8, 128], F32R)
    gwl = slot("gwl", 8, [128, 8, 128], F32R, 4096)
    g2b = slot("g2b", 9, [128, 1024])
    gs = []

    def ff_mid():
        turn_f(1)
        s = dve(lambda e: e.tensor_tensor(stat(16, 2), stat(16, 2), stat(18, 2), ALU.add), sq)
        s = inv_rms(16, D, s)
        r2.append(dve(lambda e: e.tensor_tensor(stat(16, 2), stat(16, 2), stat(16, 2), ALU.mult), s))
        l_gw = load("gw", gw[:, :, :], w_in2[:, GT:GT + 8].rearrange("(c p) n -> p c n", p=128), m_ready, eng="pool")
        zg = [pool(lambda e: e.memset(gwh[:, :, :].bitcast(F32), 0.0), proj_done),
              pool(lambda e: e.memset(gwl[:, :, :].bitcast(F32), 0.0), proj_done)]
        for k in range(2):
            o, i_ = slice(32 * k, 32 * k + 4), slice(4 * k, 4 * k + 4)
            h = dve(lambda e: e.tensor_copy(gwh[:, :, o], gw[:, :, i_]), l_gw, zg)
            gs.append(dve(lambda e: e.tensor_tensor(gwl[:, :, o], gw[:, :, i_], gwh[:, :, o].bitcast(F32),
                                                    ALU.subtract), h))

    l_g2b = load("g2b", g2b[:, :], A["g_norm2_2"].broadcast_to([128, 1024]), sig[1], eng="pool")
    zr = {}
    zT2 = {}
    for g in range(9):
        if g < 8:
            b, m = dense(fh, fl, f_ready, ff_mid if g == 0 else None)
            zr[g] = []
            for t in range(2):
                s = act(lambda e: e.activation(zz[g % 2][:, t, :], bank[b[t]][:, :], ACT.Relu), m,
                        zz_free[g % 2])
                freed[b[t]] = [s]
                zr[g].append(dve(lambda e: e.tensor_tensor(zz[g % 2][:, t, :], zz[g % 2][:, t, :],
                                                           zz[g % 2][:, t, :], ALU.mult), s))
        if g > 0:
            p = g - 1
            two = [next_half(), next_half()] if p == 7 else None
            for t_ in ((0, 1) if p == 7 else (None,)):
                for hf in range(2):
                    half = two[hf] if two else next_half()
                    i, s, h, lo = half
                    for c in range(2):
                        f = 2 * hf + c
                        for t in range(2) if t_ is None else (t_,):
                            for which, lhs in ((0, zh), (1, zl)):
                                a = lhs[p % 2][:, f, 128 * t:128 * t + 128]
                                for n in range(2):
                                    o = bank[ff_b[2 * t + n]][:, :]
                                    r_h = whi[s][:, 1024 * c + 512 * n:1024 * c + 512 * n + 512]
                                    r_l = wlo[s][:, 1024 * c + 512 * n:1024 * c + 512 * n + 512]
                                    first = p == 0 and f == 0 and which == 0
                                    end = p == 7 and f == 3 and which == 1
                                    m = pe(lambda e: e.matmul(o, a, r_h, start=first, stop=end), h, zT2[p],
                                           freed[ff_b[2 * t + n]] if first else None)
                                    if which == 0:
                                        m = pe(lambda e: e.matmul(o, a, r_l, start=False, stop=False), lo)
                    if t_ is None:
                        half_done(i, s, m)
                    elif t_ == 1:
                        half_done(i, s, m, True)
                if t_ == 0:
                    t0_done = m
            z2_free[p % 2] = [m]
        if g < 8:
            zT2[g] = turned(piece_of(zz[g % 2]), range(2), zr[g], hi_lo(zh[g % 2], zl[g % 2], z2_free[g % 2]))
            zz_free[g % 2] = [Q.last["pe"]]
    ff_done = m
    s_a2 = dve(lambda e: e.scalar_tensor_tensor(out=scale2b[:, :], in0=scale2b[:, :], scalar=1.0, in1=g2b[:, :],
                                                op0=ALU.add, op1=ALU.mult), l_g2b, ada_done[8], ada_done[9])
    a1 = small("a1", [128, 8])
    a1_ready = dve(lambda e: e.scalar_tensor_tensor(
        out=a1[:, :], in0=ada_cols[:, 8:16], scalar=1.0, in1=vec[:, VEC["g1"]:VEC["g1"] + 8], op0=ALU.add,
        op1=ALU.mult), ada_done[2], ada_done[3], l_vec)
    a1_ready = dve(lambda e: e.tensor_tensor(a1[:, :], a1[:, :], vec[:, VEC["g_nf"]:VEC["g_nf"] + 8], ALU.mult),
                   a1_ready)
    xg = slot("xg", 3, [128, 2, 1024])
    junk9 = slot("junk9", 9, [128, 1024], F32, 4096)
    x2_ready = []
    sums = []
    for t, d in ((0, t0_done), (1, ff_done)):
        for n in range(2):
            o = slice(512 * n, 512 * n + 512)
            b = ff_b[2 * t + n]
            s = dve(lambda e: e.scalar_tensor_tensor(out=x[:, t, o], in0=bank[b][:, :], scalar=stat(16 + t),
                                                     in1=x[:, t, o], op0=ALU.mult, op1=ALU.add), d, r2)
            freed[b] = [s]
            x2_ready.append(s)
        s1 = squares(x[:, t, :], 24 + t, junk9[:, :], [x2_ready[-2:], sums])
        s = dve(lambda e: e.tensor_tensor(xg[:, t, :], x[:, t, :], nfb[:, :], ALU.mult), x2_ready[-2:], l_nfb,
                zT2[7])
        sums.append(s1)
        sums.append(squares(xg[:, t, :], 26 + t, junk9[:, :], [s, s1]))
    dump("x2", x[:, :, :], x2_ready)
    pool_of_banks[0] = list(range(8))
    xT_b = []

    def keep(k, b, m):
        xT_b.append((k, b, m))
        return []

    turned(piece_of(x), range(4), x2_ready, keep)
    r1 = inv_rms(24, D, sums)
    s = dve(lambda e: e.tensor_tensor(stat(28, 2), stat(24, 2), stat(24, 2), ALU.mult), r1)
    s = dve(lambda e: e.tensor_tensor(stat(26, 2), stat(26, 2), stat(28, 2), ALU.mult), s)
    s = inv_rms(26, D, s)
    s = dve(lambda e: e.tensor_tensor(stat(28, 2), stat(24, 2), stat(26, 2), ALU.mult), s)
    diag = slot("diag", 7, [128, 2, 128], F32, 1024)
    Rb = slot("Rb", 7, [128, 256], F32, 2048)
    dg = [dve(lambda e, t=t: e.tensor_scalar(diag[:, t, :], C("ident"), stat(28 + t), None, ALU.mult), s, l_cst)
          for t in range(2)]
    b = take()
    for t in range(2):
        m = pe(lambda e: e.matmul(bank[b][:, 128 * t:128 * t + 128], C("ones"), diag[:, t, :], start=True, stop=True),
               dg, freed[b])
    rb = act(lambda e: e.activation(Rb[:, :], bank[b][:, 0:256], ACT.Copy), m)
    freed[b] = [rb]
    nh = slot("nh", 5, [128, 8, 256], F32R)
    nl = slot("nl", 6, [128, 8, 256], F32R)
    nf = slot("nf", 4, [128, 8, 256])
    n_ready = []

    def modulate(which):
        for k, bk, m in xT_b[which]:
            fs = []
            for c in range(2):
                q = 2 * k + c
                src = bk[:, 256 * c:256 * c + 256]
                f = dve(lambda e: e.scalar_tensor_tensor(
                    out=nf[:, q, :], in0=src, scalar=a1[:, q:q + 1], in1=Rb[:, :], op0=ALU.mult, op1=ALU.mult),
                    m, a1_ready, rb)
                h = act(lambda e: e.activation(nh[:, q, :], nf[:, q, :], ACT.Identity, bias=ada_cols[:, q:q + 1]),
                        f, ff_done, ada_done[0], ada_done[1])
                fs.append(f)
                n_ready.append(h)
            for c in range(2):
                q = 2 * k + c
                n_ready.append(dve(lambda e: e.scalar_tensor_tensor(
                    out=nl[:, q, :], in0=nf[:, q, :], scalar=ada_cols[:, q:q + 1], in1=nh[:, q, :].bitcast(F32),
                    op0=ALU.add, op1=ALU.subtract), n_ready[-2:], ff_done))
            for bb in range(8):
                if bank[bb] is bk:
                    freed[bb] = fs

    modulate(slice(0, 2))
    x_ready = []

    def more_n():
        modulate(slice(2, 4))
        for t in range(2):
            x_ready.append(act(lambda e: e.activation(x[:, t, :], xg[:, t, :], ACT.Copy, scale=stat(24 + t)),
                               [m_ for _, _, m_ in xT_b], r1))

    qt = slot("qt", 3, [128, 2, 1024])
    q_ready = []

    def raw_into(dst, g, ready, after, mid=None, fn=None):
        b, m = dense(nh, nl, n_ready, mid)
        for t in range(2):
            s = act(lambda e: e.activation(dst[:, t, 512 * g:512 * g + 512], bank[b[t]][:, :], fn or ACT.Copy), m,
                    after)
            freed[b[t]] = [s]
            ready.append(s)

    raw_into(qt, 0, q_ready, x_ready, more_n)
    b = take()
    for c in range(8):
        for a_, r_ in ((gwh, nh), (gwh, nl), (gwl, nh)):
            m = pe(lambda e: e.matmul(bank[b][:, 0:256], a_[:, c, :], r_[:, c, :],
                                      start=c == 0 and a_ is gwh and r_ is nh, stop=c == 7 and a_ is gwl),
                   gs, n_ready, freed[b])
    gates_mm = m
    flush()
    R = {}
    for k, n in enumerate(("i", "f", "w0", "w1")):
        R[n] = slot(f"row_{n}", 10, [4, 256], F32, 2048 + 1024 * k)
    for k, n in enumerate(("F", "M")):
        R[n] = slot(f"row_{n}", 10, [4, 256], F32, 6144 + 1024 * k)
    rd = [gates_mm, x_ready, ada_done[11]]
    s1 = dve(lambda e: e.tensor_scalar(R["i"][:, :], bank[b][0:4, 0:256], V("bg", 0, slice(0, 4)), None,
                                       ALU.add), rd)
    s2 = dve(lambda e: e.tensor_scalar(R["f"][:, :], bank[b][32:36, 0:256], V("bg", 1, slice(32, 36)), None,
                                       ALU.add), rd)
    freed[b] = [s1, s2]
    s3 = dve(lambda e: e.tensor_scalar(R["w0"][:, :], R["f"][:, :], -1.0, None, ALU.mult), s2)
    s3 = dve(lambda e: e.tensor_tensor(R["w0"][:, :], R["w0"][:, :], R["f"][:, :], ALU.min), s3)
    s3 = act(lambda e: e.activation(R["w0"][:, :], R["w0"][:, :], ACT.Exp), s3)
    s3 = dve(lambda e: e.tensor_scalar(R["w0"][:, :], R["w0"][:, :], 1.0, None, ALU.add), s3)
    s3 = act(lambda e: e.activation(R["w0"][:, :], R["w0"][:, :], ACT.Ln), s3)
    s3 = dve(lambda e: e.scalar_tensor_tensor(out=R["f"][:, :], in0=R["f"][:, :], scalar=0.0, in1=R["w0"][:, :],
                                              op0=ALU.min, op1=ALU.subtract), s3)
    z1 = dve(lambda e: e.memset(R["w1"][:, :], 0.0), rd)
    s4 = dve(lambda e: e.tensor_tensor_scan(R["F"][:, :], R["f"][:, :], R["w1"][:, :], 0.0, ALU.add, ALU.add),
             s3, z1)
    s5 = dve(lambda e: e.tensor_tensor(R["i"][:, :], R["i"][:, :], R["F"][:, :], ALU.subtract), s4, s1)
    s6 = dve(lambda e: e.tensor_tensor_scan(R["M"][:, :], R["i"][:, :], R["w1"][:, :], 0.0, ALU.max, ALU.max), s5)
    s7 = dve(lambda e: e.tensor_tensor(R["w0"][:, :], R["F"][:, :], R["M"][:, :], ALU.add), s6)
    s7 = act(lambda e: e.activation(R["w0"][:, :], R["w0"][:, :], ACT.Exp, scale=-1.0), s7)
    acol = small("acol", [128, 2, 4])
    ecol = small("ecol", [128, 2, 4])
    raw_into(qt, 1, q_ready, x_ready)

    ET = slot("ET", 9, [128, 4, 2, 256])
    e_ready = {}
    cols_of = []

    def decays():
        b = take()
        for k, (n, rdy) in enumerate((("i", s5), ("w0", s7))):
            for t in range(2):
                m = pe(lambda e: e.transpose(
                    bank[b][:, 8 * k + 4 * t:8 * k + 4 * t + 4], R[n][:, 128 * t:128 * t + 128],
                    cst[0:4, CST["ident"]:CST["ident"] + 4]), rdy, freed[b])
        col1 = dve(lambda e: e.tensor_copy(acol[:, :, :], bank[b][:, 0:8].rearrange("p (t h) -> p t h", t=2)), m)
        col2 = dve(lambda e: e.tensor_copy(ecol[:, :, :], bank[b][:, 8:16].rearrange("p (t h) -> p t h", t=2)), m)
        freed[b] = [col1, col2]
        cols_of.extend([col1, col2])
        for h in range(4):
            b2 = take()
            m = pe(lambda e: e.matmul(
                bank[b2][:, 0:256], cst[0:4, CST["ident"] + h:CST["ident"] + h + 1].to_broadcast([4, 128]),
                R["M"][:, :], start=True, stop=True), s6, freed[b2])
            fs = []
            for s_ in range(2):
                o = slice(128 * s_, 256)
                d = dve(lambda e: e.tensor_scalar(ET[:, h, s_, o], bank[b2][:, o], acol[:, s_, h:h + 1], 0.0,
                                                  ALU.subtract, ALU.max), m, col1, s_a2, sums)
                fs.append(d)
                d = dve(lambda e: e.tensor_tensor(
                    ET[:, h, s_, 128 * s_:128 * s_ + 128], ET[:, h, s_, 128 * s_:128 * s_ + 128], C("pen_st"),
                    ALU.add), d)
                e_ready[h, s_] = act(lambda e: e.activation(ET[:, h, s_, o], ET[:, h, s_, o], ACT.Exp, scale=-1.0),
                                     d)
            freed[b2] = fs

    qT = slot("qT", 4, [128, 8, 256])
    qT_ready = []
    qc = slot("qc", 7, [128, 8, 256])
    qc_ready = []

    def turn_q():
        qT_ready.extend(turned(piece_of(qt), range(4), q_ready, plain(qT, n_ready)))

    def conv2(c0):
        for c in range(c0, c0 + 4):
            s = dve(lambda e: e.tensor_scalar(qc[:, c, :], qT[:, c, :], V("conv2", 24 + c), V("bconv2", c),
                                              ALU.mult, ALU.add), qT_ready, n_ready, gs)
            for k, d in ((2, 1), (1, 2), (0, 3)):
                s = dve(lambda e: e.scalar_tensor_tensor(
                    out=qc[:, c, d:256], in0=qT[:, c, 0:256 - d], scalar=V("conv2", 8 * k + c), in1=qc[:, c, d:256],
                    op0=ALU.mult, op1=ALU.add), s)
            qc_ready.append(act(lambda e: e.activation(qc[:, c, :], qc[:, c, :], ACT.Silu), s))

    qa = slot("qa", 8, [128, 2, 1024])
    qa_ready = []
    qaT = slot("qaT", 3, [128, 8, 256])
    qaT_ready = []
    vmt = slot("vmt", 2, [128, 2, 512])
    vat = slot("vat", 2, [128, 2, 512], F32, 4096)
    omt = slot("omt", 1, [128, 2, 512])
    va_ready, vm_ready, om_ready = [], [], []
    MSC = 128 ** -0.5
    ASC = 64 ** -0.5
    sc_ready = {}

    def turn_qa(pairs):
        qaT_ready.extend(turned(piece_of(qa), pairs, qa_ready, plain(qaT, qT_ready)))

    def mlstm_scores():
        for h in range(4):
            b = take()
            where = [(s_, slice(128 * s_, 256), slice(256 * s_ + 128 * s_, 256 * s_ + 256)) for s_ in range(2)]
            for s_, o, po in where:
                m = pe(lambda e: e.matmul(bank[b][:, po], qc[:, 4 + h, 128 * s_:128 * s_ + 128], qc[:, h, o],
                                          start=True, stop=True), qc_ready, freed[b])
            for s_, o, po in where:
                sc_ready[h, s_] = dve(lambda e: e.scalar_tensor_tensor(
                    out=ET[:, h, s_, o], in0=bank[b][:, po], scalar=MSC, in1=ET[:, h, s_, o], op0=ALU.mult,
                    op1=ALU.mult), m, e_ready[h, s_])
            freed[b] = [sc_ready[h, 0], sc_ready[h, 1]]

    mix = slot("mix", 10, [128, 2, 1024])
    junk1 = slot("junk1", 1, [128, 128], F32, 4096)
    ghb = slot("ghb", 1, [128, 512], F32, 4608)
    wr = slot("wr", 1, [128, 8, 36], F32, 6656)
    brb = slot("brb", 1, [128, 36], F32, 7808)
    hm_last = []

    def mlstm_out(t):
        b = take()
        dn = take()
        for h in range(4):
            for s_ in range(t + 1):
                lhs = ET[:, h, s_, 128 * t:128 * t + 128]
                pe(lambda e: e.matmul(
                    bank[b][:, 128 * h:128 * h + 128], lhs, vmt[:, s_, 128 * h:128 * h + 128],
                    start=(s_ == 0), stop=(s_ == t)), sc_ready[h, s_], vm_ready, freed[b])
            for s_ in range(t + 1):
                lhs = ET[:, h, s_, 128 * t:128 * t + 128]
                m = pe(lambda e: e.matmul(bank[dn][:, h:h + 1], lhs, C("ones", 0, 1), start=(s_ == 0),
                                          stop=(s_ == t)), freed[dn])
        k = 40 + 16 * t
        d1 = dve(lambda e: e.tensor_scalar(stat(k, 4), bank[dn][:, 0:4], -1.0, None, ALU.mult), m)
        d2 = dve(lambda e: e.tensor_tensor(stat(k, 4), stat(k, 4), bank[dn][:, 0:4], ALU.max), d1)
        d3 = dve(lambda e: e.tensor_tensor(stat(k, 4), stat(k, 4), ecol[:, t, :], ALU.max), d2)
        d4 = dve(lambda e: e.reciprocal(stat(k, 4), stat(k, 4)), d3)
        freed[dn] = [d2]
        hs, ss = [], []
        for h in range(4):
            o = slice(128 * h, 128 * h + 128)
            s = dve(lambda e: e.tensor_scalar(mix[:, t, o], bank[b][:, o], stat(k + h), None, ALU.mult), d4, m,
                    rows_done)
            hs.append(s)
            ss.append(act(lambda e: e.activation(junk1[:, :], mix[:, t, o], ACT.Square, accum_out=stat(k + 4 + h)),
                          s, ss[-1] if ss else last_junk))
        last_junk[:] = [ss[-1]]
        freed[b] = hs
        d = dve(lambda e: e.tensor_tensor(omt[:, t, :], omt[:, t, :], ghb[:, :], ALU.mult), om_ready, l_ghb)
        d5 = inv_rms(k + 4, 128, ss, 4)
        for h in range(4):
            o = slice(128 * h, 128 * h + 128)
            hm_last.append(dve(lambda e: e.scalar_tensor_tensor(
                out=mix[:, t, o], in0=mix[:, t, o], scalar=stat(k + 4 + h), in1=omt[:, t, o], op0=ALU.mult,
                op1=ALU.mult), d, d5))

    last_junk = []
    S = [slot("S0", 4, [128, 4, 384]), slot("S1", 8, [128, 4, 384])]
    PTt = [slot("PTt0", 3, [128, 4, 384]), slot("PTt1", 4, [128, 4, 384])]
    exps, recips, pts, att_last = {}, {}, {}, []
    S_free = [qc_ready, qaT_ready]
    pt_free = {}
    pen = C("pen_ts").unsqueeze(1)

    def att_scores(half):
        Sx = S[half]
        b0, b1, b2 = take(3)
        for hq in range(4):
            h = 2 * hq + half
            c, p0 = h // 2, 64 * (h % 2)
            q0 = qaT[p0:p0 + 64, c, :]
            k0 = qaT[p0:p0 + 64, 4 + c, :]
            o0 = bank[b0][:, 128 * hq:128 * hq + 128]
            o1 = bank[[b1, b2][hq // 2]][:, 256 * (hq % 2):256 * (hq % 2) + 256]
            pe(lambda e: e.matmul(o0, q0[:, 0:128], k0[:, 0:128], start=True, stop=True), qaT_ready, freed[b0])
            m = pe(lambda e: e.matmul(o1, q0[:, 128:256], k0, start=True, stop=True), freed[[b1, b2][hq // 2]])
        w = []
        w.append(dve(lambda e: e.tensor_tensor(
            Sx[:, :, 0:128], bank[b0][:, :].rearrange("p (h s) -> p h s", h=4),
            pen.broadcast_to([128, 4, 128]), ALU.add), m, S_free[half]))
        for k, bb in enumerate((b1, b2)):
            src = bank[bb][:, :].rearrange("p (h s) -> p h s", h=2)
            w.append(act(lambda e: e.activation(Sx[:, 2 * k:2 * k + 2, 128:256], src[:, :, 0:128], ACT.Copy), m,
                         S_free[half]))
            w.append(dve(lambda e: e.tensor_tensor(
                Sx[:, 2 * k:2 * k + 2, 256:384], src[:, :, 128:256], pen.broadcast_to([128, 2, 128]), ALU.add),
                m, w[-1], S_free[half]))
        freed[b0], freed[b1], freed[b2] = [w[0]], [w[1], w[2]], [w[3], w[4]]
        k = 72 + 28 * half
        mx = [dve(lambda e: e.tensor_reduce(stat(k, 4), Sx[:, :, 0:128], AX, ALU.max, negate=False), w),
              dve(lambda e: e.tensor_reduce(stat(k + 4, 4), Sx[:, :, 128:384], AX, ALU.max, negate=False), w)]
        mx = dve(lambda e: e.tensor_scalar(stat(k, 8), stat(k, 8), -ASC, None, ALU.mult), mx)
        ex = []
        for hq in range(4):
            for t, o in ((0, slice(0, 128)), (1, slice(128, 384))):
                ex.append(act(lambda e: e.activation(
                    Sx[:, hq, o], Sx[:, hq, o], ACT.Exp, bias=stat(k + 4 * t + hq), scale=ASC,
                    accum_out=stat(k + 8 + 4 * t + hq)), mx))
        exps[half] = ex
        recips[half] = dve(lambda e: e.reciprocal(stat(k + 16, 8), stat(k + 8, 8)), ex)
        pt_free[half] = [m]

    def att_turn(half):
        Sx = S[half]
        pts[half] = []
        for hq in range(4):
            b = take()
            for j in range(3):
                m = pe(lambda e: e.transpose(bank[b][:, 128 * j:128 * j + 128], Sx[:, hq, 128 * j:128 * j + 128],
                                             C("ident")), exps[half], freed[b])
            if hq % 2:
                s = act(lambda e: e.activation(PTt[half][:, hq, :], bank[b][:, 0:384], ACT.Copy), m,
                        pt_free[half])
            else:
                s = dve(lambda e: e.tensor_copy(PTt[half][:, hq, :], bank[b][:, 0:384]), m, pt_free[half])
            freed[b] = [s]
            pts[half].append(s)
        if half == 0:
            pt_free[1] = [m]

    def att_values(half):
        k = 72 + 28 * half
        P = PTt[half]
        b = take()
        for hq in range(4):
            h = 2 * hq + half
            vv = [vat[:, s_, 64 * h:64 * h + 64] for s_ in range(2)]
            o0 = bank[b][:, 64 * hq:64 * hq + 64]
            o1 = bank[b][:, 256 + 64 * hq:256 + 64 * hq + 64]
            pe(lambda e: e.matmul(o0, P[:, hq, 0:128], vv[0], start=True, stop=True), pts[half], va_ready, freed[b])
            pe(lambda e: e.matmul(o1, P[:, hq, 128:256], vv[0], start=True, stop=False))
            m = pe(lambda e: e.matmul(o1, P[:, hq, 256:384], vv[1], start=False, stop=True))
        fs = []
        for t in range(2):
            o = mix[:, t, 512:1024].rearrange("p (h w d) -> p w h d", h=4, w=2)[:, half, :, :]
            fs.append(dve(lambda e: e.tensor_tensor(
                o, bank[b][:, 256 * t:256 * t + 256].rearrange("p (h d) -> p h d", h=4),
                stat(k + 16 + 4 * t, 4).unsqueeze(2).broadcast_to([128, 4, 64]), ALU.mult), m, recips[half],
                rows_done))
        freed[b] = fs
        att_last.extend(fs)

    raw_into(qa, 0, qa_ready, gates_mm, turn_q)
    flush()
    conv2(0)
    raw_into(qa, 1, qa_ready, gates_mm, decays)
    rows_done = [s7, *cols_of, *e_ready.values(), gs[-1]]
    flush()
    conv2(4)
    l_ghb = load("ghb", ghb[:, :], A["g_mlstm_head_2"].broadcast_to([128, 512]), ff_done, eng="pool")
    l_wr0 = load("wr0", wr[:, :, 0:4], A["w_router_group_2"][0].rearrange("(c p) n -> p c n", p=128), ff_done,
                 eng="pool")
    l_wr1 = load("wr1", wr[:, :, 4:36], A["w_router_expert_2"][0].rearrange("(c p) n -> p c n", p=128), ff_done,
                 eng="pool")
    l_br0 = load("br0", brb[:, 0:4], A["b_router_group_2"].broadcast_to([128, 4]), ff_done, eng="pool")
    l_br1 = load("br1", brb[:, 4:36], A["b_router_expert_2"].broadcast_to([128, 32]), ff_done, eng="pool")
    b, m = dense(nh, nl, n_ready, lambda: turn_qa(range(4)))
    for t in range(2):
        s = act(lambda e: e.activation(vat[:, t, :], bank[b[t]][:, :], ACT.Copy), m)
        freed[b[t]] = [s]
        va_ready.append(s)
    flush()
    att_scores(0)
    att_scores(1)
    pt_free[0] = pt_free[1]
    b, m = dense(nh, nl, n_ready, mlstm_scores)
    for t in range(2):
        s = act(lambda e: e.activation(vmt[:, t, :], bank[b[t]][:, :], ACT.Copy), m)
        freed[b[t]] = [s]
        vm_ready.append(s)
    flush()
    att_turn(0)
    b, m = dense(nh, nl, n_ready, lambda: att_turn(1))
    for t in range(2):
        s = act(lambda e: e.activation(omt[:, t, :], bank[b[t]][:, :], ACT.Sigmoid), m)
        freed[b[t]] = [s]
        om_ready.append(s)
    nh_done = m
    flush()
    att_values(0)
    att_values(1)
    mlstm_out(0)
    mlstm_out(1)
    mxh = slot("mxh", 5, [128, 8, 256], F32R)
    mxl = slot("mxl", 6, [128, 8, 256], F32R)
    mix_ready = turned(piece_of(mix), range(2, 4), att_last, hi_lo(mxh, mxl, nh_done))
    b4 = [take(2), take(2)]
    for bb in b4:
        opened.update(bb)
    for g in range(2):
        half = next_half()
        half_done(half[0], half[1], dense_half(mxh, mxl, mix_ready, b4[g], half, 1, True, False), g == 1)
    dump("mix", mix[:, :, :], [*att_last, *hm_last])
    mix_ready += turned(piece_of(mix), range(2), hm_last, hi_lo(mxh, mxl, nh_done))
    gx = slot("gx", 3, [128, 2, 1024])
    x_ready = []
    sq = []
    junk4 = slot("junk4", 4, [128, 2, 1024])
    for g in range(2):
        half = next_half()
        m = dense_half(mxh, mxl, mix_ready, b4[g], half, 0, False, True)
        half_done(half[0], half[1], m, True)
        for t in range(2):
            o = slice(512 * g, 512 * g + 512)
            b = b4[g][t]
            s = dve(lambda e: e.tensor_tensor(gx[:, t, o], bank[b][:, :], gate1b[:, o], ALU.mult), m, ada_done[4],
                    ada_done[5], att_last, pts[0])
            freed[b] = [s]
            x_ready.append(dve(lambda e: e.tensor_tensor(x[:, t, o], x[:, t, o], gx[:, t, o], ALU.add), s))
            sq.append(squares(x[:, t, o], 2 * g + t, junk4[:, t, o], [x_ready[-1], att_last]))
    opened.clear()
    mixes_done = m
    dump("x3", x[:, :, :], x_ready)
    gfb = slot("gfb", 7, [128, 1024])
    l_gfb = load("gfb", gfb[:, :], A["g_final_2"].broadcast_to([128, 1024]), x_ready, eng="pool")
    h2 = slot("h2", 10, [128, 2, 1024])
    s = dve(lambda e: e.tensor_tensor(stat(0, 2), stat(0, 2), stat(2, 2), ALU.add), sq)
    r = inv_rms(0, D, s)
    h2r = []
    for t in range(2):
        s = dve(lambda e: e.scalar_tensor_tensor(out=h2[:, t, :], in0=x[:, t, :], scalar=stat(t),
                                                 in1=scale2b[:, :], op0=ALU.mult, op1=ALU.mult), r, s_a2, mix_ready)
        h2r.append(dve(lambda e: e.tensor_tensor(h2[:, t, :], h2[:, t, :], shift2b[:, :], ALU.add), s,
                       ada_done[6], ada_done[7]))
    dump("h2", h2[:, :, :], h2r)
    h2T = slot("h2T", 3, [128, 8, 256])
    h2T_ready = turned(piece_of(h2), range(4), h2r, plain(h2T, x_ready))
    th = slot("th", 2, [128, 2, 1024], F32R)
    tl = slot("tl", 9, [128, 2, 1024], F32R)
    b = take()
    for t in range(2):
        for c in range(8):
            m = pe(lambda e: e.matmul(
                bank[b][:, 36 * t:36 * t + 36], h2T[:, c, 128 * t:128 * t + 128], wr[:, c, :], start=(c == 0),
                stop=(c == 7)), h2T_ready, l_wr0, l_wr1, freed[b])
    router_mm = m
    th_r = [act(lambda e, t=t: e.activation(th[:, t, :], h2[:, t, :], ACT.Copy), h2r, mixes_done)
            for t in range(2)]
    flush()

    lg = small("lg", [128, 2, 36])
    WT, MK, RK, T0, T1, T2 = (tab[:, k, :, :] for k in range(6))
    rs = small("rs", [128, 2, 16])

    def B(ap, n):
        return ap.broadcast_to([128, 2, n])

    s = dve(lambda e, b=b: e.tensor_tensor(
        lg[:, :, :], bank[b][:, 0:72].rearrange("p (t n) -> p t n", t=2),
        brb[:, 0:36].unsqueeze(1).broadcast_to([128, 2, 36]), ALU.add), m, l_br0, l_br1)
    freed[b] = [s]
    tl_r = [dve(lambda e, t=t: e.tensor_tensor(tl[:, t, :], h2[:, t, :], th[:, t, :].bitcast(F32), ALU.subtract),
                th_r, s_a2, s) for t in range(2)]
    dump("lg", lg[:, :, :], s)

    def chain(fn, *after):
        cur[0] = dve(fn, cur[0], *after)
        return cur[0]

    cur = [s]

    def first_max(src, n, top, hot, tmp):
        chain(lambda e: e.tensor_reduce(top, src, AX, ALU.max))
        chain(lambda e: e.tensor_tensor(tmp, src, B(top, n), ALU.is_lt))
        io = C("iota32", 0, n).unsqueeze(1).broadcast_to([128, 2, n])
        chain(lambda e: e.scalar_tensor_tensor(out=tmp, in0=tmp, scalar=FAR, in1=io, op0=ALU.mult, op1=ALU.add))
        chain(lambda e: e.tensor_reduce(rs[:, :, 15:16], tmp, AX, ALU.min))
        return chain(lambda e: e.tensor_tensor(hot, io, B(rs[:, :, 15:16], n), ALU.is_equal))

    G = lg[:, :, 0:4]
    E_ = lg[:, :, 4:36]
    first_max(G, 4, rs[:, :, 0:1], rs[:, :, 4:8], rs[:, :, 8:12])
    chain(lambda e: e.tensor_tensor(rs[:, :, 8:12], G, B(rs[:, :, 0:1], 4), ALU.subtract))
    ex = act(lambda e: e.activation(rs[:, :, 8:12], rs[:, :, 8:12], ACT.Exp), cur[0])
    cur[0] = ex
    chain(lambda e: e.tensor_reduce(rs[:, :, 1:2], rs[:, :, 8:12], AX, ALU.add))
    chain(lambda e: e.reciprocal(rs[:, :, 1:2], rs[:, :, 1:2]))
    hot8 = rs[:, :, 4:8].unsqueeze(3).broadcast_to([128, 2, 4, 8])
    chain(lambda e: e.tensor_copy(T0.rearrange("p t (g n) -> p t g n", g=4), hot8))
    chain(lambda e: e.tensor_tensor(T1, T0, E_, ALU.mult))
    chain(lambda e: e.tensor_scalar(T0, T0, BIG, -BIG, ALU.mult, ALU.add))
    chain(lambda e: e.tensor_tensor(T1, T1, T0, ALU.add))
    first_max(T1, 32, rs[:, :, 2:3], WT, T0)
    chain(lambda e: e.scalar_tensor_tensor(out=T1, in0=WT, scalar=-2 * BIG, in1=T1, op0=ALU.mult, op1=ALU.add))
    first_max(T1, 32, rs[:, :, 3:4], T2, T0)
    chain(lambda e: e.tensor_tensor(MK, WT, T2, ALU.add))
    chain(lambda e: e.tensor_tensor(rs[:, :, 8:9], rs[:, :, 3:4], rs[:, :, 2:3], ALU.subtract))
    cur[0] = act(lambda e: e.activation(rs[:, :, 8:9], rs[:, :, 8:9], ACT.Exp), cur[0])
    chain(lambda e: e.tensor_scalar(rs[:, :, 9:10], rs[:, :, 8:9], 1.0, None, ALU.add))
    chain(lambda e: e.reciprocal(rs[:, :, 9:10], rs[:, :, 9:10]))
    chain(lambda e: e.tensor_tensor(rs[:, :, 9:10], rs[:, :, 9:10], rs[:, :, 1:2], ALU.mult))
    chain(lambda e: e.tensor_tensor(rs[:, :, 8:9], rs[:, :, 8:9], rs[:, :, 9:10], ALU.mult))
    chain(lambda e: e.tensor_tensor(WT, WT, B(rs[:, :, 9:10], 32), ALU.mult))
    chain(lambda e: e.tensor_tensor(T2, T2, B(rs[:, :, 8:9], 32), ALU.mult))
    wt_ready = chain(lambda e: e.tensor_tensor(WT, WT, T2, ALU.add))
    b = take()
    pe(lambda e, b=b: e.matmul(bank[b][:, 0:32], C("lt"), MK[:, 0, :], start=True, stop=True), cur[0], freed[b])
    pe(lambda e, b=b: e.matmul(bank[b][:, 32:64], C("lt"), MK[:, 1, :], start=True, stop=False))
    pe(lambda e, b=b: e.matmul(bank[b][:, 32:64], C("ones"), MK[:, 0, :], start=False, stop=True))
    pe(lambda e, b=b: e.matmul(bank[b][:, 64:96], C("ones"), MK[:, 0, :], start=True, stop=False))
    m = pe(lambda e, b=b: e.matmul(bank[b][:, 64:96], C("ones"), MK[:, 1, :], start=False, stop=True))
    chain(lambda e: e.tensor_scalar(T0, MK, -FAR, FAR, ALU.mult, ALU.add), m)
    rk_ready = chain(lambda e, b=b: e.tensor_tensor(
        RK, T0, bank[b][:, 0:64].rearrange("p (t n) -> p t n", t=2), ALU.add))
    cnt = small("cnt", [128, 8, 32])
    chain(lambda e, b=b: e.tensor_copy(cnt[:, 0, :], bank[b][:, 64:96]))
    freed[b] = [cur[0]]
    THR = [float(SLOTS * k) for k in (1, 2, 3)]
    for k in range(3):
        chain(lambda e, k=k: e.tensor_scalar(cnt[:, 1 + k, :], cnt[:, 0, :], THR[k], None, ALU.is_gt))
    chain(lambda e: e.tensor_tensor(cnt[:, 1, :], cnt[:, 1, :], cnt[:, 2, :], ALU.add))
    chain(lambda e: e.tensor_tensor(cnt[:, 1, :], cnt[:, 1, :], cnt[:, 3, :], ALU.add))
    chain(lambda e: e.memset(cnt[:, 2, :], 0.0))
    chain(lambda e: e.tensor_tensor_scan(cnt[:, 3, :], cnt[:, 1, :], cnt[:, 2, :], 0.0, ALU.add, ALU.add))
    chain(lambda e: e.tensor_tensor(cnt[:, 4, :], cnt[:, 3, :], cnt[:, 1, :], ALU.subtract))
    ov_ready = chain(lambda e: e.tensor_copy(ovf[:, 0:1], cnt[:, 3, 31:32]))
    for j in range(NOV):
        chain(lambda e, j=j: e.tensor_scalar(cnt[:, 5, :], cnt[:, 3, :], float(j), None, ALU.is_le))
        chain(lambda e, j=j: e.tensor_reduce(cnt[:, 6, j:j + 1], cnt[:, 5, :], AX, ALU.add))
    chain(lambda e: e.tensor_scalar(cnt[:, 7, 0:NOV], cnt[:, 6, 0:NOV], float(NE - 1), None, ALU.min))
    ids_step = chain(lambda e: e.tensor_copy(ovf[:, 8:8 + NOV], cnt[:, 7, 0:NOV]))
    ids_ready.append(ids_step)
    dump("tab", tab[:, :, :, :], cur[0])

    x_rk = [*th_r, *tl_r, rk_ready, wt_ready]
    XT = [[slot(f"XT{k}{q}", (3, 4, 8, 11)[2 * k + q], [128, 2, 8, 2, SLOTS], F32R) for q in range(2)]
          for k in range(2)]
    GU = [slot(f"GU{k}", 6, [128, 2, 512], F32, 4096 * k) for k in range(2)]
    YH = [slot(f"YH{k}", 5, [128, 512], F32R, 4096 * k) for k in range(2)]
    YL = [slot(f"YL{k}", 5, [128, 512], F32R, 4096 * k + 2048) for k in range(2)]
    HF = [slot(f"HF{k}", 1, [128, 256], F32, 1024 * k) for k in range(2)]
    HS = [slot(f"HS{k}", 1, [128, 4, 2, SLOTS], F32R, 2048 + 2048 * k) for k in range(2)]
    PP = [slot(f"PP{k}", 10, [128, 2, 4, 2, SLOTS], F32R, 4096 * k) for k in range(2)]
    PT = [slot(f"PT{k}", 12, [128, 256], F32R, 1024 * k) for k in range(4)]
    wsl = small("wsl", [128, 4])
    pool_of_banks[0] = [0, 1, 2, 3]
    acc = [4, 5, 6, 7]
    h2_done = [*tl_r, *th_r, *h2T_ready]
    fr = {("PP", k): [*h2_done, *x_ready] for k in range(2)}
    fr.update({("PT", k): list(h2_done) for k in range(4)})
    fr.update({("XT", k): [router_mm, *h2T_ready, *x_ready] for k in range(2)})
    fr.update({("GU", k): [mixes_done] for k in range(2)})
    fr.update({("Y", k): [mixes_done] for k in range(2)})
    fr.update({("H", k): [mixes_done] for k in range(2)})
    fr.update({("wsl", k): [] for k in range(4)})
    io4 = C("iota64").unsqueeze(1).unsqueeze(1).broadcast_to([128, 4, 2, SLOTS])

    def blocks(n, rk, wt, after, first, last_of_all, base):
        ready = {}

        def one_hots(p):
            k = p % 2
            s = []
            for t in range(2):
                src = rk(t, 4 * p, 4).unsqueeze(2).unsqueeze(3).broadcast_to([128, 4, 2, SLOTS])
                s.append(dve(lambda e, t=t, k=k, src=src: e.tensor_tensor(PP[k][:, t, :, :, :], io4, src,
                                                                          ALU.is_equal), after, fr["PP", k]))
            ready["P", p] = s

        def gather(p, c):
            k = p % 2
            b = take()
            dst = bank[b][:, :].rearrange("p (x h s) -> p x h s", x=4, h=2)
            for hl_, src in ((0, th), (1, tl)):
                for t in range(2):
                    m = pe(lambda e: e.matmul(
                        dst[:, :, hl_, :], src[:, t, 128 * c:128 * c + 128], PP[k][:, t, :, 0, :],
                        start=(t == 0), stop=(t == 1)), ready["P", p], x_rk, freed[b])
            fs = []
            for q in range(2):
                v = dst[:, 2 * q:2 * q + 2, :, :]
                o = XT[k][q][:, :, c, :, :]
                if c % 2:
                    fs.append(act(lambda e: e.activation(o, v, ACT.Copy), m, fr["XT", k]))
                else:
                    fs.append(dve(lambda e: e.tensor_copy(o, v), m, fr["XT", k]))
            freed[b] = fs
            ready.setdefault(("X", p), []).append(fs)

        def turn_p(j):
            k = j // 4 % 2
            b = take()
            Pm = [PP[k][:, t, j % 4, :, :].rearrange("p d s -> p (d s)").bitcast(F32) for t in range(2)]
            for t in range(2):
                pe(lambda e: e.transpose(bank[b][:, 128 * t:128 * t + 128], Pm[t], C("ident")),
                   ready["P", j // 4], freed[b])
            for t in range(2):
                m = pe(lambda e, w=wt(t, j): e.matmul(bank[b][:, 256:257], Pm[t], w, start=(t == 0), stop=(t == 1)),
                       after, x_rk)
            q = j % 4
            s1 = act(lambda e: e.activation(PT[q][:, :], bank[b][:, 0:256], ACT.Copy), m, fr["PT", q])
            s2 = act(lambda e: e.activation(wsl[:, q:q + 1], bank[b][:, 256:257], ACT.Copy), m, fr["wsl", q])
            freed[b] = [s1, s2]
            ready["T", j] = [s1]
            ready["w", j] = [s2]
            if j % 4 == 3:
                fr["PP", k] = [m]

        def gate_up(j, w, hf):
            k = j % 2
            if hf == 0:
                ready["b", w] = take()
            b = ready["b", w]
            half = next_half()
            for c in range(4):
                q = 4 * hf + c
                a = XT[j // 4 % 2][j % 4 // 2][:, j % 2, q, :, :].rearrange("p h s -> p (h s)")
                m = times(bank[b][:, :], a, half, slice(512 * c, 512 * c + 512), q == 0, q == 7,
                          ready["X", j // 4], freed[b])
            if hf == 1:
                e_ = act(lambda e: e.activation(GU[k][:, w, :], bank[b][:, :], ACT.Copy), m, fr["GU", k])
                freed[b] = [e_]
                ready["GU", j, w] = e_
            half_done(half[0], half[1], m)
            if w == 1 and hf == 1 and j % 4 == 3:
                fr["XT", j // 4 % 2] = [m]

        def hidden(j):
            k = j % 2
            b = take()
            for w in range(2):
                for f in range(4):
                    m = pe(lambda e: e.matmul(
                        bank[b][:, 256 * w + 64 * f:256 * w + 64 * f + 64], GU[k][:, w, 128 * f:128 * f + 128],
                        C("ident2"), start=True, stop=True), ready["GU", j, w], freed[b])
            fr["GU", k] = [m]
            s1 = act(lambda e: e.activation(HF[k][:, :], bank[b][:, 0:256], ACT.Silu), m, fr["H", k])
            s2 = dve(lambda e: e.tensor_tensor(HF[k][:, :], HF[k][:, :], bank[b][:, 256:512], ALU.mult), s1)
            freed[b] = [s2]
            v = HF[k][:, :].rearrange("p (f s) -> p f s", f=4)
            s3 = act(lambda e: e.activation(HS[k][:, :, 0, :], v, ACT.Copy), s2, fr["H", k])
            s4 = dve(lambda e: e.tensor_tensor(HS[k][:, :, 1, :], v, HS[k][:, :, 0, :].bitcast(F32),
                                               ALU.subtract), s3)
            ready["H", j] = [s3, s4]

        def down(j, hf):
            k = j % 2
            if hf == 0:
                ready["b", 2] = take(2)
            b = ready["b", 2]
            half = next_half()
            for c in range(2):
                f = 2 * hf + c
                a = HS[k][:, f, :, :].rearrange("p h s -> p (h s)")
                for n in range(2):
                    o = slice(1024 * c + 512 * n, 1024 * c + 512 * n + 512)
                    m = times(bank[b[n]][:, :], a, half, o, f == 0, f == 3, ready["H", j], freed[b[n]])
            if hf == 1:
                fr["H", k] = [m]
                q = j % 4
                for n in range(2):
                    s1 = act(lambda e: e.activation(YH[n][:, :], bank[b[n]][:, :], ACT.Copy, scale=wsl[:, q:q + 1]),
                             m, fr["Y", n], ready["w", j])
                    s2 = dve(lambda e: e.scalar_tensor_tensor(
                        out=YL[n][:, :], in0=bank[b[n]][:, :], scalar=wsl[:, q:q + 1],
                        in1=YH[n][:, :].bitcast(F32), op0=ALU.mult, op1=ALU.subtract), s1, fr["Y", n])
                    freed[b[n]] = [s2]
                    ready["Y", j, n] = [s1, s2]
                fr["wsl", q] = [s2]
            half_done(half[0], half[1], m)

        def combine(j):
            q = j % 4
            for n in range(2):
                for t in range(2):
                    o = bank[acc[2 * t + n]][:, :]
                    a = PT[q][:, 128 * t:128 * t + 128]
                    i0 = first and j == 0
                    i1 = j == n_blocks - 1
                    m0 = [] if not i0 else freed[acc[2 * t + n]]
                    pe(lambda e: e.matmul(o, a, YH[n][:, :], start=i0, stop=False, skip_group_check=True),
                       ready["Y", j, n], ready["T", j], m0)
                    m = pe(lambda e: e.matmul(o, a, YL[n][:, :], start=False, stop=i1, skip_group_check=True))
                fr["Y", n] = [m]
            fr["PT", q] = [m]

        n_blocks = n
        one_hots(0)
        for c in range(8):
            gather(0, c)
        for j in range(n + 2):
            p, q = j // 4 + 1, j % 4
            if j < n:
                gate_up(j, 0, 0)
            if 0 < j <= n:
                hidden(j - 1)
            if j < n:
                gate_up(j, 0, 1)
            if j > 1:
                combine(j - 2)
            if q == 0 and 4 * p < n:
                one_hots(p)
            if j < n:
                gate_up(j, 1, 0)
                if 4 * p < n:
                    gather(p, 2 * q)
                gate_up(j, 1, 1)
                turn_p(j)
            if 0 < j <= n:
                down(j - 1, 0)
            if j < n and 4 * p < n:
                gather(p, 2 * q + 1)
            if 0 < j <= n:
                down(j - 1, 1)

    blocks(NE, lambda t, j, n: RK[:, t, j:j + n], lambda t, j: WT[:, t, j:j + 1], [rk_ready, wt_ready], True,
           False, 0)

    count = {}
    for e_ in Q.ENGINES:
        put(e_, lambda e: count.update(n=e.value_load(ovf[0:1, 0:1], min_val=0, max_val=NOV - 1)), ov_ready)
    def overflow():
        in_branch[0] = True
        ok = small("ok", [128, 2, NOV])
        ow = small("ow", [128, 2, NOV])
        kb = cnt[:, 4, :].unsqueeze(1).broadcast_to([128, 2, 32])
        cur[0] = dve(lambda e: e.scalar_tensor_tensor(out=T0, in0=kb, scalar=float(SLOTS), in1=RK, op0=ALU.mult,
                                                      op1=ALU.add), ids_step)
        for j in range(NOV):
            chain(lambda e, j=j: e.tensor_scalar(cnt[:, 5, :], cnt[:, 4, :], float(j), None, ALU.is_le))
            chain(lambda e, j=j: e.tensor_scalar(cnt[:, 6, :], cnt[:, 3, :], float(j), None, ALU.is_gt))
            chain(lambda e: e.tensor_tensor(cnt[:, 5, :], cnt[:, 5, :], cnt[:, 6, :], ALU.mult))
            hot = cnt[:, 5, :].unsqueeze(1).broadcast_to([128, 2, 32])
            chain(lambda e, hot=hot: e.tensor_tensor(T1, T0, hot, ALU.mult))
            chain(lambda e, j=j: e.tensor_reduce(ok[:, :, j:j + 1], T1, AX, ALU.add))
            chain(lambda e, j=j: e.tensor_scalar(ok[:, :, j:j + 1], ok[:, :, j:j + 1], float(-SLOTS * (j + 1)), None,
                                                 ALU.add))
            chain(lambda e: e.tensor_reduce(cnt[:, 7, 16:17], cnt[:, 5, :], AX, ALU.add))
            chain(lambda e: e.tensor_scalar(cnt[:, 7, 17:18], cnt[:, 7, 16:17], -FAR, FAR, ALU.mult, ALU.add))
            chain(lambda e, j=j: e.tensor_scalar(ok[:, :, j:j + 1], ok[:, :, j:j + 1], cnt[:, 7, 17:18], None,
                                                 ALU.add))
            chain(lambda e, hot=hot: e.tensor_tensor(T1, WT, hot, ALU.mult))
            chain(lambda e, j=j: e.tensor_reduce(ow[:, :, j:j + 1], T1, AX, ALU.add))
        ov_tab = cur[0]
        for _ in range(RAW):
            feed()
        for _ in range(RING):
            split_ahead()
        blocks(NOV, lambda t, j, n: ok[:, t, j:j + n], lambda t, j: ow[:, t, j:j + 1], [ov_tab], False, True, 0)

    known = dict(Q.seen)
    if Q.who:
        with Q.eng.If(count["n"] > 0):
            overflow()
    else:
        overflow()
    Q.seen = known

    Q.era = 1
    all_done = pe(lambda e: e.drain())
    ysc = slot("ysc", 3, [128, 2, 1024])
    xr = []
    for t in range(2):
        for n in range(2):
            o = slice(512 * n, 512 * n + 512)
            s = dve(lambda e, t=t, n=n, o=o: e.tensor_tensor(ysc[:, t, o], bank[acc[2 * t + n]][:, :],
                                                             gate2b[:, o], ALU.mult), all_done, ada_done[10],
                    ada_done[11])
            xr.append(dve(lambda e, t=t, o=o: e.tensor_tensor(x[:, t, o], x[:, t, o], ysc[:, t, o], ALU.add), s))
    fin = slot("fin", 4, [128, 2, 1024])
    s_out = sem("s_out")
    for t in range(2):
        k = 8 * t
        sq = act(lambda e, t=t, k=k: e.activation(fin[:, t, :], x[:, t, :], ACT.Square, accum_out=stat(k)), xr)
        a = dve(lambda e, k=k: e.tensor_scalar(stat(k + 1), stat(k), 1.0 / D, EPS, ALU.mult, ALU.add), sq)
        a = act(lambda e, k=k: e.activation(stat(k + 2), stat(k + 1), ACT.Sqrt), a)
        a = dve(lambda e, k=k: e.reciprocal(stat(k + 3), stat(k + 2)), a)
        a = dve(lambda e, t=t, k=k: e.scalar_tensor_tensor(out=fin[:, t, :], in0=x[:, t, :], scalar=stat(k + 3),
                                                           in1=gfb[:, :], op0=ALU.mult, op1=ALU.mult), a, l_gfb)
        put("sp", lambda e, t=t: e.dma_start(out[0, 128 * t:128 * t + 128, :], fin[:, t, :]).then_inc(s_out, 16),
            a)
    put("sp", lambda e: e.wait_ge(s_out, 32))


def build_two_blocks(nc, A, out):
    kept, named = {}, set()
    program(nc, A, out, kept, Queues(None, None, named, {}))
    with nc.Block() as block:
        block.sync(lambda eng: program(nc, A, out, kept, Queues("sp", eng, named, {})))
        block.scalar(lambda eng: program(nc, A, out, kept, Queues("act", eng, named, {})))
        block.gpsimd(lambda eng: program(nc, A, out, kept, Queues("pool", eng, named, {})))
        block.vector(lambda eng: program(nc, A, out, kept, Queues("dve", eng, named, {})))
        block.tensor(lambda eng: program(nc, A, out, kept, Queues("pe", eng, named, {})))


def constants():
    c = np.zeros((128, NCST), np.float32)
    i = np.arange(128)
    c[:, CST["ident"]:CST["ident"] + 128] = np.eye(128)
    c[:, CST["ident2"]:CST["ident2"] + 64] = (i[:, None] % 64 == np.arange(64)[None])
    c[:, CST["lt"]:CST["lt"] + 128] = i[:, None] < i[None]
    c[:, CST["pen_ts"]:CST["pen_ts"] + 128] = np.where(i[None] > i[:, None], -BIG, 0.0)
    c[:, CST["pen_st"]:CST["pen_st"] + 128] = np.where(i[:, None] > i[None], BIG, 0.0)
    c[:, CST["iota64"]:CST["iota64"] + 64] = np.arange(64)[None]
    c[:, CST["iota32"]:CST["iota32"] + 32] = np.arange(32)[None]
    c[:, CST["ones"]:CST["ones"] + 128] = 1.0
    return c


_PACKED = ("norm_mix_g", "norm_ff_g", "g_norm1_2", "b_s", "conv_w", "w_conv_2", "b_conv_2", "c_2", "b_gates_2", "w_s")
_NAMES = ("x", "w_in", "b_gate", "norm_v_g", "w_proj_a", "w_proj_b", "w_out", "w_ff1", "w_ff2", "norm_final_g",
          "w_ada_2", "b_ada_2", "w_in_2", "g_mlstm_head_2", "w_out_2", "g_norm2_2", "w_router_group_2",
          "b_router_group_2", "w_router_expert_2", "b_router_expert_2", "w_expert_gate_2", "w_expert_up_2",
          "w_expert_down_2", "g_final_2")


def lay_out(inputs):
    def by_part(a):
        return np.ascontiguousarray(np.asarray(a).reshape(-1, 8, 128).transpose(2, 0, 1).reshape(128, -1))

    i = {k: np.asarray(v) for k, v in inputs.items()}
    bg = np.zeros((128, 2), np.float32)
    bg[0:4, 0] = i["b_gates_2"][0, 0:4]
    bg[32:36, 1] = i["b_gates_2"][0, 4:8]
    vecs = np.concatenate([by_part(i["norm_mix_g"]), by_part(i["norm_final_g"]), by_part(i["norm_ff_g"]), by_part(i["g_norm1_2"]),
                           i["b_s"][0].T, by_part(i["conv_w"]), by_part(i["w_conv_2"]), by_part(i["b_conv_2"]),
                           by_part(i["c_2"]), bg], axis=1)
    arrays = {k: np.ascontiguousarray(i[k]) for k in _NAMES}
    arrays["norm_final_g"] = arrays["norm_final_g"].reshape(1, -1)
    arrays["g_final_2"] = arrays["g_final_2"].reshape(1, -1)
    arrays["vecs"] = np.ascontiguousarray(vecs)
    arrays["w_sT"] = np.ascontiguousarray(i["w_s"][0].transpose(2, 0, 1))
    arrays["cst"] = constants()
    return arrays


def make(nc, arrays):
    A = {k: nc.dram_tensor(f"in_{k}", a.shape, F32, kind="ExternalInput").ap() for k, a in arrays.items()}
    out = nc.dram_tensor("out_0", (1, 256, 1024), F32, kind="ExternalOutput").ap()
    return A, out


def kernel(**inputs):
    import concourse.bacc as _bacc
    from concourse.bass_utils import run_bass_kernel_spmd as _run

    nc = _bacc.Bacc("TRN2", target_bir_lowering=False, num_devices=1)
    arrays = lay_out(inputs)
    A, out = make(nc, arrays)
    build_two_blocks(nc, A, out)
    r = _run(nc, [{f"in_{k}": a for k, a in arrays.items()}], core_ids=[0])
    return r.results[0]["out_0"]
```

```python
import numpy as np

import concourse.bass as bass
from concourse import mybir

DT = mybir.dt
F32 = DT.float32
F32R = DT.float32r
I32 = DT.int32
ACT = mybir.ActivationFunctionType
ALU = mybir.AluOpType
AX = mybir.AxisListType.X

EPS = 1e-6
D = 1024
BIG = 1.0e30
FAR = 4096.0
NE = 32
SLOTS = 64
NOV = 8
RAW = 6
RING = 3
ADA_AGE = 1

VEC = {}
_at = 0
for _n, _w in (("g_mix", 8), ("g_nf", 8), ("g2", 8), ("g_ff", 8), ("g1", 8), ("b_s", 8), ("conv", 24), ("conv2", 32), ("bconv2", 8),
               ("c", 8), ("bg", 2)):
    VEC[_n] = _at
    _at += _w
NVEC = _at
CST = {}
_at = 0
for _n, _w in (("ident", 128), ("ident2", 64), ("lt", 128), ("pen_ts", 128), ("pen_st", 128), ("iota64", 64),
               ("iota32", 32), ("ones", 128)):
    CST[_n] = _at
    _at += _w
NCST = _at


class Step:

    def __init__(self, n):
        self.n = n
        self.sem = self.value = None


class Load:

    def __init__(self, sem, value):
        self.sem, self.value = sem, value


class Queues:

    ENGINES = ("pe", "act", "dve", "pool", "sp")

    def __init__(self, who, eng, named, sems):
        self.who, self.eng, self.named, self.sems = who, eng, named, sems
        self.era = 0
        self.n = 0
        self.value = {}
        self.last = {}
        self.seen = {}

    def put(self, engine, fn, *after):
        flat, open_ = [], list(after)
        while open_:
            a = open_.pop(0)
            if isinstance(a, (list, tuple)):
                open_ += a
            elif a is not None:
                flat.append(a)
        s = Step(self.n)
        self.n += 1
        self.last[engine] = s
        if self.who is None:
            self.named.update(a.n for a in flat if isinstance(a, Step))
            return s
        if s.n in self.named:
            key = engine, self.era
            self.value[key] = self.value.get(key, 0) + 1
            s.sem, s.value = self.sems[key], self.value[key]
        if engine == self.who:
            for a in flat:
                if self.seen.get(a.sem.name, 0) < a.value:
                    self.eng.wait_ge(a.sem, a.value)
                    self.seen[a.sem.name] = a.value
            ins = fn(self.eng)
            if s.value is not None:
                ins.then_inc(s.sem, 1)
        return s


def program(nc, A, out, kept, Q):
    base = 16512
    offs = {"raw": base, "hi": base + RAW * 8192, "lo": base + (RAW + RING) * 8192,
            "slot": base + (RAW + 2 * RING) * 8192}
    rest = [offs["slot"] + 13 * 8192]

    def at(name, shape, dt, off):
        if name not in kept:
            kept[name] = nc.alloc_sbuf_tensor_at(name, shape, dt, offset=off)
        return kept[name]

    def slot(name, k, shape, dt=F32, off=0):
        n = int(np.prod(shape[1:])) * 4
        assert off + n <= 8192, name
        return at(name, shape, dt, offs["slot"] + 8192 * k + off)

    def small(name, shape, dt=F32):
        n = (int(np.prod(shape[1:])) * 4 + 31) // 32 * 32
        t = at(name, shape, dt, rest[0])
        rest[0] += n
        assert rest[0] <= 229360, name
        return t

    def sem(name):
        if name not in kept:
            kept[name] = nc.alloc_semaphore(name)
        return kept[name]

    put = Q.put
    for e in Q.ENGINES:
        for era in (0, 1):
            Q.sems[e, era] = sem(f"s_{e}{era}")

    def pe(fn, *a):
        return put("pe", fn, *a)

    def act(fn, *a):
        return put("act", fn, *a)

    def dve(fn, *a):
        return put("dve", fn, *a)

    def pool(fn, *a):
        return put("pool", fn, *a)

    def load(name, dst, src, *after, eng="act"):
        s = sem(f"l_{name}")
        put(eng, lambda e: e.dma_start(dst, src).then_inc(s, 16), *after)
        return Load(s, 16)

    cst = small("cst", [128, NCST])
    vec = small("vec", [128, NVEC])
    st = small("st", [128, 128])
    tab = small("tab", [128, 6, 2, 32])
    ovf = small("ovf", [128, 32], I32)

    def C(n, lo=0, hi=None, rows=slice(0, 128)):
        a = CST[n]
        w = {"ident": 128, "ident2": 64, "lt": 128, "pen_ts": 128, "pen_st": 128, "iota64": 64, "iota32": 32,
             "ones": 128}[n]
        return cst[rows, a + lo:a + (w if hi is None else hi)]

    def V(n, k, rows=slice(0, 128)):
        return vec[rows, VEC[n] + k:VEC[n] + k + 1]

    x = slot("x", 0, [128, 2, 1024])
    l_cst = load("cst", cst[:, :], A["cst"], eng="sp")
    l_x = [load(f"x{t}", x[:, t, :], A["x"][0, 128 * t:128 * t + 128, :], eng="sp") for t in range(2)]
    l_vec = load("vec", vec[:, :], A["vecs"], eng="sp")

    if "banks" not in kept:
        kept["banks"] = [nc.alloc_psum_tensor(f"bank{i}", [128, 512], F32) for i in range(8)]
    bank = kept["banks"]
    freed = [[] for _ in range(8)]
    turn = [0]
    opened = set()
    pool_of_banks = [list(range(8))]

    def take(n=1):
        got = []
        while len(got) < n:
            k = pool_of_banks[0][turn[0] % len(pool_of_banks[0])]
            turn[0] += 1
            if k not in opened:
                got.append(k)
        return got if n > 1 else got[0]

    raw = [at(f"raw{i}", [128, 2048], F32, offs["raw"] + 8192 * i) for i in range(RAW)]
    whi = [at(f"whi{i}", [128, 2048], F32R, offs["hi"] + 8192 * i) for i in range(RING)]
    wlo = [at(f"wlo{i}", [128, 2048], F32R, offs["lo"] + 8192 * i) for i in range(RING)]
    raw_sem = [sem(f"s_raw{i}") for i in range(RAW)]

    halves = []

    def cols(w, r0, c0):
        return ("mm", lambda: w[r0:r0 + 512, c0:c0 + 512].rearrange("(c p) n -> p c n", p=128), 4)

    def rows(w, r0):
        return ("mm", lambda: w[r0:r0 + 256, :].rearrange("(c p) n -> p c n", p=128), 2)

    def group(w, c0):
        return [cols(w, 0, c0), cols(w, 512, c0)]

    w_in, w_in2 = A["w_in"][0], A["w_in_2"][0]
    ada_at = []

    def ada():
        g, k = divmod(len(ada_at), 2)
        if g < 12:
            ada_at.append(len(halves))
            halves.append(("ada", cols(A["w_ada_2"][0], 512 * k, 512 * g)[1], (g, k)))

    for n, g in enumerate((2, 3, 0, 1, 6, 7, 8, 9, 4, 5, 10, 11, 12, 13)):
        pair = group(w_in, 512 * g)
        halves += pair[:1]
        if n > 3 and n not in (8, 9, 10):
            ada()
        halves += pair[1:]
    for w in (A["w_proj_a"][0], A["w_proj_b"][0], A["w_out"][0]):
        for c0 in (0, 512):
            pair = group(w, c0)
            halves += pair[:1]
            if w is not A["w_out"][0]:
                ada()
            halves += pair[1:]
    for g in range(9):
        if g < 8:
            halves += group(A["w_ff1"][0], 512 * g)
            ada()
        if g > 0:
            halves.append(rows(A["w_ff2"][0], 512 * (g - 1)))
            if g < 6:
                ada()
            halves.append(rows(A["w_ff2"][0], 512 * (g - 1) + 256))
    QK, VM, OM, GT, QA, KA, VA = 0, 1024, 1536, 2048, 2056, 2568, 3080
    for c0 in (QK, QK + 512, QA, KA, VA, VM, OM):
        halves += group(w_in2, c0)
    halves += [cols(A["w_out_2"][0], r0, c0) for r0 in (512, 0) for c0 in (0, 512)]

    def expert(e, what):
        if what == "d":
            w = A["w_expert_down_2"][0, e]
            first = rows(w, 0)
            return [first if e >= NE - 3 else ("whole", *first[1:]), rows(w, 256)]
        return group(A["w_expert_gate_2" if what == "g" else "w_expert_up_2"][0, e], 0)

    for e in range(NE + 1):
        if e < NE:
            halves += expert(e, "g") + expert(e, "u")
        if e > 0:
            halves += expert(e - 1, "d")
    n_static = len(halves)

    def moving(name, j, r0, n_rows, chunks):
        w = A[name]

        def src(e):
            v = e.value_load(ovf[0:1, 8 + j:9 + j], min_val=0, max_val=NE - 1)
            return w[0, bass.ds(v, 1), r0:r0 + n_rows, :].rearrange("a (c p) n -> p (a c) n", p=128)
        return ("mm", src, chunks)

    for j in range(NOV + 1):
        if j < NOV:
            for n in ("w_expert_gate_2", "w_expert_up_2"):
                halves += [moving(n, j, 0, 512, 4), moving(n, j, 512, 512, 4)]
        if j > 0:
            halves += [moving("w_expert_down_2", j - 1, 0, 256, 2), moving("w_expert_down_2", j - 1, 256, 256, 2)]

    n_loaded = [0]
    read = {}
    loads = {}
    in_branch = [False]
    ids_ready = []

    def feed():
        while n_loaded[0] < (len(halves) if in_branch[0] else n_static):
            i = n_loaded[0]
            if i >= RAW and i - RAW not in read:
                return
            n_loaded[0] += 1
            kind, src, k = halves[i]
            r = i % RAW
            dst = raw[r][:, :].rearrange("p (c n) -> p c n", c=4 if kind == "ada" else k)
            if i >= n_static:
                put("sp", lambda e: e.dma_start(dst, src(e)).then_inc(raw_sem[r], 16), read[i - RAW], ids_ready)
            else:
                put("sp", lambda e: e.dma_start(dst, src()).then_inc(raw_sem[r], 16), read.get(i - RAW))
            loads[i] = Load(raw_sem[r], 16 * (i // RAW + 1))

    feed()

    n_split = [0]
    n_mm = [0]
    parts = {}
    parts_free = [[] for _ in range(RING)]
    used = [0]

    def split_ahead():
        while n_split[0] < n_loaded[0]:
            i = n_split[0]
            kind, _, info = halves[i]
            r = i % RAW
            n_split[0] += 1
            if kind == "ada":
                ada_half(i, *info)
                feed()
            elif kind == "mm":
                s = n_mm[0] % RING
                n_mm[0] += 1
                h = act(lambda e: e.activation(whi[s][:, :], raw[r][:, :], ACT.Copy), loads[i], parts_free[s])
                lo = dve(lambda e: e.tensor_tensor(wlo[s][:, :], raw[r][:, :], whi[s][:, :].bitcast(F32),
                                                   ALU.subtract), h, parts_free[s])
                parts[i] = (s, h, lo)
                read[i] = [lo]
                feed()
                return

    def next_half(first=True):
        if first:
            flush()
        i = used[0]
        while halves[i][0] == "ada":
            i += 1
        used[0] = i + 1
        if halves[i][0] == "whole":
            return i, i % RAW, loads[i], None
        return i, *parts.pop(i)

    owed = [0]

    def flush():
        while owed[0]:
            owed[0] -= 1
            split_ahead()

    def half_done(i, s, step, later=False):
        if halves[i][0] == "whole":
            read[i] = [step]
            feed()
        else:
            parts_free[s] = [step]
            owed[0] += 1
            if not later:
                flush()

    def times(o, a, half, c, start, stop, *after):
        _, s, ready, lo = half
        if lo is None:
            return pe(lambda e: e.matmul(o, a.bitcast(F32), raw[s][:, c], start=start, stop=stop), ready, *after)
        pe(lambda e: e.matmul(o, a, whi[s][:, c], start=start, stop=False), ready, *after)
        return pe(lambda e: e.matmul(o, a, wlo[s][:, c], start=False, stop=stop), lo)

    sc = small("silu_c", [128, 8])
    ada_acc = [slot(f"ada_acc{k}", 10, [128, 512], F32, 2048 * k) for k in range(2)]
    ada_free = [[], []]
    ada_done = {}
    gate1b, scale2b = slot("gate1b", 11, [128, 1024]), slot("scale2b", 11, [128, 1024], F32, 4096)
    shift2b, gate2b = slot("shift2b", 12, [128, 1024]), slot("gate2b", 12, [128, 1024], F32, 4096)
    ada_cols = small("ada_cols", [128, 32])
    ada_tasks = []
    ada_cell = {}
    bada = [[sem(f"l_bada{k}"), 0] for k in range(2)]
    silu_c = act(lambda e: e.activation(sc[:, :], vec[:, VEC["c"]:VEC["c"] + 8], ACT.Silu), l_vec)

    def ada_half(i, g, k):
        acc = ada_acc[g % 2]
        r = i % RAW
        if k == 0:
            if any(t[0] % 2 == g % 2 for t in ada_tasks):
                ada_finish()
            z = pool(lambda e: e.memset(acc[:, :], 0.0), ada_free[g % 2])
            row = A["b_ada_2"][0:1, 512 * g:512 * g + 512]
            s = bada[g % 2]
            s[1] += 16
            put("pool", lambda e: e.dma_start(acc[0:1, :], row).then_inc(s[0], 16), z)
            ada_cell["b", g] = Load(s[0], s[1])
        last = ada_cell.get(("last", g))
        for c in range(4):
            last = dve(lambda e, c=c: e.scalar_tensor_tensor(
                out=acc[:, :], in0=raw[r][:, 512 * c:512 * c + 512], scalar=sc[:, 4 * k + c:4 * k + c + 1],
                in1=acc[:, :], op0=ALU.mult, op1=ALU.add), loads[i], silu_c, ada_cell["b", g], last)
        read[i] = [last]
        ada_cell["last", g] = last
        if k == 1:
            ada_tasks.append((g, last))

    ada_age = []

    def ada_finish(now=True):
        while len(ada_age) < len(ada_tasks):
            ada_age.append(0)
        ada_age[:] = [n + 1 for n in ada_age]
        while ada_tasks and (now or ada_age[0] > ADA_AGE):
            ada_age.pop(0)
            g, ready = ada_tasks.pop(0)
            acc = ada_acc[g % 2]
            ev = []
            if g < 4 or 6 <= g < 10:
                b = take()
                for c in range(4):
                    m = pe(lambda e: e.matmul(bank[b][:, c:c + 1], acc[:, 128 * c:128 * c + 128],
                                              C("ones", 0, 1), start=True, stop=True), ready, freed[b], l_cst)
                o = 4 * g if g < 4 else 4 * g - 8
                ev.append(act(lambda e: e.activation(ada_cols[:, o:o + 4], bank[b][:, 0:4], ACT.Copy), m))
                freed[b] = ev[-1:]
            if g >= 4:
                b = take()
                t = [gate1b, shift2b, scale2b, gate2b][g // 2 - 2]
                m = pe(lambda e: e.matmul(bank[b][:, :], C("ones"), acc[:, :], start=True, stop=True),
                       ready, freed[b], l_cst)
                ev.append(act(lambda e: e.activation(t[:, 512 * (g % 2):512 * (g % 2) + 512], bank[b][:, :],
                                                     ACT.Copy), m))
                freed[b] = ev[-1:]
            ada_free[g % 2] = [m]
            ada_done[g] = ev

    def dense(xh, xl, x_ready, mid=None, hold=False):
        b = take(2)
        opened.update(b)
        for hf in range(2):
            half = next_half()
            last = dense_half(xh, xl, x_ready, b, half, hf, hf == 0, hf == 1)
            if hf == 0 and mid:
                mid()
            half_done(half[0], half[1], last, hf == 1)
            if hf == 0:
                ada_finish(False)
        if not hold:
            opened.difference_update(b)
        return b, last

    def dense_turned(xh, xl, x_ready, mid=None):
        b = take(2)
        opened.update(b)
        for hf in range(2):
            half = next_half()
            _, s, h, lo = half
            for c in range(4):
                k = 4 * hf + c
                xr = x_ready[k // 2] if isinstance(x_ready, dict) else x_ready
                for n in range(4):
                    o = bank[b[n // 2]][:, 256 * (n % 2):256 * (n % 2) + 256]
                    w_h = whi[s][:, 512 * c + 128 * n:512 * c + 128 * n + 128]
                    w_l = wlo[s][:, 512 * c + 128 * n:512 * c + 128 * n + 128]
                    first, end = k == 0 and n % 2 == 0, k == 7
                    pe(lambda e: e.matmul(o, w_h, xh[:, k, :], start=first, stop=False, skip_group_check=True),
                       h, xr, freed[b[n // 2]] if first else None)
                    pe(lambda e: e.matmul(o, w_h, xl[:, k, :], start=False, stop=False, skip_group_check=True))
                    last = pe(lambda e: e.matmul(o, w_l, xh[:, k, :], start=False, stop=end,
                                                 skip_group_check=True), lo)
            if hf == 0 and mid:
                mid()
            half_done(half[0], half[1], last, hf == 1)
            if hf == 0:
                ada_finish(False)
        opened.difference_update(b)
        return b, last

    def dense_half(xh, xl, x_ready, b, half, hf, first, end):
        _, s, h, lo = half
        for c in range(4):
            k = 4 * hf + c
            for t in range(2):
                o = bank[b[t]][:, :]
                a_h, a_l = xh[:, k, 128 * t:128 * t + 128], xl[:, k, 128 * t:128 * t + 128]
                r_h, r_l = whi[s][:, 512 * c:512 * c + 512], wlo[s][:, 512 * c:512 * c + 512]
                xr = x_ready[k // 2] if isinstance(x_ready, dict) else x_ready
                pe(lambda e: e.matmul(o, a_h, r_h, start=first and c == 0, stop=False),
                   h, xr, freed[b[t]] if first and c == 0 else None)
                pe(lambda e: e.matmul(o, a_h, r_l, start=False, stop=False), lo)
                last = pe(lambda e: e.matmul(o, a_l, r_h, start=False, stop=end and c == 3))
        return last

    def stat(k, n=1):
        return st[:, k:k + n]

    def squares(src, k, junk, after):
        return act(lambda e: e.activation(junk, src, ACT.Square, accum_out=stat(k)), after)

    def inv_rms(k, n, ready, w=2):
        a = dve(lambda e: e.tensor_scalar(stat(k, w), stat(k, w), 1.0 / n, EPS, ALU.mult, ALU.add), ready)
        b = act(lambda e: e.activation(stat(k, w), stat(k, w), ACT.Sqrt), a)
        return dve(lambda e: e.reciprocal(stat(k, w), stat(k, w)), b)

    def turned(src, pairs, ready, use):
        outs = []
        for k in pairs:
            b = take()
            for c in range(2):
                for t in range(2):
                    piece = src(t, 2 * k + c)
                    m = pe(lambda e: e.transpose(
                        bank[b][:, 256 * c + 128 * t:256 * c + 128 * t + 128], piece, C("ident")), ready, freed[b], l_cst)
            r = use(k, bank[b], m)
            freed[b] = list(r)
            outs += list(r)
        return outs

    def piece_of(t_):
        return lambda t, c: t_[:, t, 128 * c:128 * c + 128]

    def hi_lo(dh, dl, after=None):
        def use(k, b, m):
            o = slice(2 * k, 2 * k + 2)
            src = b[:, :].rearrange("p (c t) -> p c t", c=2)
            h = act(lambda e: e.activation(dh[:, o, :], src, ACT.Copy), m, after)
            lo = dve(lambda e: e.tensor_tensor(dl[:, o, :], src, dh[:, o, :].bitcast(F32), ALU.subtract), h, after)
            return h, lo
        return use

    def hi_lo_scaled(dh, dl, name, after=None):
        def use(k, b, m):
            out = []
            for c in range(2):
                ch = 2 * k + c
                s = b[:, 256 * c:256 * c + 256]
                h = act(lambda e, s=s, ch=ch: e.activation(dh[:, ch, :], s, ACT.Copy, scale=V(name, ch)),
                        m, after, l_vec)
            for c in range(2):
                ch = 2 * k + c
                s = b[:, 256 * c:256 * c + 256]
                out.append(dve(lambda e, s=s, ch=ch: e.scalar_tensor_tensor(
                    out=dl[:, ch, :], in0=s, scalar=V(name, ch), in1=dh[:, ch, :].bitcast(F32),
                    op0=ALU.mult, op1=ALU.subtract), h, after))
                out.append(h)
            return out
        return use

    dbg = A.get("_dbg")
    n_dbg = [0]

    def dump(name, ap, ready):
        if dbg is not None and name in dbg:
            d = load(f"dbg_{name}", dbg[name], ap, ready, eng="sp")
            for q in Q.ENGINES:
                put(q, lambda e: None, d)

    hh = slot("hh", 1, [128, 8, 256], F32R)
    hl = slot("hl", 2, [128, 8, 256], F32R)
    ws = slot("ws", 8, [128, 8, 128])
    gvb = slot("gvb", 8, [128, 1024], F32, 4096)
    junk3 = slot("junk3", 3, [128, 2, 1024])
    z_ws = dve(lambda e: e.memset(ws[64:128, :, 0:64], 0.0))
    h_ready = {}
    for k in range(4):
        h_ready[k] = turned(piece_of(x), [k], l_x, hi_lo_scaled(hh, hl, "g_mix"))
        if k == 1:
            split_ahead()
    for _ in range(RING - 1):
        split_ahead()
    l_ws0 = load("ws0", ws[0:64, :, :], A["w_sT"][0:64], loads[1], eng="pool")
    l_ws1 = load("ws1", ws[64:128, :, 64:128], A["w_sT"][64:128, :, 64:128], loads[1], eng="pool")
    l_gvb = load("gvb", gvb[:, :], A["norm_v_g"].broadcast_to([128, 1024]), loads[2], eng="pool")
    bgb = slot("bgb", 9, [128, 2048])
    l_bgb = load("bgb", bgb[:, :], A["b_gate"].broadcast_to([128, 2048]), loads[4], eng="pool")
    nfb = slot("nfb", 10, [128, 1024], F32, 4096)
    l_nfb = load("nfb", nfb[:, :], A["norm_final_g"].broadcast_to([128, 1024]), loads[5], eng="pool")

    def more_h():
        r1.append(inv_rms(0, D, [squares(x[:, t, :], t, junk3[:, t, :], l_x[t]) for t in range(2)]))

    r1 = []

    vt = slot("vt", 3, [128, 2, 1024])
    ut = slot("ut", 4, [128, 2, 1024])

    def into(dst, fn, after, mids=(None, None), first=None):
        out = []
        for g in range(2):
            b, m = first if first and g == 0 else dense(hh, hl, h_ready, mids[g])
            for t in range(2):
                s = act(lambda e: e.activation(dst[:, t, 512 * g:512 * g + 512], bank[b[t]][:, :], fn,
                                               scale=stat(t)), m, r1, after)
                freed[b[t]] = [s]
                opened.discard(b[t])
                out.append(s)
        return out

    v_ready = into(vt, ACT.Gelu, None, (more_h, None))
    junk5 = slot("junk5", 5, [128, 2, 1024])
    vjunk = slot("vjunk", 4, [128, 1024])
    vs = []

    def norm_v():
        r = inv_rms(8, D, [squares(vt[:, t, :], 8 + t, junk5[:, t, :], v_ready) for t in range(2)])
        for t in range(2):
            vs.append(dve(lambda e: e.scalar_tensor_tensor(
                out=vt[:, t, :], in0=vt[:, t, :], scalar=stat(8 + t), in1=gvb[:, :], op0=ALU.mult,
                op1=ALU.mult), r, l_gvb))

    u_ready = into(ut, ACT.Gelu, None, (norm_v, None))
    a_steps = []
    mixed = []

    def mix_a(t):
        for q in range(2):
            b = take()
            for g in range(4):
                gg = 4 * q + g
                m = pe(lambda e: e.matmul(bank[b][:, 128 * g:128 * g + 128], ws[:, gg, :],
                                          vt[:, t, 128 * gg:128 * gg + 128], start=True, stop=True),
                       vs, z_ws, l_ws0, l_ws1, freed[b])
            fs = []
            for g in range(4):
                gg = 4 * q + g
                fs.append(dve(lambda e: e.scalar_tensor_tensor(
                    out=ut[:, t, 128 * gg:128 * gg + 128], in0=bank[b][:, 128 * g:128 * g + 128],
                    scalar=V("b_s", gg), in1=ut[:, t, 128 * gg:128 * gg + 128], op0=ALU.add, op1=ALU.mult),
                    m, u_ready, l_vec))
            freed[b] = fs
            mixed.append(m)
            a_steps.extend(fs)

    cgt = slot("cgt", 7, [128, 2, 1024])
    cg = into(cgt, ACT.Copy, None, (lambda: mix_a(0), lambda: mix_a(1)))
    dump("a", ut[:, :, :], a_steps)
    ah = slot("ah", 5, [128, 8, 256], F32R)
    al = slot("al", 6, [128, 8, 256], F32R)
    zt = slot("zt", 3, [128, 2, 1024])
    z_ready = []
    a_ready = []
    for g in range(2):
        b, m = dense(hh, hl, h_ready, lambda: a_ready.extend(
            turned(piece_of(ut), range(2 * g, 2 * g + 2), a_steps, hi_lo(ah, al, vs))))
        for t in range(2):
            s = dve(lambda e: e.scalar_tensor_tensor(
                out=zt[:, t, 512 * g:512 * g + 512], in0=bank[b[t]][:, :], scalar=stat(t),
                in1=cgt[:, t, 512 * g:512 * g + 512], op0=ALU.mult, op1=ALU.mult), m, cg, mixed)
            freed[b[t]] = [s]
            z_ready.append(s)
    zT = slot("zT", 4, [128, 8, 256])

    def plain(dst, after=None):
        def use(k, b, m):
            src = b[:, :].rearrange("p (c t) -> p c t", c=2)
            return [act(lambda e: e.activation(dst[:, 2 * k:2 * k + 2, :], src, ACT.Copy), m, after)]
        return use

    zT_ready = []
    y = slot("y", 7, [128, 8, 256])
    y_ready = []

    def conv(q):
        zT_ready.extend(turned(piece_of(zt), range(2 * q, 2 * q + 2), z_ready, plain(zT, a_ready)))
        for c in range(4 * q, 4 * q + 4):
            s = act(lambda e: e.activation(y[:, c, :], zT[:, c, :], ACT.Copy, scale=V("conv", 16 + c)),
                    zT_ready, z_ready)
            for k, d in ((1, 1), (0, 2)):
                s = dve(lambda e: e.scalar_tensor_tensor(
                    out=y[:, c, d:256], in0=zT[:, c, 0:256 - d], scalar=V("conv", 8 * k + c), in1=y[:, c, d:256],
                    op0=ALU.mult, op1=ALU.add), s)
            y_ready.append(s)

    bt = slot("bt", 3, [128, 2, 1024])
    first_bg = dense(hh, hl, h_ready, lambda: conv(0), hold=True)
    flush()
    conv(1)
    b_ready = into(bt, ACT.Copy, zT_ready, first=first_bg)
    ga = slot("ga", 3, [128, 2, 1024])
    ch = slot("ch", 8, [128, 8, 256], F32R)
    cl = slot("cl", 4, [128, 8, 256], F32R)

    def into_c(k, b, m):
        o = slice(2 * k, 2 * k + 2)
        src = b[:, :].rearrange("p (c t) -> p c t", c=2)
        p = dve(lambda e: e.tensor_tensor(y[:, o, :], y[:, o, :], src, ALU.mult), m, y_ready)
        h = act(lambda e: e.activation(ch[:, o, :], y[:, o, :], ACT.Copy), p, mixed, vs)
        lo = dve(lambda e: e.tensor_tensor(cl[:, o, :], y[:, o, :], ch[:, o, :].bitcast(F32), ALU.subtract),
                 h, y_ready)
        return p, h, lo

    c_ready = []
    gate_raw = dense(hh, hl, h_ready, lambda: c_ready.extend(turned(piece_of(bt), range(4), b_ready, into_c)),
                     hold=True)
    dump("cT", y[:, :, :], c_ready)
    gb = slot("gb", 7, [128, 2, 1024])
    sig = {0: [], 1: []}
    for which, dst in ((0, ga), (1, gb)):
        for g in range(2):
            b, m = gate_raw if (which, g) == (0, 0) else dense(hh, hl, h_ready)
            for t in range(2):
                o = slice(512 * g, 512 * g + 512)
                q = slice(1024 * which + 512 * g, 1024 * which + 512 * g + 512)
                s = dve(lambda e: e.scalar_tensor_tensor(
                    out=dst[:, t, o], in0=bank[b[t]][:, :], scalar=stat(t), in1=bgb[:, q], op0=ALU.mult,
                    op1=ALU.add), m, l_bgb, c_ready)
                freed[b[t]] = [s]
                opened.discard(b[t])
                sig[which].append(act(lambda e: e.activation(dst[:, t, o], dst[:, t, o], ACT.Sigmoid), s))
    hh_done = m
    m_ready = []
    mh = slot("mh", 1, [128, 8, 256], F32R)
    ml = slot("ml", 2, [128, 8, 256], F32R)
    mT_ready = []

    def turn_m(q):
        mT_ready.extend(turned(piece_of(ga), range(2 * q, 2 * q + 2), m_ready, hi_lo(mh, ml, hh_done)))

    for which, xh_, xl_, rd, dst in ((0, ah, al, a_ready, ga), (1, ch, cl, c_ready, gb)):
        for g in range(2):
            b, m = dense(xh_, xl_, rd, (lambda: turn_m(0)) if (which, g) == (1, 1) else None)
            for t in range(2):
                o = slice(512 * g, 512 * g + 512)
                s = dve(lambda e: e.tensor_tensor(dst[:, t, o], dst[:, t, o], bank[b[t]][:, :], ALU.mult), m,
                        sig[which])
                freed[b[t]] = [s]
                if which:
                    s = dve(lambda e: e.tensor_tensor(ga[:, t, o], ga[:, t, o], gb[:, t, o], ALU.add), s)
                    m_ready.append(s)
    proj_done = m
    dump("m", ga[:, :, :], m_ready)

    x_ready = []
    fh = slot("fh", 5, [128, 8, 256], F32R)
    fl = slot("fl", 6, [128, 8, 256], F32R)
    f_ready = []

    def turn_f(q):
        f_ready.extend(turned(piece_of(x), range(2 * q, 2 * q + 2), x_ready, hi_lo_scaled(fh, fl, "g_ff", proj_done)))

    sq = []
    for g in range(2):
        b, m = dense(mh, ml, mT_ready, (lambda: turn_m(1)) if g == 0 else lambda: turn_f(0))
        for t in range(2):
            o = slice(512 * g, 512 * g + 512)
            s = dve(lambda e: e.tensor_tensor(x[:, t, o], x[:, t, o], bank[b[t]][:, :], ALU.add), m)
            freed[b[t]] = [s]
            x_ready.append(s)
            sq.append(squares(x[:, t, o], 16 + 2 * g + t, vjunk[:, 512 * t:512 * t + 512], s))
    mm_out = m
    dump("x1", x[:, :, :], x_ready)

    pool_of_banks[0] = [0, 1, 2, 3]
    zz = [slot(f"zz{k}", 3, [128, 4, 256], F32, 4096 * k) for k in range(2)]
    zh = [slot(f"zh{k}", 1, [128, 4, 256], F32R, 4096 * k) for k in range(2)]
    zl = [slot(f"zl{k}", 2, [128, 4, 256], F32R, 4096 * k) for k in range(2)]
    zz_free = [list(mT_ready), list(mT_ready)]
    z2_free = [[mm_out], [mm_out]]
    ff_b = [4, 5, 6, 7]
    r2 = []
    gw = slot("gw", 7, [128, 8, 8])
    gwh = slot("gwh", 8, [128, 8, 128], F32R)
    gwl = slot("gwl", 8, [128, 8, 128], F32R, 4096)
    g2b = slot("g2b", 9, [128, 1024])
    gs = []

    def ff_mid():
        turn_f(1)
        s = dve(lambda e: e.tensor_tensor(stat(16, 2), stat(16, 2), stat(18, 2), ALU.add), sq)
        s = inv_rms(16, D, s)
        r2.append(dve(lambda e: e.tensor_tensor(stat(16, 2), stat(16, 2), stat(16, 2), ALU.mult), s))
        l_gw = load("gw", gw[:, :, :], w_in2[:, GT:GT + 8].rearrange("(c p) n -> p c n", p=128), m_ready, eng="pool")
        zg = [pool(lambda e: e.memset(gwh[:, :, :].bitcast(F32), 0.0), proj_done),
              pool(lambda e: e.memset(gwl[:, :, :].bitcast(F32), 0.0), proj_done)]
        for k in range(2):
            o, i_ = slice(32 * k, 32 * k + 4), slice(4 * k, 4 * k + 4)
            h = dve(lambda e: e.tensor_copy(gwh[:, :, o], gw[:, :, i_]), l_gw, zg)
            gs.append(dve(lambda e: e.tensor_tensor(gwl[:, :, o], gw[:, :, i_], gwh[:, :, o].bitcast(F32),
                                                    ALU.subtract), h))

    l_g2b = load("g2b", g2b[:, :], A["g_norm2_2"].broadcast_to([128, 1024]), sig[1], eng="pool")
    zr = {}
    zT2 = {}
    for g in range(9):
        if g < 8:
            b, m = dense_turned(fh, fl, f_ready, ff_mid if g == 0 else None)
            z_ = zz[g % 2]
            zT2[g] = []
            for k in range(2):
                o = slice(2 * k, 2 * k + 2)
                s = act(lambda e: e.activation(z_[:, o, :], bank[b[k]][:, :].rearrange("p (c t) -> p c t", c=2),
                                               ACT.Relu), m, zz_free[g % 2])
                freed[b[k]] = [s]
                zr[k] = dve(lambda e: e.tensor_tensor(z_[:, o, :], z_[:, o, :], z_[:, o, :], ALU.mult), s)
            for k in range(2):
                o = slice(2 * k, 2 * k + 2)
                h = act(lambda e: e.activation(zh[g % 2][:, o, :], z_[:, o, :], ACT.Copy), zr[k], z2_free[g % 2])
                lo = dve(lambda e: e.tensor_tensor(zl[g % 2][:, o, :], z_[:, o, :],
                                                   zh[g % 2][:, o, :].bitcast(F32), ALU.subtract), h,
                         z2_free[g % 2])
                zT2[g] += [h, lo]
            zz_free[g % 2] = zT2[g]
        if g > 0:
            p = g - 1
            two = [next_half(), next_half()] if p == 7 else None
            for t_ in ((0, 1) if p == 7 else (None,)):
                for hf in range(2):
                    half = two[hf] if two else next_half()
                    i, s, h, lo = half
                    for c in range(2):
                        f = 2 * hf + c
                        for t in range(2) if t_ is None else (t_,):
                            for which, lhs in ((0, zh), (1, zl)):
                                a = lhs[p % 2][:, f, 128 * t:128 * t + 128]
                                for n in range(2):
                                    o = bank[ff_b[2 * t + n]][:, :]
                                    r_h = whi[s][:, 1024 * c + 512 * n:1024 * c + 512 * n + 512]
                                    r_l = wlo[s][:, 1024 * c + 512 * n:1024 * c + 512 * n + 512]
                                    first = p == 0 and f == 0 and which == 0
                                    end = p == 7 and f == 3 and which == 1
                                    m = pe(lambda e: e.matmul(o, a, r_h, start=first, stop=end), h, zT2[p],
                                           freed[ff_b[2 * t + n]] if first else None)
                                    if which == 0:
                                        m = pe(lambda e: e.matmul(o, a, r_l, start=False, stop=False), lo)
                    if t_ is None:
                        half_done(i, s, m, hf == 1)
                    elif t_ == 1:
                        half_done(i, s, m, True)
                if t_ == 0:
                    t0_done = m
            z2_free[p % 2] = [m]
    ff_done = m
    s_a2 = dve(lambda e: e.scalar_tensor_tensor(out=scale2b[:, :], in0=scale2b[:, :], scalar=1.0, in1=g2b[:, :],
                                                op0=ALU.add, op1=ALU.mult), l_g2b, ada_done[8], ada_done[9])
    a1 = small("a1", [128, 8])
    a1_ready = dve(lambda e: e.scalar_tensor_tensor(
        out=a1[:, :], in0=ada_cols[:, 8:16], scalar=1.0, in1=vec[:, VEC["g1"]:VEC["g1"] + 8], op0=ALU.add,
        op1=ALU.mult), ada_done[2], ada_done[3], l_vec)
    a1_ready = dve(lambda e: e.tensor_tensor(a1[:, :], a1[:, :], vec[:, VEC["g_nf"]:VEC["g_nf"] + 8], ALU.mult),
                   a1_ready)
    a2c = small("a2c", [128, 8])
    a2c_ready = dve(lambda e: e.scalar_tensor_tensor(
        out=a2c[:, :], in0=ada_cols[:, 24:32], scalar=1.0, in1=vec[:, VEC["g2"]:VEC["g2"] + 8], op0=ALU.add,
        op1=ALU.mult), ada_done[8], ada_done[9], l_vec)
    xg = slot("xg", 3, [128, 2, 1024])
    junk9 = slot("junk9", 9, [128, 1024], F32, 4096)
    x2_ready = []
    sums = []
    for t, d in ((0, t0_done), (1, ff_done)):
        for n in range(2):
            o = slice(512 * n, 512 * n + 512)
            b = ff_b[2 * t + n]
            s = dve(lambda e: e.scalar_tensor_tensor(out=x[:, t, o], in0=bank[b][:, :], scalar=stat(16 + t),
                                                     in1=x[:, t, o], op0=ALU.mult, op1=ALU.add), d, r2)
            freed[b] = [s]
            x2_ready.append(s)
            s1 = squares(x[:, t, o], 24 + 4 * n + t, junk9[:, 512:1024], [s, sums[-1:]])
            s = dve(lambda e: e.tensor_tensor(xg[:, t, o], x[:, t, o], nfb[:, o], ALU.mult), s, l_nfb, zT2[7])
            sums.append(s1)
            sums.append(squares(xg[:, t, o], 26 + 4 * n + t, junk9[:, 0:512], [s, sums[-2:-1]]))
    dump("x2", x[:, :, :], x2_ready)
    pool_of_banks[0] = list(range(8))
    xT_b = []

    def keep(k, b, m):
        xT_b.append((k, b, m))
        return []

    turned(piece_of(x), range(4), x2_ready, keep)
    s = dve(lambda e: e.tensor_tensor(stat(24, 4), stat(24, 4), stat(28, 4), ALU.add), sums)
    r1 = inv_rms(24, D, s)
    s = dve(lambda e: e.tensor_tensor(stat(28, 2), stat(24, 2), stat(24, 2), ALU.mult), r1)
    s = dve(lambda e: e.tensor_tensor(stat(26, 2), stat(26, 2), stat(28, 2), ALU.mult), s)
    s = inv_rms(26, D, s)
    s = dve(lambda e: e.tensor_tensor(stat(28, 2), stat(24, 2), stat(26, 2), ALU.mult), s)
    diag = slot("diag", 7, [128, 2, 128], F32, 1024)
    Rb = slot("Rb", 7, [128, 256], F32, 2048)
    dg = [dve(lambda e, t=t: e.tensor_scalar(diag[:, t, :], C("ident"), stat(28 + t), None, ALU.mult), s, l_cst)
          for t in range(2)]
    b = take()
    for t in range(2):
        m = pe(lambda e: e.matmul(bank[b][:, 128 * t:128 * t + 128], C("ones"), diag[:, t, :], start=True, stop=True),
               dg, freed[b])
    rb = act(lambda e: e.activation(Rb[:, :], bank[b][:, 0:256], ACT.Copy), m)
    freed[b] = [rb]
    nh = slot("nh", 5, [128, 8, 256], F32R)
    nl = slot("nl", 6, [128, 8, 256], F32R)
    nf = slot("nf", 4, [128, 8, 256])
    n_by = {}
    for k, bk, m in xT_b:
        fs, hs_ = [], []
        for c in range(2):
            q = 2 * k + c
            src = bk[:, 256 * c:256 * c + 256]
            f = dve(lambda e: e.scalar_tensor_tensor(
                out=nf[:, q, :], in0=src, scalar=a1[:, q:q + 1], in1=Rb[:, :], op0=ALU.mult, op1=ALU.mult),
                m, a1_ready, rb)
            hs_.append(act(lambda e: e.activation(nh[:, q, :], nf[:, q, :], ACT.Identity,
                                                  bias=ada_cols[:, q:q + 1]),
                           f, ff_done, ada_done[0], ada_done[1]))
            fs.append(f)
        n_by[k] = hs_
        for bb in range(8):
            if bank[bb] is bk:
                freed[bb] = fs
        if k % 2 == 1:
            for q in range(2 * k - 2, 2 * k + 2):
                n_by[q // 2].append(dve(lambda e: e.scalar_tensor_tensor(
                    out=nl[:, q, :], in0=nf[:, q, :], scalar=ada_cols[:, q:q + 1], in1=nh[:, q, :].bitcast(F32),
                    op0=ALU.add, op1=ALU.subtract), n_by[q // 2], ff_done))
    n_ready = list(n_by.values())
    x_ready = []

    def more_n():
        for t in range(2):
            x_ready.append(act(lambda e: e.activation(x[:, t, :], xg[:, t, :], ACT.Copy, scale=stat(24 + t)),
                               [m_ for _, _, m_ in xT_b], r1))

    qT = slot("qT", 4, [128, 8, 256])
    qT_ready = []

    def turned_into(dst, g, ready, after, mid=None):
        b, m = dense_turned(nh, nl, n_by, mid)
        for k in range(2):
            o = slice(4 * g + 2 * k, 4 * g + 2 * k + 2)
            s = act(lambda e: e.activation(dst[:, o, :], bank[b[k]][:, :].rearrange("p (c t) -> p c t", c=2),
                                           ACT.Copy), m, after)
            freed[b[k]] = [s]
            ready.append(s)

    turned_into(qT, 0, qT_ready, n_ready, more_n)
    b = take()
    for c in range(8):
        for a_, r_ in ((gwh, nh), (gwh, nl), (gwl, nh)):
            m = pe(lambda e: e.matmul(bank[b][:, 0:256], a_[:, c, :], r_[:, c, :],
                                      start=c == 0 and a_ is gwh and r_ is nh, stop=c == 7 and a_ is gwl),
                   gs, n_ready, freed[b])
    gates_mm = m
    flush()
    R = {}
    for k, n in enumerate(("i", "f", "w0", "w1")):
        R[n] = slot(f"row_{n}", 10, [4, 256], F32, 2048 + 1024 * k)
    for k, n in enumerate(("F", "M")):
        R[n] = slot(f"row_{n}", 10, [4, 256], F32, 6144 + 1024 * k)
    rd = [gates_mm, x_ready, ada_done[11]]
    s1 = dve(lambda e: e.tensor_scalar(R["i"][:, :], bank[b][0:4, 0:256], V("bg", 0, slice(0, 4)), None,
                                       ALU.add), rd)
    s2 = dve(lambda e: e.tensor_scalar(R["f"][:, :], bank[b][32:36, 0:256], V("bg", 1, slice(32, 36)), None,
                                       ALU.add), rd)
    freed[b] = [s1, s2]
    s3 = dve(lambda e: e.tensor_scalar(R["w0"][:, :], R["f"][:, :], -1.0, None, ALU.mult), s2)
    s3 = dve(lambda e: e.tensor_tensor(R["w0"][:, :], R["w0"][:, :], R["f"][:, :], ALU.min), s3)
    s3 = act(lambda e: e.activation(R["w0"][:, :], R["w0"][:, :], ACT.Exp), s3)
    s3 = dve(lambda e: e.tensor_scalar(R["w0"][:, :], R["w0"][:, :], 1.0, None, ALU.add), s3)
    s3 = act(lambda e: e.activation(R["w0"][:, :], R["w0"][:, :], ACT.Ln), s3)
    s3 = dve(lambda e: e.scalar_tensor_tensor(out=R["f"][:, :], in0=R["f"][:, :], scalar=0.0, in1=R["w0"][:, :],
                                              op0=ALU.min, op1=ALU.subtract), s3)
    z1 = dve(lambda e: e.memset(R["w1"][:, :], 0.0), rd)
    s4 = dve(lambda e: e.tensor_tensor_scan(R["F"][:, :], R["f"][:, :], R["w1"][:, :], 0.0, ALU.add, ALU.add),
             s3, z1)
    s5 = dve(lambda e: e.tensor_tensor(R["i"][:, :], R["i"][:, :], R["F"][:, :], ALU.subtract), s4, s1)
    s6 = dve(lambda e: e.tensor_tensor_scan(R["M"][:, :], R["i"][:, :], R["w1"][:, :], 0.0, ALU.max, ALU.max), s5)
    s7 = dve(lambda e: e.tensor_tensor(R["w0"][:, :], R["F"][:, :], R["M"][:, :], ALU.add), s6)
    s7 = act(lambda e: e.activation(R["w0"][:, :], R["w0"][:, :], ACT.Exp, scale=-1.0), s7)
    acol = small("acol", [128, 2, 4])
    ecol = small("ecol", [128, 2, 4])
    turned_into(qT, 1, qT_ready, n_ready)

    ET = slot("ET", 9, [128, 4, 2, 256])
    e_ready = {}
    et_ready = []
    cols_of = []

    def decays():
        b = take()
        for k, (n, rdy) in enumerate((("i", s5), ("w0", s7))):
            for t in range(2):
                m = pe(lambda e: e.transpose(
                    bank[b][:, 8 * k + 4 * t:8 * k + 4 * t + 4], R[n][:, 128 * t:128 * t + 128],
                    cst[0:4, CST["ident"]:CST["ident"] + 4]), rdy, freed[b])
        col1 = dve(lambda e: e.tensor_copy(acol[:, :, :], bank[b][:, 0:8].rearrange("p (t h) -> p t h", t=2)), m)
        col2 = dve(lambda e: e.tensor_copy(ecol[:, :, :], bank[b][:, 8:16].rearrange("p (t h) -> p t h", t=2)), m)
        freed[b] = [col1, col2]
        cols_of.extend([col1, col2])
        for h in range(4):
            b2 = take()
            m = pe(lambda e: e.matmul(
                bank[b2][:, 0:256], cst[0:4, CST["ident"] + h:CST["ident"] + h + 1].to_broadcast([4, 128]),
                R["M"][:, :], start=True, stop=True), s6, freed[b2])
            fs = []
            for s_ in range(2):
                o = slice(128 * s_, 256)
                d = dve(lambda e: e.tensor_scalar(ET[:, h, s_, o], bank[b2][:, o], acol[:, s_, h:h + 1], 0.0,
                                                  ALU.subtract, ALU.max), m, col1, s_a2, sums)
                fs.append(d)
                et_ready.append(d)
            freed[b2] = fs
        d = [dve(lambda e, s_=s_: e.tensor_tensor(
            ET[:, :, s_, 128 * s_:128 * s_ + 128], ET[:, :, s_, 128 * s_:128 * s_ + 128],
            C("pen_st").unsqueeze(1).broadcast_to([128, 4, 128]), ALU.add), et_ready) for s_ in range(2)]
        for s_ in range(2):
            r = act(lambda e: e.activation(ET[:, :, s_, 128 * s_:256], ET[:, :, s_, 128 * s_:256], ACT.Exp,
                                           scale=-1.0), d)
            for h in range(4):
                e_ready[h, s_] = r

    qc = slot("qc", 7, [128, 8, 256])
    qc_ready = []
    conv_ready = []

    def conv2(c0):
        for c in range(c0, c0 + 4):
            s = act(lambda e: e.activation(qc[:, c, :], qT[:, c, :], ACT.Identity, scale=V("conv2", 24 + c),
                                           bias=V("bconv2", c)), qT_ready, n_ready, gs)
            for k, d in ((2, 1), (1, 2), (0, 3)):
                s = dve(lambda e: e.scalar_tensor_tensor(
                    out=qc[:, c, d:256], in0=qT[:, c, 0:256 - d], scalar=V("conv2", 8 * k + c), in1=qc[:, c, d:256],
                    op0=ALU.mult, op1=ALU.add), s)
            conv_ready.append(s)

    def silu2():
        for o in (slice(0, 4), slice(4, 8)):
            qc_ready.append(act(lambda e: e.activation(qc[:, o, :], qc[:, o, :], ACT.Silu), conv_ready))

    qaT = slot("qaT", 3, [128, 8, 256])
    qaT_ready = []
    vmt = slot("vmt", 2, [128, 2, 512])
    vat = slot("vat", 2, [128, 2, 512], F32, 4096)
    omt = slot("omt", 1, [128, 2, 512])
    va_ready, vm_ready, om_ready = [], [], []
    MSC = 128 ** -0.5
    ASC = 64 ** -0.5
    sc_ready = {}

    def mlstm_scores():
        for h in range(4):
            b = take()
            where = [(s_, slice(128 * s_, 256), slice(256 * s_ + 128 * s_, 256 * s_ + 256)) for s_ in range(2)]
            for s_, o, po in where:
                m = pe(lambda e: e.matmul(bank[b][:, po], qc[:, 4 + h, 128 * s_:128 * s_ + 128], qc[:, h, o],
                                          start=True, stop=True), qc_ready, freed[b])
            for s_, o, po in where:
                sc_ready[h, s_] = dve(lambda e: e.scalar_tensor_tensor(
                    out=ET[:, h, s_, o], in0=bank[b][:, po], scalar=MSC, in1=ET[:, h, s_, o], op0=ALU.mult,
                    op1=ALU.mult), m, e_ready[h, s_])
            freed[b] = [sc_ready[h, 0], sc_ready[h, 1]]

    mix = slot("mix", 10, [128, 2, 1024])
    junk1 = slot("junk1", 1, [128, 128], F32, 4096)
    ghb = slot("ghb", 1, [128, 512], F32, 4608)
    wr = slot("wr", 1, [128, 8, 36], F32, 6656)
    brb = slot("brb", 1, [128, 36], F32, 7808)
    hm_last = []

    def mlstm_mm(t):
        b = take()
        dn = take()
        for h in range(4):
            for s_ in range(t + 1):
                lhs = ET[:, h, s_, 128 * t:128 * t + 128]
                pe(lambda e: e.matmul(
                    bank[b][:, 128 * h:128 * h + 128], lhs, vmt[:, s_, 128 * h:128 * h + 128],
                    start=(s_ == 0), stop=(s_ == t)), sc_ready[h, s_], vm_ready, freed[b])
            for s_ in range(t + 1):
                lhs = ET[:, h, s_, 128 * t:128 * t + 128]
                m = pe(lambda e: e.matmul(bank[dn][:, h:h + 1], lhs, C("ones", 0, 1), start=(s_ == 0),
                                          stop=(s_ == t)), freed[dn])
        return b, dn, m

    def mlstm_out(t, b, dn, m):
        k = 40 + 16 * t
        d1 = dve(lambda e: e.tensor_scalar(stat(k, 4), bank[dn][:, 0:4], -1.0, None, ALU.mult), m)
        d2 = dve(lambda e: e.tensor_tensor(stat(k, 4), stat(k, 4), bank[dn][:, 0:4], ALU.max), d1)
        d3 = dve(lambda e: e.tensor_tensor(stat(k, 4), stat(k, 4), ecol[:, t, :], ALU.max), d2)
        d4 = dve(lambda e: e.reciprocal(stat(k, 4), stat(k, 4)), d3)
        freed[dn] = [d2]
        hs, ss = [], []
        for h in range(4):
            o = slice(128 * h, 128 * h + 128)
            s = dve(lambda e: e.tensor_scalar(mix[:, t, o], bank[b][:, o], stat(k + h), None, ALU.mult), d4, m,
                    rows_done)
            hs.append(s)
            ss.append(act(lambda e: e.activation(junk1[:, :], mix[:, t, o], ACT.Square, accum_out=stat(k + 4 + h)),
                          s, ss[-1] if ss else last_junk))
        last_junk[:] = [ss[-1]]
        freed[b] = hs
        d = dve(lambda e: e.tensor_tensor(omt[:, t, :], omt[:, t, :], ghb[:, :], ALU.mult), om_ready, l_ghb)
        d5 = inv_rms(k + 4, 128, ss, 4)
        for h in range(4):
            o = slice(128 * h, 128 * h + 128)
            hm_last.append(dve(lambda e: e.scalar_tensor_tensor(
                out=mix[:, t, o], in0=mix[:, t, o], scalar=stat(k + 4 + h), in1=omt[:, t, o], op0=ALU.mult,
                op1=ALU.mult), d, d5))

    last_junk = []
    S = [slot("S0", 4, [128, 4, 384]), slot("S1", 8, [128, 4, 384])]
    PTt = [slot("PTt0", 3, [128, 4, 384]), slot("PTt1", 4, [128, 4, 384])]
    exps, recips, pts, att_last = {}, {}, {}, []
    S_free = [conv_ready, [gates_mm]]
    pt_free = {}
    pen = C("pen_ts").unsqueeze(1)

    def att_scores(half):
        Sx = S[half]
        b0, b1, b2 = take(3)
        for hq in range(4):
            h = 2 * hq + half
            c, p0 = h // 2, 64 * (h % 2)
            q0 = qaT[p0:p0 + 64, c, :]
            k0 = qaT[p0:p0 + 64, 4 + c, :]
            o0 = bank[b0][:, 128 * hq:128 * hq + 128]
            o1 = bank[[b1, b2][hq // 2]][:, 256 * (hq % 2):256 * (hq % 2) + 256]
            pe(lambda e: e.matmul(o0, q0[:, 0:128], k0[:, 0:128], start=True, stop=True), qaT_ready, freed[b0])
            m = pe(lambda e: e.matmul(o1, q0[:, 128:256], k0, start=True, stop=True), freed[[b1, b2][hq // 2]])
        w = []
        w.append(dve(lambda e: e.tensor_tensor(
            Sx[:, :, 0:128], bank[b0][:, :].rearrange("p (h s) -> p h s", h=4),
            pen.broadcast_to([128, 4, 128]), ALU.add), m, S_free[half]))
        for k, bb in enumerate((b1, b2)):
            src = bank[bb][:, :].rearrange("p (h s) -> p h s", h=2)
            w.append(act(lambda e: e.activation(Sx[:, 2 * k:2 * k + 2, 128:256], src[:, :, 0:128], ACT.Copy), m,
                         S_free[half]))
            w.append(dve(lambda e: e.tensor_tensor(
                Sx[:, 2 * k:2 * k + 2, 256:384], src[:, :, 128:256], pen.broadcast_to([128, 2, 128]), ALU.add),
                m, w[-1], S_free[half]))
        freed[b0], freed[b1], freed[b2] = [w[0]], [w[1], w[2]], [w[3], w[4]]
        k = 72 + 28 * half
        mx = [dve(lambda e: e.tensor_reduce(stat(k, 4), Sx[:, :, 0:128], AX, ALU.max, negate=False), w),
              dve(lambda e: e.tensor_reduce(stat(k + 4, 4), Sx[:, :, 128:384], AX, ALU.max, negate=False), w)]
        mx = dve(lambda e: e.tensor_scalar(stat(k, 8), stat(k, 8), -ASC, None, ALU.mult), mx)
        ex = []
        for hq in range(4):
            for t, o in ((0, slice(0, 128)), (1, slice(128, 384))):
                ex.append(act(lambda e: e.activation(
                    Sx[:, hq, o], Sx[:, hq, o], ACT.Exp, bias=stat(k + 4 * t + hq), scale=ASC,
                    accum_out=stat(k + 8 + 4 * t + hq)), mx))
        exps[half] = ex
        recips[half] = dve(lambda e: e.reciprocal(stat(k + 16, 8), stat(k + 8, 8)), ex)
        pt_free[half] = [m]

    def att_turn(half):
        Sx = S[half]
        pts[half] = []
        for hq in range(4):
            b = take()
            for j in range(3):
                m = pe(lambda e: e.transpose(bank[b][:, 128 * j:128 * j + 128], Sx[:, hq, 128 * j:128 * j + 128],
                                             C("ident")), exps[half], freed[b])
            if hq % 2:
                s = act(lambda e: e.activation(PTt[half][:, hq, :], bank[b][:, 0:384], ACT.Copy), m,
                        pt_free[half])
            else:
                s = dve(lambda e: e.tensor_copy(PTt[half][:, hq, :], bank[b][:, 0:384]), m, pt_free[half])
            freed[b] = [s]
            pts[half].append(s)
        if half == 0:
            pt_free[1] = [m]
        pt_free[2] = [m]

    def att_values(half):
        k = 72 + 28 * half
        P = PTt[half]
        b = take()
        for hq in range(4):
            h = 2 * hq + half
            vv = [vat[:, s_, 64 * h:64 * h + 64] for s_ in range(2)]
            o0 = bank[b][:, 64 * hq:64 * hq + 64]
            o1 = bank[b][:, 256 + 64 * hq:256 + 64 * hq + 64]
            pe(lambda e: e.matmul(o0, P[:, hq, 0:128], vv[0], start=True, stop=True), pts[half], va_ready, freed[b])
            pe(lambda e: e.matmul(o1, P[:, hq, 128:256], vv[0], start=True, stop=False))
            m = pe(lambda e: e.matmul(o1, P[:, hq, 256:384], vv[1], start=False, stop=True))
        fs = []
        for t in range(2):
            o = mix[:, t, 512:1024].rearrange("p (h w d) -> p w h d", h=4, w=2)[:, half, :, :]
            fs.append(dve(lambda e: e.tensor_tensor(
                o, bank[b][:, 256 * t:256 * t + 256].rearrange("p (h d) -> p h d", h=4),
                stat(k + 16 + 4 * t, 4).unsqueeze(2).broadcast_to([128, 4, 64]), ALU.mult), m, recips[half],
                rows_done))
        freed[b] = fs
        att_last.extend(fs)

    flush()
    conv2(0)
    turned_into(qaT, 0, qaT_ready, x_ready)
    flush()
    decays()
    rows_done = [s7, *cols_of, *e_ready.values(), gs[-1]]
    turned_into(qaT, 1, qaT_ready, x_ready)
    flush()
    conv2(4)
    l_ghb = load("ghb", ghb[:, :], A["g_mlstm_head_2"].broadcast_to([128, 512]), ff_done, eng="pool")
    l_wr0 = load("wr0", wr[:, :, 0:4], A["w_router_group_2"][0].rearrange("(c p) n -> p c n", p=128), ff_done,
                 eng="pool")
    l_wr1 = load("wr1", wr[:, :, 4:36], A["w_router_expert_2"][0].rearrange("(c p) n -> p c n", p=128), ff_done,
                 eng="pool")
    l_br0 = load("br0", brb[:, 0:4], A["b_router_group_2"].broadcast_to([128, 4]), ff_done, eng="pool")
    l_br1 = load("br1", brb[:, 4:36], A["b_router_expert_2"].broadcast_to([128, 32]), ff_done, eng="pool")
    b, m = dense(nh, nl, n_ready)
    for t in range(2):
        s = act(lambda e: e.activation(vat[:, t, :], bank[b[t]][:, :], ACT.Copy), m)
        freed[b[t]] = [s]
        va_ready.append(s)
    flush()
    silu2()
    att_scores(0)
    att_scores(1)
    pt_free[0] = pt_free[1]
    b, m = dense(nh, nl, n_ready, mlstm_scores)
    for t in range(2):
        s = act(lambda e: e.activation(vmt[:, t, :], bank[b[t]][:, :], ACT.Copy), m)
        freed[b[t]] = [s]
        vm_ready.append(s)
    att_turn(0)
    flush()
    br_ready = []

    def shift_route():
        b = take()
        for c in range(8):
            m = pe(lambda e: e.matmul(bank[b][:, 0:36], ada_cols[:, 16 + c:17 + c].to_broadcast([128, 128]),
                                      wr[:, c, :], start=c == 0, stop=c == 7), l_wr0, l_wr1, ada_done[6], ada_done[7],
                   freed[b])
        s = dve(lambda e: e.tensor_tensor(brb[:, :], brb[:, :], bank[b][:, 0:36], ALU.add), m, l_br0, l_br1)
        freed[b] = [s]
        br_ready.append(s)

    b, m = dense(nh, nl, n_ready, lambda: (att_turn(1), shift_route()))
    for t in range(2):
        s = act(lambda e: e.activation(omt[:, t, :], bank[b[t]][:, :], ACT.Sigmoid), m)
        freed[b[t]] = [s]
        om_ready.append(s)
    nh_done = m
    flush()
    att_values(0)
    att_values(1)
    mxh = slot("mxh", 5, [128, 8, 256], F32R)
    mxl = slot("mxl", 6, [128, 8, 256], F32R)
    mm01 = [mlstm_mm(0), mlstm_mm(1)]
    mix_ready = turned(piece_of(mix), range(2, 4), att_last, hi_lo(mxh, mxl, nh_done))
    mlstm_out(0, *mm01[0])
    mlstm_out(1, *mm01[1])
    b4 = [take(2), take(2)]
    for bb in b4:
        opened.update(bb)
    for g in range(2):
        half = next_half(g == 0)
        half_done(half[0], half[1], dense_half(mxh, mxl, mix_ready, b4[g], half, 1, True, False), True)
    dump("mix", mix[:, :, :], [*att_last, *hm_last])
    mix_ready += turned(piece_of(mix), range(2), hm_last, hi_lo(mxh, mxl, nh_done))
    gx = slot("gx", 3, [128, 2, 1024])
    x_ready = []
    sq = []
    junk4 = slot("junk4", 4, [128, 2, 1024])
    h2T = slot("h2T", 8, [128, 8, 256])
    b_rt = take()
    opened.add(b_rt)
    h2T_ready = []

    def x3(g, m):
        for t in range(2):
            o = slice(512 * g, 512 * g + 512)
            b = b4[g][t]
            s = dve(lambda e: e.tensor_tensor(gx[:, t, o], bank[b][:, :], gate1b[:, o], ALU.mult), m, ada_done[4],
                    ada_done[5], att_last, pts[0])
            freed[b] = [s]
            x_ready.append(dve(lambda e: e.tensor_tensor(x[:, t, o], x[:, t, o], gx[:, t, o], ALU.add), s))

    def sums_of(g):
        for t in range(2):
            o = slice(512 * g, 512 * g + 512)
            sq.append(squares(x[:, t, o], 2 * g + t, junk4[:, t, o], [x_ready[2 * g + t], att_last, conv_ready]))

    def by_a2(k, b, m):
        return [act(lambda e, q=q: e.activation(h2T[:, q, :], b[:, 256 * (q % 2):256 * (q % 2) + 256], ACT.Copy,
                                                scale=a2c[:, q:q + 1]), m, a2c_ready, exps[1], pt_free[2])
                for q in (2 * k, 2 * k + 1)]

    def route(k):
        for c in range(4 * k, 4 * k + 4):
            for t in range(2):
                m = pe(lambda e: e.matmul(
                    bank[b_rt][:, 36 * t:36 * t + 36], h2T[:, c, 128 * t:128 * t + 128], wr[:, c, :],
                    start=c == 0 and t == 0, stop=c == 7 and t == 1, skip_group_check=True), h2T_ready, l_wr0,
                    l_wr1, freed[b_rt])
        return m

    half = next_half()
    m = dense_half(mxh, mxl, mix_ready, b4[0], half, 0, False, True)
    half_done(half[0], half[1], m, True)
    x3(0, m)
    sums_of(0)
    half = next_half(False)
    mixes_done = dense_half(mxh, mxl, mix_ready, b4[1], half, 0, False, True)
    half_done(half[0], half[1], mixes_done, True)
    h2T_ready += turned(piece_of(x), range(2), x_ready, by_a2)
    route(0)
    x3(1, mixes_done)
    h2T_ready += turned(piece_of(x), range(2, 4), x_ready, by_a2)
    router_mm = route(1)
    sums_of(1)
    opened.clear()
    dump("x3", x[:, :, :], x_ready)
    gfb = slot("gfb", 7, [128, 1024])
    l_gfb = load("gfb", gfb[:, :], A["g_final_2"].broadcast_to([128, 1024]), x_ready, eng="pool")
    h2 = slot("h2", 10, [128, 2, 1024])
    s = dve(lambda e: e.tensor_tensor(stat(0, 2), stat(0, 2), stat(2, 2), ALU.add), sq)
    r = inv_rms(0, D, s)
    th = slot("th", 2, [128, 2, 1024], F32R)
    tl = slot("tl", 9, [128, 2, 1024], F32R)
    h2r = []
    th_r = []
    tl_r = []
    for t in (1, 0):
        if t == 0:
            s = dve(lambda e: e.scalar_tensor_tensor(out=h2[:, t, :], in0=x[:, t, :], scalar=stat(t),
                                                     in1=scale2b[:, :], op0=ALU.mult, op1=ALU.mult), r, s_a2,
                    mix_ready)
        else:
            s = act(lambda e: e.activation(h2[:, t, :], x[:, t, :], ACT.Copy, scale=stat(t)), r, mix_ready)
            s = pool(lambda e: e.tensor_tensor(h2[:, t, :], h2[:, t, :], scale2b[:, :], ALU.mult), s, s_a2)
        h2r.append((pool if t else dve)(
            lambda e: e.tensor_tensor(h2[:, t, :], h2[:, t, :], shift2b[:, :], ALU.add), s, ada_done[6], ada_done[7]))

    def split_h2():
        for t in (0, 1):
            th_r.append(act(lambda e: e.activation(th[:, t, :], h2[:, t, :], ACT.Copy), h2r[1 - t], mixes_done))
            tl_r.append(pool(lambda e: e.tensor_tensor(tl[:, t, :], h2[:, t, :], th[:, t, :].bitcast(F32),
                                                       ALU.subtract), th_r[-1], s_a2, mixes_done))

    dump("h2", h2[:, :, :], h2r)

    lg = small("lg", [128, 2, 36])
    WT, MK, RK, T0, T1, T2 = (tab[:, k, :, :] for k in range(6))
    rs = small("rs", [128, 2, 16])

    def B(ap, n):
        return ap.broadcast_to([128, 2, n])

    ls = [dve(lambda e, t=t: e.scalar_tensor_tensor(
        out=lg[:, t, :], in0=bank[b_rt][:, 36 * t:36 * t + 36], scalar=stat(t), in1=brb[:, :], op0=ALU.mult,
        op1=ALU.add), router_mm, r, br_ready) for t in range(2)]
    freed[b_rt] = list(ls)
    s = ls[1]
    dump("lg", lg[:, :, :], ls)

    def chain(fn, *after):
        cur[0] = dve(fn, cur[0], *after)
        return cur[0]

    cur = [ls]

    def first_max(src, n, top, hot, tmp):
        chain(lambda e: e.tensor_reduce(top, src, AX, ALU.max))
        chain(lambda e: e.tensor_tensor(tmp, src, B(top, n), ALU.is_lt))
        io = C("iota32", 0, n).unsqueeze(1).broadcast_to([128, 2, n])
        chain(lambda e: e.scalar_tensor_tensor(out=tmp, in0=tmp, scalar=FAR, in1=io, op0=ALU.mult, op1=ALU.add))
        chain(lambda e: e.tensor_reduce(rs[:, :, 15:16], tmp, AX, ALU.min))
        return chain(lambda e: e.tensor_tensor(hot, io, B(rs[:, :, 15:16], n), ALU.is_equal))

    G = lg[:, :, 0:4]
    E_ = lg[:, :, 4:36]
    first_max(G, 4, rs[:, :, 0:1], rs[:, :, 4:8], rs[:, :, 8:12])
    chain(lambda e: e.tensor_tensor(rs[:, :, 8:12], G, B(rs[:, :, 0:1], 4), ALU.subtract))
    ex = act(lambda e: e.activation(rs[:, :, 8:12], rs[:, :, 8:12], ACT.Exp), cur[0])
    split_h2()
    chain(lambda e: e.tensor_scalar(rs[:, :, 4:8], rs[:, :, 4:8], BIG, -BIG, ALU.mult, ALU.add))
    pen8 = rs[:, :, 4:8].unsqueeze(3).broadcast_to([128, 2, 4, 8])
    chain(lambda e: e.tensor_tensor(T1.rearrange("p t (g n) -> p t g n", g=4),
                                    E_.rearrange("p t (g n) -> p t g n", g=4), pen8, ALU.add))
    first_max(T1, 32, rs[:, :, 2:3], WT, T0)
    chain(lambda e: e.scalar_tensor_tensor(out=T1, in0=WT, scalar=-2 * BIG, in1=T1, op0=ALU.mult, op1=ALU.add))
    first_max(T1, 32, rs[:, :, 3:4], T2, T0)
    mk_ready = chain(lambda e: e.tensor_tensor(MK, WT, T2, ALU.add))
    b_rk = take()
    mk = MK.rearrange("p t n -> p (t n)")
    pe(lambda e: e.matmul(bank[b_rk][:, 0:64], C("lt"), mk, start=True, stop=False, skip_group_check=True),
       mk_ready, freed[b_rk])
    rk_mm = pe(lambda e: e.matmul(bank[b_rk][:, 32:64], C("ones"), MK[:, 0, :], start=False, stop=True,
                                   skip_group_check=True))
    chain(lambda e: e.tensor_reduce(rs[:, :, 1:2], rs[:, :, 8:12], AX, ALU.add), ex)
    chain(lambda e: e.reciprocal(rs[:, :, 1:2], rs[:, :, 1:2]))
    chain(lambda e: e.tensor_tensor(rs[:, :, 8:9], rs[:, :, 3:4], rs[:, :, 2:3], ALU.subtract))
    cur[0] = act(lambda e: e.activation(rs[:, :, 8:9], rs[:, :, 8:9], ACT.Exp), cur[0])
    chain(lambda e: e.tensor_scalar(rs[:, :, 9:10], rs[:, :, 8:9], 1.0, None, ALU.add))
    chain(lambda e: e.reciprocal(rs[:, :, 9:10], rs[:, :, 9:10]))
    chain(lambda e: e.tensor_tensor(rs[:, :, 9:10], rs[:, :, 9:10], rs[:, :, 1:2], ALU.mult))
    chain(lambda e: e.tensor_tensor(rs[:, :, 8:9], rs[:, :, 8:9], rs[:, :, 9:10], ALU.mult))
    chain(lambda e: e.tensor_scalar(T0, MK, -FAR, FAR, ALU.mult, ALU.add))
    rk_ready = chain(lambda e: e.tensor_tensor(
        RK, T0, bank[b_rk][:, 0:64].rearrange("p (t n) -> p t n", t=2), ALU.add), rk_mm)
    chain(lambda e: e.tensor_tensor(WT, WT, B(rs[:, :, 9:10], 32), ALU.mult))
    chain(lambda e: e.tensor_tensor(T2, T2, B(rs[:, :, 8:9], 32), ALU.mult))
    wt_ready = chain(lambda e: e.tensor_tensor(WT, WT, T2, ALU.add))
    freed[b_rk] = [rk_ready]
    cnt = small("cnt", [128, 8, 32])
    ov_ready = []
    tl_cell = []

    def count_overflow():
        def chain(fn, *after, mark=None):
            todo.append((fn, after, mark))

        b = take()
        pe(lambda e: e.matmul(bank[b][:, 0:32], C("ones"), MK[:, 0, :], start=True, stop=False), wt_ready, freed[b])
        m = pe(lambda e: e.matmul(bank[b][:, 0:32], C("ones"), MK[:, 1, :], start=False, stop=True))
        done = []
        chain(lambda e: e.tensor_copy(cnt[:, 0, :], bank[b][:, 0:32]), m, mark=done)
        freed[b] = done
        THR = [float(SLOTS * k) for k in (1, 2, 3)]
        for k in range(3):
            chain(lambda e, k=k: e.tensor_scalar(cnt[:, 1 + k, :], cnt[:, 0, :], THR[k], None, ALU.is_gt))
        chain(lambda e: e.tensor_tensor(cnt[:, 1, :], cnt[:, 1, :], cnt[:, 2, :], ALU.add))
        chain(lambda e: e.tensor_tensor(cnt[:, 1, :], cnt[:, 1, :], cnt[:, 3, :], ALU.add))
        chain(lambda e: e.memset(cnt[:, 2, :], 0.0))
        chain(lambda e: e.tensor_tensor_scan(cnt[:, 3, :], cnt[:, 1, :], cnt[:, 2, :], 0.0, ALU.add, ALU.add))
        chain(lambda e: e.tensor_tensor(cnt[:, 4, :], cnt[:, 3, :], cnt[:, 1, :], ALU.subtract))
        chain(lambda e: e.tensor_copy(ovf[:, 0:1], cnt[:, 3, 31:32]), mark=ov_ready)
        for j in range(NOV):
            chain(lambda e, j=j: e.tensor_scalar(cnt[:, 5, :], cnt[:, 3, :], float(j), None, ALU.is_le))
            chain(lambda e, j=j: e.tensor_reduce(cnt[:, 6, j:j + 1], cnt[:, 5, :], AX, ALU.add))
        chain(lambda e: e.tensor_scalar(cnt[:, 7, 0:NOV], cnt[:, 6, 0:NOV], float(NE - 1), None, ALU.min))
        chain(lambda e: e.tensor_copy(ovf[:, 8:8 + NOV], cnt[:, 7, 0:NOV]), mark=ids_ready)
        some(2)

    todo = []

    def some(n):
        for fn, after, mark in todo[:n]:
            cur[0] = dve(fn, cur[0], *after)
            if mark is not None:
                mark.append(cur[0])
        del todo[:n]

    x_rk = [*th_r, *tl_r, rk_ready, wt_ready]
    XT = [[slot(f"XT{k}{q}", (3, 4, 8, 11)[2 * k + q], [128, 2, 8, 2, SLOTS], F32R) for q in range(2)]
          for k in range(2)]
    GU = [slot(f"GU{k}", 6, [128, 2, 512], F32, 4096 * k) for k in range(2)]
    YH = [slot(f"YH{k}", 5, [128, 512], F32R, 4096 * k) for k in range(2)]
    YL = [slot(f"YL{k}", 5, [128, 512], F32R, 4096 * k + 2048) for k in range(2)]
    HF = [slot(f"HF{k}", 1, [128, 256], F32, 1024 * k) for k in range(2)]
    HS = [slot(f"HS{k}", 1, [128, 4, 2, SLOTS], F32R, 2048 + 2048 * k) for k in range(2)]
    PP = [slot(f"PP{k}", 10, [128, 2, 4, 2, SLOTS], F32R, 4096 * k) for k in range(2)]
    PT = [slot(f"PT{k}", 12, [128, 256], F32R, 1024 * k) for k in range(4)]
    wsl = small("wsl", [128, 4])
    pool_of_banks[0] = [0, 1, 2, 3]
    acc = [4, 5, 6, 7]
    h2_done = [*tl_r, *th_r, *h2T_ready]
    fr = {("PP", k): [*h2_done, *x_ready] for k in range(2)}
    fr.update({("PT", k): list(h2_done) for k in range(4)})
    fr.update({("XT", k): [router_mm, *h2T_ready, *x_ready] for k in range(2)})
    fr.update({("GU", k): [mixes_done] for k in range(2)})
    fr.update({("Y", k): [mixes_done] for k in range(2)})
    fr.update({("H", k): [mixes_done] for k in range(2)})
    fr.update({("wsl", k): [] for k in range(4)})
    io4 = C("iota64").unsqueeze(1).unsqueeze(1).broadcast_to([128, 4, 2, SLOTS])

    def blocks(n, rk, wt, after, first, last_of_all, base):
        ready = {}

        def one_hots(p):
            k = p % 2
            s = []
            for t in range(2):
                src = rk(t, 4 * p, 4).unsqueeze(2).unsqueeze(3).broadcast_to([128, 4, 2, SLOTS])
                s.append(dve(lambda e, t=t, k=k, src=src: e.tensor_tensor(PP[k][:, t, :, :, :], io4, src,
                                                                          ALU.is_equal), after, fr["PP", k]))
            ready["P", p] = s

        def gather(p, c):
            k = p % 2
            b = take()
            dst = bank[b][:, :].rearrange("p (x h s) -> p x h s", x=4, h=2)
            for hl_, src in ((0, th), (1, tl)):
                for t in range(2):
                    m = pe(lambda e: e.matmul(
                        dst[:, :, hl_, :], src[:, t, 128 * c:128 * c + 128], PP[k][:, t, :, 0, :],
                        start=(t == 0), stop=(t == 1)), ready["P", p], x_rk, freed[b])
            fs = []
            for q in range(2):
                v = dst[:, 2 * q:2 * q + 2, :, :]
                o = XT[k][q][:, :, c, :, :]
                if c % 2:
                    fs.append(act(lambda e: e.activation(o, v, ACT.Copy), m, fr["XT", k]))
                else:
                    fs.append(dve(lambda e: e.tensor_copy(o, v), m, fr["XT", k]))
            freed[b] = fs
            ready.setdefault(("X", p), []).append(fs)

        def turn_p(j):
            k = j // 4 % 2
            b = take()
            Pm = [PP[k][:, t, j % 4, :, :].rearrange("p d s -> p (d s)").bitcast(F32) for t in range(2)]
            for t in range(2):
                pe(lambda e: e.transpose(bank[b][:, 128 * t:128 * t + 128], Pm[t], C("ident")),
                   ready["P", j // 4], freed[b])
            for t in range(2):
                m = pe(lambda e, w=wt(t, j): e.matmul(bank[b][:, 256:257], Pm[t], w, start=(t == 0), stop=(t == 1)),
                       after, x_rk)
            q = j % 4
            s1 = act(lambda e: e.activation(PT[q][:, :], bank[b][:, 0:256], ACT.Copy), m, fr["PT", q])
            s2 = act(lambda e: e.activation(wsl[:, q:q + 1], bank[b][:, 256:257], ACT.Copy), m, fr["wsl", q])
            freed[b] = [s1, s2]
            ready["T", j] = [s1]
            ready["w", j] = [s2]
            if j % 4 == 3:
                fr["PP", k] = [m]

        def gate_up(j, w, hf):
            k = j % 2
            if hf == 0:
                ready["b", w] = take()
                opened.add(ready["b", w])
            b = ready["b", w]
            half = next_half()
            for c in range(4):
                q = 4 * hf + c
                a = XT[j // 4 % 2][j % 4 // 2][:, j % 2, q, :, :].rearrange("p h s -> p (h s)")
                m = times(bank[b][:, :], a, half, slice(512 * c, 512 * c + 512), q == 0, q == 7,
                          ready["X", j // 4][:q + 1], freed[b])
            if hf == 1:
                opened.discard(b)
                e_ = act(lambda e: e.activation(GU[k][:, w, :], bank[b][:, :], ACT.Copy), m, fr["GU", k])
                freed[b] = [e_]
                ready["GU", j, w] = e_
            half_done(half[0], half[1], m, j + w + hf == 0)
            if w == 1 and hf == 1 and j % 4 == 3:
                fr["XT", j // 4 % 2] = [m]

        def hidden(j):
            k = j % 2
            b = take()
            for w in range(2):
                for f in range(4):
                    m = pe(lambda e: e.matmul(
                        bank[b][:, 256 * w + 64 * f:256 * w + 64 * f + 64], GU[k][:, w, 128 * f:128 * f + 128],
                        C("ident2"), start=True, stop=True), ready["GU", j, w], freed[b])
            fr["GU", k] = [m]
            s1 = act(lambda e: e.activation(HF[k][:, :], bank[b][:, 0:256], ACT.Silu), m, fr["H", k])
            s2 = dve(lambda e: e.tensor_tensor(HF[k][:, :], HF[k][:, :], bank[b][:, 256:512], ALU.mult), s1)
            freed[b] = [s2]
            v = HF[k][:, :].rearrange("p (f s) -> p f s", f=4)
            s3 = act(lambda e: e.activation(HS[k][:, :, 0, :], v, ACT.Copy), s2, fr["H", k])
            s4 = dve(lambda e: e.tensor_tensor(HS[k][:, :, 1, :], v, HS[k][:, :, 0, :].bitcast(F32),
                                               ALU.subtract), s3)
            ready["H", j] = [s3, s4]

        def down(j, hf):
            k = j % 2
            if hf == 0:
                ready["b", 2] = take(2)
            b = ready["b", 2]
            half = next_half()
            for c in range(2):
                f = 2 * hf + c
                a = HS[k][:, f, :, :].rearrange("p h s -> p (h s)")
                for n in range(2):
                    o = slice(1024 * c + 512 * n, 1024 * c + 512 * n + 512)
                    m = times(bank[b[n]][:, :], a, half, o, f == 0, f == 3, ready["H", j], freed[b[n]])
            if hf == 1:
                fr["H", k] = [m]
                q = j % 4
                for n in range(2):
                    s1 = act(lambda e: e.activation(YH[n][:, :], bank[b[n]][:, :], ACT.Copy, scale=wsl[:, q:q + 1]),
                             m, fr["Y", n], ready["w", j])
                    s2 = dve(lambda e: e.scalar_tensor_tensor(
                        out=YL[n][:, :], in0=bank[b[n]][:, :], scalar=wsl[:, q:q + 1],
                        in1=YH[n][:, :].bitcast(F32), op0=ALU.mult, op1=ALU.subtract), s1, fr["Y", n])
                    freed[b[n]] = [s2]
                    ready["Y", j, n] = [s1, s2]
                fr["wsl", q] = [s2]
            half_done(half[0], half[1], m)

        def combine(j):
            q = j % 4
            for n in range(2):
                for t in range(2):
                    o = bank[acc[2 * t + n]][:, :]
                    a = PT[q][:, 128 * t:128 * t + 128]
                    i0 = first and j == 0
                    i1 = j == n_blocks - 1
                    m0 = [] if not i0 else freed[acc[2 * t + n]]
                    pe(lambda e: e.matmul(o, a, YH[n][:, :], start=i0, stop=False, skip_group_check=True),
                       ready["Y", j, n], ready["T", j], m0)
                    m = pe(lambda e: e.matmul(o, a, YL[n][:, :], start=False, stop=i1, skip_group_check=True))
                fr["Y", n] = [m]
            fr["PT", q] = [m]

        n_blocks = n
        hook = [count_overflow] if first else []
        one_hots(0)
        flush()
        for c in range(4):
            gather(0, c)
        for j in range(n + 2):
            p, q = j // 4 + 1, j % 4
            if j < n:
                gate_up(j, 0, 0)
            if j == 0:
                for c in range(4, 8):
                    gather(0, c)
                one_hots(1)
            if 0 < j < n:
                hidden(j - 1)
            if j < n:
                gate_up(j, 0, 1)
            if j == n:
                down(n - 1, 0)
            if j > 1:
                combine(j - 2)
            if j == 2 and hook:
                hook.pop()()
            some(2)
            if j < n:
                turn_p(j)
                if q == 3 and 4 * (p + 1) < n:
                    one_hots(p + 1)
                gate_up(j, 1, 0)
                if 4 * p < n:
                    gather(p, 2 * q)
                gate_up(j, 1, 1)
            if 0 < j < n:
                down(j - 1, 0)
            if j == n - 1:
                hidden(j)
            if j < n and 4 * p < n:
                gather(p, 2 * q + 1)
            if 0 < j <= n:
                down(j - 1, 1)

    blocks(NE, lambda t, j, n: RK[:, t, j:j + n], lambda t, j: WT[:, t, j:j + 1], [rk_ready, wt_ready], True,
           False, 0)

    count = {}
    for e_ in Q.ENGINES:
        put(e_, lambda e: count.update(n=e.value_load(ovf[0:1, 0:1], min_val=0, max_val=NOV - 1)), ov_ready)
    def overflow():
        in_branch[0] = True
        assert not todo
        ok = small("ok", [128, 2, NOV])
        ow = small("ow", [128, 2, NOV])
        kb = cnt[:, 4, :].unsqueeze(1).broadcast_to([128, 2, 32])
        cur[0] = dve(lambda e: e.scalar_tensor_tensor(out=T0, in0=kb, scalar=float(SLOTS), in1=RK, op0=ALU.mult,
                                                      op1=ALU.add), ids_ready)
        for j in range(NOV):
            chain(lambda e, j=j: e.tensor_scalar(cnt[:, 5, :], cnt[:, 4, :], float(j), None, ALU.is_le))
            chain(lambda e, j=j: e.tensor_scalar(cnt[:, 6, :], cnt[:, 3, :], float(j), None, ALU.is_gt))
            chain(lambda e: e.tensor_tensor(cnt[:, 5, :], cnt[:, 5, :], cnt[:, 6, :], ALU.mult))
            hot = cnt[:, 5, :].unsqueeze(1).broadcast_to([128, 2, 32])
            chain(lambda e, hot=hot: e.tensor_tensor(T1, T0, hot, ALU.mult))
            chain(lambda e, j=j: e.tensor_reduce(ok[:, :, j:j + 1], T1, AX, ALU.add))
            chain(lambda e, j=j: e.tensor_scalar(ok[:, :, j:j + 1], ok[:, :, j:j + 1], float(-SLOTS * (j + 1)), None,
                                                 ALU.add))
            chain(lambda e: e.tensor_reduce(cnt[:, 7, 16:17], cnt[:, 5, :], AX, ALU.add))
            chain(lambda e: e.tensor_scalar(cnt[:, 7, 17:18], cnt[:, 7, 16:17], -FAR, FAR, ALU.mult, ALU.add))
            chain(lambda e, j=j: e.tensor_scalar(ok[:, :, j:j + 1], ok[:, :, j:j + 1], cnt[:, 7, 17:18], None,
                                                 ALU.add))
            chain(lambda e, hot=hot: e.tensor_tensor(T1, WT, hot, ALU.mult))
            chain(lambda e, j=j: e.tensor_reduce(ow[:, :, j:j + 1], T1, AX, ALU.add))
        ov_tab = cur[0]
        for _ in range(RAW):
            feed()
        for _ in range(RING):
            split_ahead()
        blocks(NOV, lambda t, j, n: ok[:, t, j:j + n], lambda t, j: ow[:, t, j:j + 1], [ov_tab], False, True, 0)

    known = dict(Q.seen)
    if Q.who:
        with Q.eng.If(count["n"] > 0):
            overflow()
    else:
        overflow()
    Q.seen = known

    Q.era = 1
    all_done = pe(lambda e: e.drain())
    warm = dve(lambda e: e.memset(stat(32, 2), 1.0), all_done)
    ysc = slot("ysc", 3, [128, 2, 1024])
    fin = slot("fin", 4, [128, 2, 1024])
    s_out = sem("s_out")
    ends = []
    act(lambda e: e.activation(stat(32), stat(33), ACT.Sqrt), warm)
    for t in range(2):
        ys, xr = [], []
        for n in range(2):
            o = slice(512 * n, 512 * n + 512)
            ys.append(dve(lambda e: e.tensor_tensor(ysc[:, t, o], bank[acc[2 * t + n]][:, :], gate2b[:, o], ALU.mult),
                          all_done, ada_done[10], ada_done[11]))
        sq = []
        for n in range(2):
            o = slice(512 * n, 512 * n + 512)
            xr.append(dve(lambda e: e.tensor_tensor(x[:, t, o], x[:, t, o], ysc[:, t, o], ALU.add), ys[n]))
            sq.append(squares(x[:, t, o], 8 * t + n, fin[:, t, o], xr[-1]))
        ends.append((xr, sq))
    for t in range(2):
        k = 8 * t
        xr, sq = ends[t]
        a = dve(lambda e: e.tensor_tensor(stat(k), stat(k), stat(k + 1), ALU.add), sq)
        a = inv_rms(k, D, a, 1)
        for n in range(2):
            o = slice(512 * n, 512 * n + 512)
            ys = dve(lambda e: e.scalar_tensor_tensor(out=fin[:, t, o], in0=x[:, t, o], scalar=stat(k),
                                                      in1=gfb[:, o], op0=ALU.mult, op1=ALU.mult), a, xr, l_gfb)
            put("sp", lambda e: e.dma_start(out[0, 128 * t:128 * t + 128, o], fin[:, t, o]).then_inc(s_out, 16), ys)
    put("sp", lambda e: e.wait_ge(s_out, 64))


def build_two_blocks(nc, A, out):
    kept, named = {}, set()
    program(nc, A, out, kept, Queues(None, None, named, {}))
    with nc.Block() as block:
        block.sync(lambda eng: program(nc, A, out, kept, Queues("sp", eng, named, {})))
        block.scalar(lambda eng: program(nc, A, out, kept, Queues("act", eng, named, {})))
        block.gpsimd(lambda eng: program(nc, A, out, kept, Queues("pool", eng, named, {})))
        block.vector(lambda eng: program(nc, A, out, kept, Queues("dve", eng, named, {})))
        block.tensor(lambda eng: program(nc, A, out, kept, Queues("pe", eng, named, {})))


def constants():
    c = np.zeros((128, NCST), np.float32)
    i = np.arange(128)
    c[:, CST["ident"]:CST["ident"] + 128] = np.eye(128)
    c[:, CST["ident2"]:CST["ident2"] + 64] = (i[:, None] % 64 == np.arange(64)[None])
    c[:, CST["lt"]:CST["lt"] + 128] = i[:, None] < i[None]
    c[:, CST["pen_ts"]:CST["pen_ts"] + 128] = np.where(i[None] > i[:, None], -BIG, 0.0)
    c[:, CST["pen_st"]:CST["pen_st"] + 128] = np.where(i[:, None] > i[None], BIG, 0.0)
    c[:, CST["iota64"]:CST["iota64"] + 64] = np.arange(64)[None]
    c[:, CST["iota32"]:CST["iota32"] + 32] = np.arange(32)[None]
    c[:, CST["ones"]:CST["ones"] + 128] = 1.0
    return c


_PACKED = ("norm_mix_g", "norm_ff_g", "g_norm1_2", "b_s", "conv_w", "w_conv_2", "b_conv_2", "c_2", "b_gates_2", "w_s")
_NAMES = ("x", "w_in", "b_gate", "norm_v_g", "w_proj_a", "w_proj_b", "w_out", "w_ff1", "w_ff2", "norm_final_g",
          "w_ada_2", "b_ada_2", "w_in_2", "g_mlstm_head_2", "w_out_2", "g_norm2_2", "w_router_group_2",
          "b_router_group_2", "w_router_expert_2", "b_router_expert_2", "w_expert_gate_2", "w_expert_up_2",
          "w_expert_down_2", "g_final_2")


def lay_out(inputs):
    def by_part(a):
        return np.ascontiguousarray(np.asarray(a).reshape(-1, 8, 128).transpose(2, 0, 1).reshape(128, -1))

    i = {k: np.asarray(v) for k, v in inputs.items()}
    bg = np.zeros((128, 2), np.float32)
    bg[0:4, 0] = i["b_gates_2"][0, 0:4]
    bg[32:36, 1] = i["b_gates_2"][0, 4:8]
    vecs = np.concatenate([by_part(i["norm_mix_g"]), by_part(i["norm_final_g"]), by_part(i["g_norm2_2"]), by_part(i["norm_ff_g"]), by_part(i["g_norm1_2"]),
                           i["b_s"][0].T, by_part(i["conv_w"]), by_part(i["w_conv_2"]), by_part(i["b_conv_2"]),
                           by_part(i["c_2"]), bg], axis=1)
    arrays = {k: np.ascontiguousarray(i[k]) for k in _NAMES}
    arrays["norm_final_g"] = arrays["norm_final_g"].reshape(1, -1)
    arrays["g_final_2"] = arrays["g_final_2"].reshape(1, -1)
    arrays["vecs"] = np.ascontiguousarray(vecs)
    arrays["w_sT"] = np.ascontiguousarray(i["w_s"][0].transpose(2, 0, 1))
    arrays["cst"] = constants()
    return arrays


def make(nc, arrays):
    A = {k: nc.dram_tensor(f"in_{k}", a.shape, F32, kind="ExternalInput").ap() for k, a in arrays.items()}
    out = nc.dram_tensor("out_0", (1, 256, 1024), F32, kind="ExternalOutput").ap()
    return A, out


def kernel(**inputs):
    import concourse.bacc as _bacc
    from concourse.bass_utils import run_bass_kernel_spmd as _run

    nc = _bacc.Bacc("TRN2", target_bir_lowering=False, num_devices=1)
    arrays = lay_out(inputs)
    A, out = make(nc, arrays)
    build_two_blocks(nc, A, out)
    r = _run(nc, [{f"in_{k}": a for k, a in arrays.items()}], core_ids=[0])
    return r.results[0]["out_0"]
```
